# Optimizing a Trainium2 kernel written in Bass

```python
import math
import jax, jax.numpy as jnp
from jax import lax
import numpy as np

D_MODEL = 1024
BATCH = 1
SEQ = 512
DEPTH = 1

HEAD_DIM = 64
ATTN_HEADS = 8
ATTN_KV_HEADS = 2
ATTN_WIDTH = ATTN_HEADS * HEAD_DIM
KV_WIDTH = ATTN_KV_HEADS * HEAD_DIM
WINDOW = 128
BLOCK = 128
RWKV_HEADS = 8
RWKV_WIDTH = RWKV_HEADS * HEAD_DIM
MIX_WIDTH = ATTN_WIDTH + RWKV_WIDTH
DECAY_LORA = 64
ICLR_LORA = 64
GATE_LORA = 128
ATTN_COLS = ATTN_WIDTH + 2 * KV_WIDTH
RWKV_COLS = 3 * RWKV_WIDTH + DECAY_LORA + ICLR_LORA + GATE_LORA
IN_COLS = ATTN_COLS + RWKV_COLS
PEER_HEADS = 8
PEER_NKEYS = 128
PEER_EXPERTS = PEER_NKEYS * PEER_NKEYS
PEER_QDIM = 256
PEER_HALF = PEER_QDIM // 2
PEER_TOPK = 16
PEER_CHUNK = 128
LN_EPS = 1e-5
GN_EPS = 64e-5

kernel_name = 'hymba_swa_sink_rwkv7_peer_deepnorm_adaln'

def _layer_norm(x, g, b):
    xf = x.astype(jnp.float32)
    mu = jnp.mean(xf, axis=-1, keepdims=True)
    var = jnp.mean(jnp.square(xf - mu), axis=-1, keepdims=True)
    return ((xf - mu) * lax.rsqrt(var + LN_EPS)).astype(x.dtype) * g + b

def _sliding_window_sink_attention(q, k, v, sink):
    B, S, H, Dh = q.shape
    KV = k.shape[2]
    G = H // KV
    NB = S // BLOCK
    qb = q.reshape(B, NB, BLOCK, KV, G, Dh)
    kb = k.reshape(B, NB, BLOCK, KV, Dh)
    vb = v.reshape(B, NB, BLOCK, KV, Dh)
    prev = lambda t: jnp.concatenate([jnp.zeros_like(t[:, :1]), t[:, :-1]], axis=1)
    kw = jnp.concatenate([prev(kb), kb], axis=2)
    vw = jnp.concatenate([prev(vb), vb], axis=2)
    s = jnp.einsum('bnqkgd,bnjkd->bnkgqj', qb, kw).astype(jnp.float32) * (Dh ** -0.5)
    qpos = jnp.arange(BLOCK)[:, None] + BLOCK
    kpos = jnp.arange(2 * BLOCK)[None, :]
    dist = qpos - kpos
    allowed = (dist >= 0) & (dist < WINDOW)
    valid = (jnp.arange(NB)[:, None] * BLOCK - BLOCK + kpos) >= 0
    mask = allowed[None, :, :] & valid[:, None, :]
    s = jnp.where(mask[None, :, None, None, :, :], s, -jnp.inf)
    sink_l = sink.astype(jnp.float32).reshape(KV, G)[None, None, :, :, None, None]
    m = jnp.maximum(jnp.max(s, axis=-1, keepdims=True), sink_l)
    p = jnp.exp(s - m)
    p = p / (jnp.sum(p, axis=-1, keepdims=True) + jnp.exp(sink_l - m))
    o = jnp.einsum('bnkgqj,bnjkd->bnqkgd', p.astype(v.dtype), vw)
    return o.reshape(B, S, H * Dh)

def _rwkv7_time_mix(p, mu, w0, w2, a0, a2, g2, k_k, k_a, r_k, lnx_g, lnx_b):
    B, S, _ = p.shape
    p_prev = jnp.pad(p, ((0, 0), (1, 0), (0, 0)))[:, :-1]
    p = p + (p_prev - p) * mu
    o0 = RWKV_WIDTH
    r = p[..., 0:o0]
    k = p[..., o0:2 * o0]
    v = p[..., 2 * o0:3 * o0]
    wd = p[..., 3 * o0:3 * o0 + DECAY_LORA]
    ad = p[..., 3 * o0 + DECAY_LORA:3 * o0 + DECAY_LORA + ICLR_LORA]
    gd = p[..., 3 * o0 + DECAY_LORA + ICLR_LORA:]
    w_log = -jax.nn.softplus(-(w0 + jnp.tanh(wd) @ w2)) - 0.5
    decay = jnp.exp(-jnp.exp(w_log.astype(jnp.float32)))
    a = jax.nn.sigmoid(a0 + ad @ a2)
    g = jax.nn.sigmoid(gd) @ g2
    hs = lambda t: t.reshape(B, S, RWKV_HEADS, HEAD_DIM)
    r, k, v, a, decay = hs(r), hs(k), hs(v), hs(a), hs(decay)
    kk = hs(k.reshape(B, S, RWKV_WIDTH) * k_k).astype(jnp.float32)
    kk = kk * lax.rsqrt(jnp.maximum(jnp.sum(kk * kk, axis=-1, keepdims=True), 1e-24))
    k = k * (1.0 + (a - 1.0) * hs(jnp.broadcast_to(k_a, (B, S, RWKV_WIDTH))))
    f32 = jnp.float32
    tm = lambda t: jnp.moveaxis(t.astype(f32), 1, 0)
    xs = (tm(r), tm(decay), tm(k), tm(v), tm(-kk), tm(kk * a.astype(f32)))

    def step(state, inp):
        r_t, w_t, k_t, v_t, na_t, b_t = inp
        sa = jnp.einsum('bhvk,bhk->bhv', state, na_t)
        state = state * w_t[:, :, None, :] + sa[..., None] * b_t[:, :, None, :] + v_t[..., None] * k_t[:, :, None, :]
        return state, jnp.einsum('bhvk,bhk->bhv', state, r_t)

    state0 = jnp.zeros((B, RWKV_HEADS, HEAD_DIM, HEAD_DIM), f32)
    _, ys = lax.scan(step, state0, xs)
    y = jnp.moveaxis(ys, 0, 1)
    mean = jnp.mean(y, axis=-1, keepdims=True)
    var = jnp.mean(jnp.square(y - mean), axis=-1, keepdims=True)
    y = ((y - mean) * lax.rsqrt(var + GN_EPS)).reshape(B, S, RWKV_WIDTH).astype(p.dtype) * lnx_g + lnx_b
    bonus = jnp.sum(r * k * r_k, axis=-1, keepdims=True) * v
    return (y + bonus.reshape(B, S, RWKV_WIDTH)) * g

def _peer(h, wq, subkeys, U, V):
    B, S, D = h.shape
    T = B * S
    hf = h.reshape(T, D)
    q = (hf @ wq).reshape(T, PEER_HEADS, 2, PEER_HALF)
    s = jnp.einsum('thcd,hcnd->thcn', q, subkeys).astype(jnp.float32)
    sv, si = lax.top_k(s, PEER_TOPK)
    cand = sv[:, :, 0, :, None] + sv[:, :, 1, None, :]
    cidx = si[:, :, 0, :, None] * PEER_NKEYS + si[:, :, 1, None, :]
    fv, fpos = lax.top_k(cand.reshape(T, PEER_HEADS, PEER_TOPK * PEER_TOPK), PEER_TOPK)
    fidx = jnp.take_along_axis(cidx.reshape(T, PEER_HEADS, PEER_TOPK * PEER_TOPK), fpos, axis=-1)
    gates = jax.nn.softmax(fv, axis=-1).astype(h.dtype)

    def chunk(args):
        xc, ic, gc = args
        u = jnp.take(U, ic, axis=0)
        act = jax.nn.gelu(jnp.einsum('chkd,cd->chk', u, xc), approximate=False)
        vv = jnp.take(V, ic, axis=0)
        return jnp.einsum('chk,chkd->cd', gc * act, vv)

    nc = T // PEER_CHUNK
    y = lax.map(chunk, (hf.reshape(nc, PEER_CHUNK, D),
                        fidx.reshape(nc, PEER_CHUNK, PEER_HEADS, PEER_TOPK),
                        gates.reshape(nc, PEER_CHUNK, PEER_HEADS, PEER_TOPK)))
    return y.reshape(B, S, D)

def setup_inputs(seed: int = 0) -> dict:
    key = jax.random.key(seed)
    ks = jax.random.split(key, 32)
    L, D = DEPTH, D_MODEL
    beta = (8.0 * DEPTH) ** -0.25
    nrm = lambda i, shape, sc: jax.random.normal(ks[i], shape, jnp.float32) * sc
    uni = lambda i, shape, lo, hi: jax.random.uniform(ks[i], shape, jnp.float32, lo, hi)
    return {
        'x': nrm(0, (BATCH, SEQ, D), 1.0),
        'c': nrm(1, (BATCH, D), 1.0),
        'ada_w': nrm(2, (L, D, 6 * D), 0.5 * D ** -0.5),
        'ada_b': nrm(3, (L, 6 * D), 0.02),
        'w_in': nrm(4, (L, D, IN_COLS), D ** -0.5),
        'attn_sink': nrm(5, (L, ATTN_HEADS), 1.0),
        'shift_mu': uni(6, (L, RWKV_COLS), 0.0, 1.0),
        'decay_w0': uni(7, (L, RWKV_WIDTH), -6.0, 1.0),
        'decay_w2': nrm(8, (L, DECAY_LORA, RWKV_WIDTH), 0.5 * DECAY_LORA ** -0.5),
        'iclr_a0': nrm(9, (L, RWKV_WIDTH), 0.5),
        'iclr_a2': nrm(10, (L, ICLR_LORA, RWKV_WIDTH), 0.5 * ICLR_LORA ** -0.5),
        'gate_g2': nrm(11, (L, GATE_LORA, RWKV_WIDTH), GATE_LORA ** -0.5),
        'k_k': 0.85 + nrm(12, (L, RWKV_WIDTH), 0.05),
        'k_a': 1.0 + nrm(13, (L, RWKV_WIDTH), 0.05),
        'r_k': nrm(14, (L, RWKV_HEADS, HEAD_DIM), 0.1),
        'lnx_g': 1.0 + nrm(15, (L, RWKV_WIDTH), 0.05),
        'lnx_b': nrm(16, (L, RWKV_WIDTH), 0.02),
        'w_out': nrm(17, (L, MIX_WIDTH, D), beta * MIX_WIDTH ** -0.5),
        'ln1_g': 1.0 + nrm(18, (L, D), 0.05),
        'ln1_b': nrm(19, (L, D), 0.02),
        'peer_wq': nrm(20, (L, D, PEER_HEADS * PEER_QDIM), D ** -0.5),
        'peer_subkeys': nrm(21, (L, PEER_HEADS, 2, PEER_NKEYS, PEER_HALF), PEER_HALF ** -0.5),
        'peer_u': nrm(22, (L, PEER_EXPERTS, D), D ** -0.5),
        'peer_v': nrm(23, (L, PEER_EXPERTS, D), beta),
        'ln2_g': 1.0 + nrm(24, (L, D), 0.05),
        'ln2_b': nrm(25, (L, D), 0.02),
    }

def reference(x, c, ada_w, ada_b, w_in, attn_sink, shift_mu, decay_w0, decay_w2, iclr_a0, iclr_a2,
              gate_g2, k_k, k_a, r_k, lnx_g, lnx_b, w_out, ln1_g, ln1_b, peer_wq, peer_subkeys,
              peer_u, peer_v, ln2_g, ln2_b):
    B, S, D = x.shape
    alpha = (2.0 * DEPTH) ** 0.25
    cs = jax.nn.silu(c)
    for l in range(DEPTH):
        mod = cs @ ada_w[l] + ada_b[l]
        sh1, sc1, gt1, sh2, sc2, gt2 = [m[:, None, :] for m in jnp.split(mod, 6, axis=-1)]
        h = x * (1.0 + sc1) + sh1
        proj = h @ w_in[l]
        q = proj[..., :ATTN_WIDTH].reshape(B, S, ATTN_HEADS, HEAD_DIM)
        k = proj[..., ATTN_WIDTH:ATTN_WIDTH + KV_WIDTH].reshape(B, S, ATTN_KV_HEADS, HEAD_DIM)
        v = proj[..., ATTN_WIDTH + KV_WIDTH:ATTN_COLS].reshape(B, S, ATTN_KV_HEADS, HEAD_DIM)
        y_attn = _sliding_window_sink_attention(q, k, v, attn_sink[l])
        y_rwkv = _rwkv7_time_mix(proj[..., ATTN_COLS:], shift_mu[l], decay_w0[l], decay_w2[l], iclr_a0[l],
                                 iclr_a2[l], gate_g2[l], k_k[l], k_a[l], r_k[l], lnx_g[l], lnx_b[l])
        y = jnp.concatenate([y_attn, y_rwkv], axis=-1) @ w_out[l]
        x = _layer_norm(alpha * x + gt1 * y, ln1_g[l], ln1_b[l])
        h = x * (1.0 + sc2) + sh2
        y = _peer(h, peer_wq[l], peer_subkeys[l], peer_u[l], peer_v[l])
        x = _layer_norm(alpha * x + gt2 * y, ln2_g[l], ln2_b[l])
    return x


_drawn_inputs = setup_inputs


def setup_inputs(seed=0):
    import zlib

    import numpy as np

    out = dict(_drawn_inputs(seed))
    spreads = {}
    factors = {'ada_b': 3.45,
     'attn_sink': 21.866,
     'decay_w2': 8.0,
     'iclr_a0': 3.979,
     'iclr_a2': 3.739,
     'k_k': 31.046,
     'k_a': 7.782,
     'r_k': 2.736,
     'lnx_g': 8.0,
     'lnx_b': 41.765,
     'ln2_b': 2.812}
    for name, (base, spread) in spreads.items():
        noise = np.random.default_rng([zlib.crc32(name.encode()), seed]).standard_normal(out[name].shape)
        drawn = base * np.exp(spread * noise) if base else spread * noise
        out[name] = __import__('jax').numpy.asarray(drawn.astype(out[name].dtype))
    for name, factor in factors.items():
        out[name] = (out[name] * factor).astype(out[name].dtype)
    return out
```

```python
import concourse.bass as bass
from concourse import mybir
from contextlib import ExitStack
import math

D = 1024
T = 512
P = 128
KD = D // P
NT = T // P
HD = 64
HEADS = 8
PAIRS = HEADS // 2
ATTN_COLS = 768
RW_TILES = 14
CH = 64
NKEYS = 128
TOPK = 16
AHEAD = 4
LN_EPS = 1e-5
GN_EPS = 64e-5
ALPHA = 2.0 ** 0.25
KAPPA = math.exp(-0.5)
NEG = -1.0e30

F32 = mybir.dt.float32
F32R = mybir.dt.float32r
U32 = mybir.dt.uint32
ALU = mybir.AluOpType
ACT = mybir.ActivationFunctionType
AX = mybir.AxisListType

R_C, R_ADAB, R_MU, R_W0, R_A0, R_KK, R_KA, R_RK, R_LXG, R_LXB = 0, 8, 56, 70, 74, 78, 82, 86, 90, 94
N_ROWS = 98


class Tally:

    def __init__(self, sem):
        self.sem, self.base, self.local, self.loop = sem, 0, 0, None

    def value(self):
        turns = 0 if self.loop is None else self.loop[0] * self.loop[1]
        return turns + (self.base + self.local)

    def inc(self, ins):
        ins.then_inc(self.sem, 1)
        self.local += 1
        return ins

    def enter(self, i, per):
        self.base, self.local, self.loop = self.base + self.local, 0, (i, per)

    def leave(self, turns):
        assert self.local == self.loop[1], (self.local, self.loop[1])
        self.base, self.local, self.loop = self.base + turns * self.local, 0, None


def stepper(eng, tally):
    def step(ins):
        tally.inc(ins)
        eng.wait_ge(tally.sem, tally.value())
    return step


def hybrid_layer(nc, x, c, ada_w, ada_b, w_in, attn_sink, shift_mu, decay_w0, decay_w2, iclr_a0, iclr_a2,
                 gate_g2, k_k, k_a, r_k, lnx_g, lnx_b, w_out, ln1_g, ln1_b, peer_wq, peer_subkeys,
                 peer_u, peer_v, ln2_g, ln2_b, out):
    ctx = ExitStack()
    with ctx:
        held, phase = [], [1]

        def sem(name):
            held.append(nc.alloc_semaphore(f"{name}_{phase[0]}"))
            return held[-1]

        def fresh():
            nc.clear_and_free_semaphores(held)
            nc.all_engine_barrier()
            held.clear()
            phase[0] += 1

        def keep(name, shape, dt=F32):
            return ctx.enter_context(nc.sbuf_tensor(name, shape, dt))

        bank = ctx.enter_context(nc.psum_tensor("bank", [P, 8 * 512], F32))
        banks = [bank[:, 512 * i:512 * i + 512] for i in range(8)]

        ident = keep("ident", [P, P])
        par = keep("par", [P, N_ROWS])
        mod = keep("mod", [P, 32])
        gt1 = keep("gt1", [P, D])
        gt2 = keep("gt2", [P, D])
        wide = keep("wide", [P, KD, T])

        gates = nc.dram_tensor("gates", [P, T // TB, NKEYS, TB], F32, kind="Internal").ap()
        mix = ExitStack()
        mix.__enter__()

        def mk(name, shape, dt=F32):
            return mix.enter_context(nc.sbuf_tensor(name, shape, dt))

        diag2 = mk("diag2", [P, P])
        qT = mk("qT", [P, 4, T])
        kT = mk("kT", [P, 2, P + T])
        vtok = mk("vtok", [P, 1 + NT, P])
        PM = mk("PM", [P, RW_TILES, T])
        yT = wide
        SW = yT[:, 0:4, :]
        CS = yT[:, 4:8, :]
        AI = mk("AI", [P, PAIRS, T])
        GG = mk("GG", [P, PAIRS, T])
        KN = mk("KN", [P, PAIRS, T])
        BO = mk("BO", [P, PAIRS, T])
        PL = mk("PL", [P, PAIRS, T // CH])

        emit_projections(nc, banks, sem, locals())
        fresh()
        emit_mixing(nc, banks, sem, locals())
        fresh()
        mix.close()

        x1 = keep("x1", [P, NT, D])
        hh = keep("hh", [P, KD, T], F32R)
        hl = keep("hl", [P, KD, T], F32R)
        ring = keep("ring", [P, 4 * AHEAD, T])
        h2 = wide
        emit_mix_out(nc, banks, sem, locals())
        fresh()
        with ExitStack() as picks:
            FV, IS, JS = (picks.enter_context(nc.sbuf_tensor(n, [P, NT, HEADS, TOPK], F32))
                          for n in ("FV", "IS", "JS"))
            emit_routing(nc, banks, sem, locals())
            fresh()
            emit_gates(nc, banks, sem, locals())
            fresh()
        acc = wide[:, :, :].rearrange("p (t h) d -> p t (h d)", t=NT)
        emit_experts(nc, bank, banks, sem, locals())


def emit_projections(nc, banks, sem, v):
    (x, c, ada_w, ada_b, w_in, shift_mu, decay_w0, decay_w2, iclr_a0, iclr_a2, gate_g2, k_k, k_a, r_k, lnx_g,
     lnx_b) = (v[n] for n in ("x", "c", "ada_w", "ada_b", "w_in", "shift_mu", "decay_w0", "decay_w2", "iclr_a0",
                              "iclr_a2", "gate_g2", "k_k", "k_a", "r_k", "lnx_g", "lnx_b"))
    (ident, par, mod, gt1, gt2, diag2, qT, kT, vtok, PM, SW, CS, AI, GG, KN, BO, PL) = (
        v[n] for n in ("ident", "par", "mod", "gt1", "gt2", "diag2", "qT", "kT", "vtok", "PM", "SW", "CS", "AI",
                       "GG", "KN", "BO", "PL"))
    ctx = ExitStack()
    with ctx:
        def sb(name, shape, dt=F32):
            return ctx.enter_context(nc.sbuf_tensor(name, shape, dt))

        rows = sb("rows", [P, P])
        csT = sb("csT", [P, KD])
        csw = sb("csw", [P, KD, P])
        omu = sb("omu", [P, RW_TILES])
        xin = [sb(f"xin{i}", [P, D]) for i in range(2)]
        hT = sb("hT", [P, KD, T])
        ada = [sb(f"ada{i}", [P, KD, 512]) for i in range(2)]
        wt = [sb(f"wt{i}", [P, KD, P]) for i in range(2)]
        w2a2 = sb("w2a2", [P, 512])
        g2 = sb("g2", [P, 512])
        PD = sb("PD", [P, PAIRS, T])
        keepm = sb("keepm", [P, T])
        tmp = [sb(f"tmp{i}", [P, T]) for i in range(4)]

        rows_in, lora_in = sem("rows_in"), sem("lora_in")
        x_in = [sem(f"x_in{i}") for i in range(2)]
        ada_in = [sem(f"ada_in{i}") for i in range(2)]
        wt_in = [sem(f"wt_in{i}") for i in range(2)]
        gb_in = sem("gb_in")
        consts, rows_up, par_up, silu_up = sem("consts"), sem("rows_up"), sem("par_up"), sem("silu_up")
        cs_up = sem("cs_up")
        xt_up, xt_used = sem("xt_up"), sem("xt_used")
        cols_up, cols_used = sem("cols_up"), sem("cols_used")
        ada_used, h_up = sem("ada_used"), sem("h_up")
        proj_up, proj_scaled, proj_mixed = sem("proj_up"), sem("proj_scaled"), sem("proj_mixed")
        lora_act, z_up, z_used = sem("lora_act"), sem("z_up"), sem("z_used")
        p_dve, p_act, p_pool = sem("p_dve"), sem("p_act"), sem("p_pool")
        gate_up, gate_used = sem("gate_up"), sem("gate_used")
        sq_up, ss_up, ss_max, ss_root = sem("sq_up"), sem("ss_up"), sem("ss_max"), sem("ss_root")
        kp_up, rk_up, rks_up, bsum_up, bo_up = sem("kp_up"), sem("rk_up"), sem("rks_up"), sem("bsum_up"), sem("bo_up")
        cs_scan, csm_up, exp_up, nk_up = sem("cs_scan"), sem("csm_up"), sem("exp_up"), sem("nk_up")

        wv = w_in.rearrange("o (k p) n -> p (o k) n", p=P)
        av = ada_w.rearrange("o (k p) n -> p (o k) n", p=P)
        xv = x.rearrange("o (t p) d -> p (o t) d", p=P)

        def ada_piece(m, half):
            return av[:, :, m * D + half * 512:m * D + half * 512 + 512]

        pieces = [(m, half) for m in (0, 1, 2, 3, 4, 5) for half in (0, 1)]

        block = ctx.enter_context(nc.Block())

        @block.sync
        def _(sp):
            for name, src, n in (("c", c, 8), ("ada_b", ada_b, 48), ("mu", shift_mu, 14), ("w0", decay_w0, 4),
                                 ("a0", iclr_a0, 4), ("kk", k_k, 4), ("ka", k_a, 4), ("rk", r_k, 4),
                                 ("lxg", lnx_g, 4), ("lxb", lnx_b, 4)):
                at = {"c": R_C, "ada_b": R_ADAB, "mu": R_MU, "w0": R_W0, "a0": R_A0, "kk": R_KK, "ka": R_KA,
                      "rk": R_RK, "lxg": R_LXG, "lxb": R_LXB}[name]
                flat = src.rearrange("o h d -> (o h d)") if name == "rk" else src.rearrange("o n -> (o n)")
                sp.dma_start(rows[at:at + n, :], flat.rearrange("(n p) -> n p", p=P)).then_inc(rows_in, 16)
            for t in range(NT):
                if t >= 2:
                    sp.wait_ge(xt_up, 2 * (t - 1))
                sp.dma_start(xin[t % 2][:, :], xv[:, t, :]).then_inc(x_in[t % 2], 16)
            for n in range(4):
                if n >= 2:
                    sp.wait_ge(ada_used, n - 1)
                sp.dma_start(ada[n % 2][:, :, :], ada_piece(*pieces[n])).then_inc(ada_in[n % 2], 16)
            sp.dma_start(w2a2[0:64, :], decay_w2[0, :, :]).then_inc(lora_in, 16)
            sp.dma_start(w2a2[64:128, :], iclr_a2[0, :, :]).then_inc(lora_in, 16)
            sp.dma_start(g2[:, :], gate_g2[0, :, :]).then_inc(lora_in, 16)
            for n in range(2):
                sp.dma_start(wt[n][:, :, :], wv[:, :, ATTN_COLS + (12 + n) * P:ATTN_COLS + (13 + n) * P])\
                    .then_inc(wt_in[n], 16)
            with sp.Fori(0, 6) as i:
                for n in range(2):
                    sp.wait_ge(proj_up, 2 * i + (n + 1))
                    sp.dma_start(wt[n][:, :, :], wv[:, :, bass.ds((i * 2 + n) * P + ATTN_COLS, P)])\
                        .then_inc(wt_in[n], 16)
            with sp.Fori(0, 2) as i:
                for n in range(2):
                    sp.wait_ge(proj_up, 2 * i + (13 + n))
                    sp.dma_start(wt[n][:, :, :], wv[:, :, bass.ds((i * 2 + n) * P, P)]).then_inc(wt_in[n], 16)
            for n in range(2):
                sp.wait_ge(proj_up, 17 + n)
                for d in range(2):
                    sp.dma_start(wt[n][:, :, 64 * d:64 * d + 64], wv[:, :, 512 + 64 * n:576 + 64 * n])\
                        .then_inc(wt_in[n], 16)
            sp.wait_ge(proj_up, 19)
            sp.dma_start(wt[0][:, :, :], wv[:, :, 640:768]).then_inc(wt_in[0], 16)
            for n in range(4, 12):
                sp.wait_ge(ada_used, n - 1)
                sp.dma_start(ada[n % 2][:, :, :], ada_piece(*pieces[n])).then_inc(ada_in[n % 2], 16)
            flat = ada_b.rearrange("o n -> (o n)")
            for dst, m in ((gt1, 2), (gt2, 5)):
                sp.dma_start(dst[:, :], flat[m * D:(m + 1) * D].partition_broadcast(P)).then_inc(gb_in, 16)
            sp.wait_ge(gb_in, 32)

        @block.gpsimd
        def _(pool):
            step = stepper(pool, Tally(p_pool))
            step(pool.memset(ident[:, :], 0.0))
            pool.affine_select(out=ident[:, :], in_=ident[:, :], compare_op=ALU.not_equal, fill=1.0, base=0,
                               pattern=[[-1, P]], channel_multiplier=1).then_inc(consts, 1)
            step(pool.memset(diag2[:, :], 1.0))
            d2 = diag2[:, :].rearrange("p (b w) -> p b w", b=2)
            step(pool.affine_select(out=d2, in_=d2, compare_op=ALU.is_ge, fill=0.0, base=0,
                                    pattern=[[-CH, 2], [0, CH]], channel_multiplier=1))
            pool.affine_select(out=d2, in_=d2, compare_op=ALU.is_ge, fill=0.0, base=CH - 1,
                               pattern=[[CH, 2], [0, CH]], channel_multiplier=-1).then_inc(consts, 1)
            step(pool.memset(keepm[:, :], 1.0))
            pool.memset(keepm[:, ::CH], 0.0).then_inc(consts, 1)
            pool.memset(kT[:, :, 0:P], 0.0).then_inc(consts, 1)
            pool.memset(vtok[:, 0, :], 0.0).then_inc(consts, 1)

            for p in range(PAIRS):
                pool.wait_ge(kp_up, p + 1)
                if p >= 2:
                    pool.wait_ge(ss_up, p - 1)
                pool.tensor_tensor(tmp[p % 2][:, :], KN[:, p, :], KN[:, p, :], ALU.mult).then_inc(sq_up, 1)
            for p in range(PAIRS):
                pool.wait_ge(cs_scan, p + 1)
                pool.tensor_tensor(SW[:, p, :], CS[:, p, :], SW[:, p, :], ALU.subtract).then_inc(csm_up, 1)
            for p in range(PAIRS):
                pool.wait_ge(kp_up, PAIRS + p + 1)
                if p >= 2:
                    pool.wait_ge(bsum_up, p - 1)
                pool.tensor_tensor(tmp[2 + p % 2][:, :], PM[:, p, :], PM[:, 4 + p, :], ALU.mult).then_inc(rk_up, 1)
            for p in range(PAIRS):
                pool.wait_ge(exp_up, 3 * PAIRS)
                pool.wait_ge(nk_up, 2 * p + 2)
                pool.tensor_tensor(AI[:, p, :], AI[:, p, :], CS[:, p, :], ALU.mult).then_inc(p_pool, 1)
            for p in range(PAIRS):
                pool.wait_ge(rk_up, p + 1)
                pool.tensor_tensor(PM[:, 4 + p, :], PM[:, 4 + p, :], CS[:, p, :], ALU.mult).then_inc(p_pool, 1)

        @block.scalar
        def _(act):
            act.wait_ge(rows_up, 1)
            act.activation(par[:, :], banks[7][:, 0:N_ROWS], ACT.Copy).then_inc(par_up, 1)
            act.wait_ge(par_up, 1)
            act.activation(csT[:, :], par[:, R_C:R_C + KD], ACT.Sigmoid).then_inc(silu_up, 1)
            for t in range(NT):
                for h in range(2):
                    act.wait_ge(xt_up, 2 * t + h + 1)
                    act.activation(hT[:, 4 * h:4 * h + 4, t * P:(t + 1) * P],
                                   banks[2 + (2 * t + h) % 4][:, :].rearrange("p (k t) -> p k t", k=4), ACT.Copy)\
                        .then_inc(xt_used, 1)
            act.wait_ge(silu_up, 3)
            for n in range(2):
                act.wait_ge(proj_up, n + 1)
                act.activation(PM[:, 12 + n, :], banks[n][:, :], ACT.Copy, scale=omu[:, 12 + n:13 + n])\
                    .then_inc(proj_scaled, 1)
            act.wait_ge(proj_mixed, 2)
            act.activation(PM[0:64, 12, :], PM[0:64, 12, :], ACT.Tanh).then_inc(lora_act, 1)
            act.activation(PM[:, 13, :], PM[:, 13, :], ACT.Sigmoid).then_inc(lora_act, 1)
            for p in range(PAIRS):
                for j, (dst, row) in enumerate(((SW, R_W0), (AI, R_A0), (GG, None))):
                    n = 3 * p + j
                    act.wait_ge(z_up, n + 1)
                    src = banks[2 + n % 2][:, :]
                    if row is None:
                        act.activation(dst[:, p, :], src, ACT.Copy).then_inc(z_used, 1)
                    else:
                        act.activation(dst[:, p, :], src, ACT.Sigmoid, bias=par[:, row + p:row + p + 1])\
                            .then_inc(z_used, 1)
            with act.Fori(0, 6) as i:
                for n in range(2):
                    act.wait_ge(proj_up, 2 * i + (3 + n))
                    act.activation(PM[:, bass.ds(2 * i + n, 1), :].rearrange("p o t -> p (o t)"), banks[n][:, :],
                                   ACT.Copy, scale=omu[:, bass.ds(2 * i + n, 1)]).then_inc(proj_scaled, 1)
            with act.Fori(0, 2) as i:
                for n in range(2):
                    act.wait_ge(proj_up, 2 * i + (15 + n))
                    act.activation(qT[:, bass.ds(2 * i + n, 1), :].rearrange("p o t -> p (o t)"), banks[n][:, :],
                                   ACT.Copy, scale=HD ** -0.5).then_inc(proj_scaled, 1)
            for n in range(2):
                act.wait_ge(proj_up, 19 + n)
                act.activation(kT[:, n, P:], banks[n][:, :], ACT.Copy).then_inc(proj_scaled, 1)
            act.wait_ge(proj_up, 21)
            act.activation(vtok[:, 1:, :], banks[0][:, :].rearrange("p (t n) -> p t n", t=NT), ACT.Copy)\
                .then_inc(proj_scaled, 1)
            for p in range(PAIRS):
                act.wait_ge(ss_max, p + 1)
                act.activation(PD[:, p, :], PD[:, p, :], ACT.Sqrt).then_inc(ss_root, 1)
            act.wait_ge(cs_scan, PAIRS)
            act.wait_ge(csm_up, PAIRS)
            act.activation(SW[:, :, :], SW[:, :, :], ACT.Exp, scale=-KAPPA).then_inc(exp_up, PAIRS)
            act.wait_ge(nk_up, 2 * PAIRS)
            act.activation(PD[:, :, :], CS[:, :, :], ACT.Exp, scale=-KAPPA).then_inc(exp_up, PAIRS)
            act.wait_ge(exp_up, 2 * PAIRS)
            act.activation(CS[:, :, :], CS[:, :, :], ACT.Exp, scale=KAPPA).then_inc(exp_up, PAIRS)

        @block.tensor
        def _(pe):
            pe.wait_ge(rows_in, 160)
            pe.wait_ge(consts, 1)
            pe.transpose(banks[7][:, 0:N_ROWS], rows[0:N_ROWS, :], ident[0:N_ROWS, 0:N_ROWS]).then_inc(rows_up, 1)
            for t in range(NT):
                pe.wait_ge(x_in[t % 2], 16 * (t // 2 + 1))
                for h in range(2):
                    n = 2 * t + h
                    if n >= 4:
                        pe.wait_ge(xt_used, n - 3)
                    for k in range(4):
                        last = pe.transpose(banks[2 + n % 4][:, k * P:(k + 1) * P],
                                            xin[t % 2][:, (4 * h + k) * P:(4 * h + k + 1) * P], ident[:, :])
                    last.then_inc(xt_up, 1)
            pe.wait_ge(silu_up, 2)
            def columns(n, col):
                pe.wait_ge(ada_in[n % 2], 16 * (n // 2 + 1))
                for j in range(4):
                    for k in range(KD):
                        last = pe.matmul(banks[6][:, col + j:col + j + 1], ada[n % 2][:, k, j * P:(j + 1) * P],
                                         csT[:, k:k + 1], start=(k == 0), stop=(k == KD - 1))
                last.then_inc(ada_used, 1)
            for n in range(4):
                columns(n, 4 * n)
            pe.wait_ge(h_up, KD)
            def project(slot, w):
                for k in range(KD):
                    last = pe.matmul(banks[slot][:, :], wt[slot][:, k, :], hT[:, k, :], start=(k == 0),
                                     stop=(k == KD - 1))
                last.then_inc(proj_up, 1)
            for n in range(2):
                pe.wait_ge(wt_in[n], 16)
                project(n, n)
            pe.wait_ge(lora_in, 48)
            pe.wait_ge(lora_act, 2)
            for p in range(PAIRS):
                for j in range(3):
                    n = 3 * p + j
                    if n >= 2:
                        pe.wait_ge(z_used, n - 1)
                    cols = slice(p * P, (p + 1) * P)
                    w, r = ((w2a2[0:64, cols], PM[0:64, 12, :]), (w2a2[64:128, cols], PM[64:128, 12, :]),
                            (g2[:, cols], PM[:, 13, :]))[j]
                    pe.matmul(banks[2 + n % 2][:, :], w, r, start=True, stop=True).then_inc(z_up, 1)
            with pe.Fori(0, 6) as i:
                for n in range(2):
                    pe.wait_ge(wt_in[n], 16 * i + 32)
                    pe.wait_ge(proj_mixed, 2 * i + (n + 1))
                    project(n, None)
            with pe.Fori(0, 2) as i:
                for n in range(2):
                    pe.wait_ge(wt_in[n], 16 * i + 128)
                    pe.wait_ge(proj_scaled, 2 * i + (13 + n))
                    pe.wait_ge(proj_mixed, 14)
                    project(n, None)
            for p in range(PAIRS):
                if p == 0:
                    pe.wait_ge(consts, 5)
                pe.wait_ge(sq_up, p + 1)
                if p >= 2:
                    pe.wait_ge(ss_max, p - 1)
                pe.matmul(banks[4 + p % 2][:, :], diag2[:, :], tmp[p % 2][:, :], start=True, stop=True)\
                    .then_inc(ss_up, 1)
            for n in range(2):
                pe.wait_ge(wt_in[n], 16 * 9 + 32)
                pe.wait_ge(proj_scaled, 17 + n)
                project(n, None)
            pe.wait_ge(wt_in[0], 16 * 9 + 48)
            pe.wait_ge(proj_scaled, 19)
            for t in range(NT):
                for k in range(KD):
                    last = pe.matmul(banks[0][:, t * P:(t + 1) * P], hT[:, k, t * P:(t + 1) * P], wt[0][:, k, :],
                                     start=(k == 0), stop=(k == KD - 1))
            last.then_inc(proj_up, 1)
            for p in range(PAIRS):
                pe.wait_ge(rks_up, p + 1)
                pe.wait_ge(ss_max, PAIRS)
                if p >= 2:
                    pe.wait_ge(bo_up, p - 1)
                pe.matmul(banks[4 + p % 2][:, :], diag2[:, :], tmp[2 + p % 2][:, :], start=True, stop=True)\
                    .then_inc(bsum_up, 1)
            def gate(n, bank):
                pe.wait_ge(ada_in[n % 2], 16 * (n // 2 + 1))
                for k in range(KD):
                    last = pe.matmul(banks[bank][:, :], csw[:, k, :], ada[n % 2][:, k, :], start=(k == 0),
                                     stop=(k == KD - 1))
                last.then_inc(ada_used, 1)
            pe.wait_ge(cols_used, 1)
            gate(4, 2)
            gate(5, 3)
            for n in range(6, 10):
                columns(n, 4 * n - 8)
            pe.wait_ge(gate_used, 2)
            gate(10, 2)
            gate(11, 3)

        @block.vector
        def _(dve):
            tally = Tally(p_dve)
            step = stepper(dve, tally)
            dve.wait_ge(par_up, 1)
            dve.wait_ge(silu_up, 1)
            dve.tensor_tensor(csT[:, :], csT[:, :], par[:, R_C:R_C + KD], ALU.mult).then_inc(silu_up, 1)
            dve.tensor_scalar(omu[:, :], par[:, R_MU:R_MU + RW_TILES], -1.0, 1.0, ALU.mult, ALU.add)\
                .then_inc(silu_up, 1)
            dve.wait_ge(silu_up, 3)
            step(dve.tensor_copy(csw[:, :, :], csT[:, :].unsqueeze(2).broadcast_to([P, KD, P])))
            dve.wait_ge(ada_used, 4)
            dve.tensor_tensor(mod[:, 0:16], banks[6][:, 0:16], par[:, R_ADAB:R_ADAB + 16], ALU.add)\
                .then_inc(cols_used, 1)
            dve.wait_ge(cols_used, 1)
            step(dve.tensor_scalar(mod[:, 8:16], mod[:, 8:16], 1.0, None, ALU.add))
            dve.wait_ge(xt_used, 8)
            for k in range(KD):
                dve.tensor_scalar(hT[:, k, :], hT[:, k, :], mod[:, 8 + k:9 + k], mod[:, k:k + 1],
                                  ALU.mult, ALU.add).then_inc(h_up, 1)
            for n in range(2):
                dve.wait_ge(proj_scaled, n + 1)
                dve.scalar_tensor_tensor(out=PM[:, 12 + n, 1:], in0=banks[n][:, 0:T - 1],
                                         scalar=par[:, R_MU + 12 + n:R_MU + 13 + n], in1=PM[:, 12 + n, 1:],
                                         op0=ALU.mult, op1=ALU.add).then_inc(proj_mixed, 1)
            with dve.Fori(0, 6) as i:
                for n in range(2):
                    dve.wait_ge(proj_scaled, 2 * i + (3 + n))
                    pm = PM[:, bass.ds(2 * i + n, 1), 1:].rearrange("p o t -> p (o t)")
                    dve.scalar_tensor_tensor(out=pm, in0=banks[n][:, 0:T - 1],
                                             scalar=par[:, bass.ds(2 * i + (R_MU + n), 1)], in1=pm,
                                             op0=ALU.mult, op1=ALU.add).then_inc(proj_mixed, 1)
            dve.wait_ge(consts, 5)
            dve.wait_ge(z_used, 12)
            dve.wait_ge(proj_mixed, 14)
            for p in range(PAIRS):
                dve.tensor_scalar(KN[:, p, :], PM[:, 4 + p, :], par[:, R_KK + p:R_KK + p + 1], None, ALU.mult)\
                    .then_inc(kp_up, 1)
            for p in range(PAIRS):
                dve.tensor_tensor_scan(out=CS[:, p, :], data0=keepm[:, :], data1=SW[:, p, :], initial=0.0,
                                       op0=ALU.mult, op1=ALU.add).then_inc(cs_scan, 1)
            for p in range(PAIRS):
                step(dve.tensor_scalar(BO[:, p, :], AI[:, p, :], -1.0, par[:, R_KA + p:R_KA + p + 1], ALU.add,
                                       ALU.mult))
                dve.scalar_tensor_tensor(out=PM[:, 4 + p, :], in0=BO[:, p, :], scalar=1.0, in1=PM[:, 4 + p, :],
                                         op0=ALU.add, op1=ALU.mult).then_inc(kp_up, 1)
            for p in range(PAIRS):
                dve.wait_ge(ss_up, p + 1)
                dve.tensor_scalar(PD[:, p, :], banks[4 + p % 2][:, :], 1e-24, None, ALU.max).then_inc(ss_max, 1)
            for p in range(PAIRS):
                dve.wait_ge(ss_root, p + 1)
                step(dve.reciprocal(PD[:, p, :], PD[:, p, :]))
                dve.scalar_tensor_tensor(out=KN[:, p, :], in0=KN[:, p, :], scalar=-1.0, in1=PD[:, p, :],
                                         op0=ALU.mult, op1=ALU.mult).then_inc(nk_up, 1)
                dve.wait_ge(nk_up, 2 * p + 1)
                dve.scalar_tensor_tensor(out=AI[:, p, :], in0=KN[:, p, :], scalar=-1.0, in1=AI[:, p, :],
                                         op0=ALU.mult, op1=ALU.mult).then_inc(nk_up, 1)
            for p in range(PAIRS):
                dve.wait_ge(rk_up, p + 1)
                dve.tensor_scalar(tmp[2 + p % 2][:, :], tmp[2 + p % 2][:, :], par[:, R_RK + p:R_RK + p + 1], None,
                                  ALU.mult).then_inc(rks_up, 1)
            for p in range(PAIRS):
                dve.wait_ge(bsum_up, p + 1)
                dve.tensor_tensor(BO[:, p, :], banks[4 + p % 2][:, :], PM[:, 8 + p, :], ALU.mult).then_inc(bo_up, 1)
            dve.wait_ge(exp_up, 2 * PAIRS)
            dve.tensor_copy(PL[:, :, :], PD[:, :, CH - 1::CH])
            dve.wait_ge(rk_up, PAIRS)
            dve.wait_ge(nk_up, 2 * PAIRS)
            for p in range(PAIRS):
                dve.tensor_tensor(PM[:, p, :], PM[:, p, :], PD[:, p, :], ALU.mult)
                dve.tensor_tensor(KN[:, p, :], KN[:, p, :], SW[:, p, :], ALU.mult)
            dve.wait_ge(gb_in, 32)
            for m, gt in ((0, gt1), (1, gt2)):
                dve.wait_ge(ada_used, 6 if m == 0 else 12)
                for h in range(2):
                    dve.tensor_tensor(gt[:, h * 512:(h + 1) * 512], banks[2 + h][:, :], gt[:, h * 512:(h + 1) * 512],
                                      ALU.add).then_inc(gate_used, 1)
                if m == 0:
                    dve.wait_ge(ada_used, 10)
                    step(dve.tensor_tensor(mod[:, 16:32], banks[6][:, 16:32],
                                           par[:, R_ADAB + 24:R_ADAB + 40], ALU.add))
                    dve.tensor_scalar(mod[:, 24:32], mod[:, 24:32], 1.0, None, ALU.add)


def emit_mixing(nc, banks, sem, v):
    attn_sink = v["attn_sink"]
    (ident, par, diag2, qT, kT, vtok, PM, AI, GG, KN, BO, PL, yT) = (
        v[n] for n in ("ident", "par", "diag2", "qT", "kT", "vtok", "PM", "AI", "GG", "KN", "BO", "PL", "yT"))
    ctx = ExitStack()
    with ctx:
        def sb(name, shape, dt=F32):
            return ctx.enter_context(nc.sbuf_tensor(name, shape, dt))

        LV = 6
        masks = sb("masks", [P, 2, P])
        lvl = sb("lvl", [P, LV, P])
        window = sb("window", [P, 2, 2 * P])
        mean2 = sb("mean2", [P, P])
        sinks = sb("sinks", [P, HEADS])
        AR = sb("AR", [P, 2, 4, P])
        Bs, Ks, Vs = (sb(n, [P, 4, P]) for n in ("Bs", "Ks", "Vs"))
        BHs, KHs = (sb(n, [P, 4, P]) for n in ("BHs", "KHs"))
        RH = sb("RH", [P, 2, HEADS, HD])
        VT = sb("VT", [P, HEADS * HD])
        BH, KH = (sb(n, [P, 2, 4, P]) for n in ("BH", "KH"))
        BM, KM = (sb(n, [P, HEADS, 2, P]) for n in ("BM", "KM"))
        PT = sb("PT", [P, HEADS, 2, P])
        NL = [[PT[:, 4 * g + 2 * b:4 * g + 2 * b + 2, :, :].rearrange("p a b c -> p (a b) c") for b in range(2)]
              for g in range(2)]
        DD, DT, XX = ([sb(f"{n}{g}", [P, 4, P]) for g in range(2)] for n in ("DD", "DT", "XX"))
        WW = sb("WW", [P, 2, HEADS, HD])
        QT = sb("QT", [P, 4, P])
        GT, HS = (sb(n, [P, 2, 4, P]) for n in ("GT", "HS"))
        dPL = sb("dPL", [P, 2, 4, P])
        S = [sb(f"S{c}", [P, 4, P]) for c in range(2)]
        Y, Yc, Yq, Yv = (sb(n, [P, 4, P]) for n in ("Y", "Yc", "Yq", "Yv"))
        qs = sb("qs", [P, 4, P])
        ks = sb("ks", [P, 2, 2 * P])
        SC = KM[:, :, :, :].rearrange("p h u k -> p h (u k)")
        mx, nm, es, rs = (sb(n, [P, HEADS]) for n in ("mx", "nm", "es", "rs"))
        ON = sb("ON", [P, HEADS * HD])

        names = ("ready sink_in ar bks vs bhs gramB maskB gramK maskK tr trA trV trB trK nl dt0 dd0 dd0c xx xxc d dc "
                 "t tc x0 x0c w wc qt qtc g gc h hc y yc st stc m mc sq va vac root rstd gn dpl "
                 "qks sc scm mx ex rsum pt ptc o oc ot otc").split()
        ev = {n: sem("mix_" + n) for n in names}
        p_dve, p_act, p_pool = sem("mix_dve"), sem("mix_act"), sem("mix_pool")
        block = ctx.enter_context(nc.Block())

        def waits(eng, n):
            def now(name, k=1, per=1):
                eng.wait_ge(ev[name], n * per + k)

            def before(name, per=1):
                eng.wait_ge(ev[name], n * per)
            return now, before

        def cols(n):
            return bass.ds(n * P, P)

        def four(ap):
            return ap.rearrange("p (a b) -> p a b", a=4)

        @block.sync
        def _(sp):
            sp.dma_start(sinks[:, :], attn_sink.rearrange("o n -> (o n)").partition_broadcast(P))\
                .then_inc(ev["sink_in"], 16)
            sp.wait_ge(ev["sink_in"], 16)

        @block.gpsimd
        def _(pool):
            step = stepper(pool, Tally(p_pool))
            step(pool.memset(masks[:, :, :], 1.0))
            for k in range(2):
                m = masks[:, k, :].rearrange("p (b w) -> p b w", b=2)
                step(pool.affine_select(out=m, in_=m, compare_op=ALU.is_ge, fill=0.0, base=k - 1,
                                        pattern=[[CH, 2], [1, CH]], channel_multiplier=-1))
                step(pool.affine_select(out=m, in_=m, compare_op=ALU.is_ge, fill=0.0, base=0,
                                        pattern=[[-CH, 2], [0, CH]], channel_multiplier=1))
            step(pool.memset(lvl[:, :, :], 1.0))
            for l in range(LV):
                w = 1 << l
                nb = P // (2 * w)
                m = lvl[:, l, :].rearrange("p (b u w) -> p b u w", u=2, w=w)
                for base, pattern, cm in ((0, [[-2 * w, nb], [0, 2], [0, w]], 1),
                                          (w - 1, [[2 * w, nb], [0, 2], [0, w]], -1),
                                          (-1, [[0, nb], [1, 2], [0, w]], 0)):
                    step(pool.affine_select(out=m, in_=m, compare_op=ALU.is_ge, fill=0.0, base=base,
                                            pattern=pattern, channel_multiplier=cm))
            step(pool.memset(window[:, :, :], 0.0))
            for base, pattern, cm in ((P, [[0, 2], [-1, 2 * P]], 1), (-1, [[0, 2], [1, 2 * P]], -1)):
                step(pool.affine_select(out=window[:, :, :], in_=window[:, :, :], compare_op=ALU.is_ge, fill=NEG,
                                        base=base, pattern=pattern, channel_multiplier=cm))
            step(pool.memset(window[:, 0, 0:P], NEG))
            for s in S:
                step(pool.memset(s[:, :, :], 0.0))
            pool.tensor_scalar(mean2[:, :], diag2[:, :], 1.0 / HD, None, ALU.mult).then_inc(ev["ready"], 1)
            with pool.Fori(0, NT) as n:
                now, before = waits(pool, n)
                before("tr", 4)
                pool.tensor_copy(Vs[:, :, :], PM[:, 8:12, cols(n)]).then_inc(ev["vs"], 1)
                decay = PL[:, :, bass.ds(2 * n, 2)].unsqueeze(3).broadcast_to([P, 4, 2, CH])
                for src, dst in ((AI[:, :, cols(n)], BHs), (PM[:, 4:8, cols(n)], KHs)):
                    pool.tensor_tensor(dst[:, :, :].rearrange("p a (c w) -> p a c w", c=2),
                                       src.rearrange("p a (c w) -> p a c w", c=2), decay, ALU.mult)\
                        .then_inc(ev["bhs"], 1)
                for l in range(1, LV):
                    for g in range(2):
                        if l == 1:
                            now("maskB", 2 * g + 2, 4)
                            before("xx", 10)
                            before("o")
                        if l >= 3:
                            now("xx", 2 * (l - 3) + g + 1, 10)
                        pool.tensor_tensor(NL[g][l % 2][:, :, :], BM[:, 4 * g:4 * g + 4, 0, :],
                                           lvl[:, l, :].unsqueeze(1).broadcast_to([P, 4, P]), ALU.mult)\
                            .then_inc(ev["nl"], 1)
                pool.wait_ge(ev["ready"], 1)
                before("gc", 2)
                for c in range(2):
                    pool.tensor_tensor(dPL[:, c, :, :], ident[:, :].unsqueeze(1).broadcast_to([P, 4, P]),
                                       PL[:, :, bass.ds(2 * n + c, 1)].broadcast_to([P, 4, P]), ALU.mult)\
                        .then_inc(ev["dpl"], 1)

        @block.scalar
        def _(act):
            with act.Fori(0, NT) as n:
                now, before = waits(act, n)
                before("gramK", 4)
                before("qtc")
                act.activation(AR[:, 0, :, :], KN[:, :, cols(n)], ACT.Copy).then_inc(ev["ar"], 1)
                act.activation(AR[:, 1, :, :], PM[:, 0:4, cols(n)], ACT.Copy).then_inc(ev["ar"], 1)
                before("sc", 4)
                act.activation(qs[:, :, :], qT[:, :, cols(n)], ACT.Copy).then_inc(ev["qks"], 1)
                act.activation(ks[:, :, :], kT[:, :, bass.ds(n * P, 2 * P)], ACT.Copy).then_inc(ev["qks"], 1)
                now("tr", 1, 4)
                before("w", 2)
                act.activation(RH[:, 0, :, :].rearrange("p h d -> p (h d)"), banks[4][:, :], ACT.Copy)\
                    .then_inc(ev["trA"], 1)
                now("tr", 2, 4)
                before("st", 2)
                act.activation(VT[:, :], banks[5][:, :], ACT.Copy).then_inc(ev["trV"], 1)
                for j, (dst, name) in enumerate(((BH, "trB"), (KH, "trK"))):
                    now("tr", 3 + j, 4)
                    for c in range(2):
                        act.activation(dst[:, c, :, :], four(banks[6 + j][:, :]), ACT.Copy,
                                       scale=diag2[:, CH * c:CH * c + 1]).then_inc(ev[name], 1)
                for g in range(2):
                    now("dd0", g + 1, 2)
                    act.activation(DD[g][:, :, :], four(banks[g][:, :]), ACT.Copy).then_inc(ev["dd0c"], 1)
                for l in range(1, LV):
                    for g in range(2):
                        if l < LV - 1:
                            now("d", 2 * (l - 1) + g + 1, 8)
                            act.activation(DD[g][:, :, :], four(banks[2 + g][:, :]), ACT.Copy)\
                                .then_inc(ev["dc"], 1)
                        now("t", 2 * (l - 1) + g + 1, 10)
                        act.activation(DT[g][:, :, :], four(banks[6 + g][:, :]), ACT.Copy).then_inc(ev["tc"], 1)
                now("x0")
                act.activation(RH[:, 1, :, :].rearrange("p h d -> p (h d)"), banks[4][:, :], ACT.Copy)\
                    .then_inc(ev["x0c"], 1)
                for g in range(2):
                    now("w", g + 1, 2)
                    act.activation(WW[:, :, 4 * g:4 * g + 4, :],
                                   banks[g][:, :].rearrange("p (h u d) -> p u h d", u=2, d=HD), ACT.Copy)\
                        .then_inc(ev["wc"], 1)
                now("y")
                before("m")
                act.activation(Y[:, :, :], four(banks[4][:, :]), ACT.Copy).then_inc(ev["yc"], 1)
                now("mc")
                act.activation(Yq[:, :, :], Yc[:, :, :], ACT.Square).then_inc(ev["sq"], 1)
                now("vac")
                act.activation(Yv[:, :, :], Yv[:, :, :], ACT.Sqrt).then_inc(ev["root"], 1)
                now("mx")
                before("rsum")
                act.activation(es[:, :], es[:, :], ACT.Exp).then_inc(ev["ex"], 1)
                for h in range(HEADS):
                    act.activation(SC[:, h, :], SC[:, h, :], ACT.Exp, bias=nm[:, h:h + 1],
                                   accum_out=rs[:, h:h + 1]).then_inc(ev["ex"], 1)
                for j in range(4):
                    now("pt", j + 1, 4)
                    act.activation(PT[:, 2 * j:2 * j + 2, :, :].rearrange("p h k q -> p (h k q)"),
                                   banks[2 + j][:, :], ACT.Copy).then_inc(ev["ptc"], 1)
                now("ot")
                act.activation(yT[:, 0:4, cols(n)], four(banks[7][:, :]), ACT.Copy).then_inc(ev["otc"], 1)

        @block.tensor
        def _(pe):
            pe.wait_ge(ev["ready"], 1)
            with pe.Fori(0, NT) as n:
                now, before = waits(pe, n)

                def grams(src, first, name):
                    for g in range(2):
                        for e in range(2):
                            for j in range(2):
                                p = 2 * g + j
                                rows = slice(64 * e, 64 * e + 64)
                                last = pe.matmul(banks[first + 2 * g + e][:, 256 * j:256 * j + 256],
                                                 src[rows, p, :], AR[rows, :, p, :], start=True, stop=True)
                            last.then_inc(ev[name], 1)
                now("ar", 2, 2)
                now("bks", 2, 2)
                before("gn")
                before("otc")
                grams(Bs, 0, "gramB")
                now("vs")
                now("bhs", 2, 2)
                for b, src in ((4, AR[:, 0]), (5, Vs), (6, BHs), (7, KHs)):
                    for p in range(4):
                        last = pe.transpose(banks[b][:, p * P:(p + 1) * P],
                                            src[:, p, :], ident[:, :])
                    last.then_inc(ev["tr"], 1)
                for g in range(2):
                    now("dt0", g + 1, 2)
                    for h in range(4):
                        last = pe.transpose(banks[g][:, h * P:(h + 1) * P], DT[g][:, h, :], ident[:, :])
                    last.then_inc(ev["dd0"], 1)
                now("maskB", 4, 4)
                now("trV")
                grams(Ks, 2, "gramK")
                for l in range(1, LV):
                    for g in range(2):
                        now("nl", 2 * (l - 1) + g + 1, 10)
                        if l == 1:
                            now("dd0c", g + 1, 2)
                        else:
                            now("dc", 2 * (l - 2) + g + 1, 8)
                        for h in range(4):
                            last = pe.matmul(banks[g][:, h * P:(h + 1) * P], NL[g][l % 2][:, h, :],
                                             DD[g][:, h, :], start=True, stop=True)
                        last.then_inc(ev["xx"], 1)
                    for g in range(2):
                        now("xxc", 2 * (l - 1) + g + 1, 10)
                        if l == 1:
                            now("maskK", 4, 4)
                            now("trK", 2, 2)
                        else:
                            now("tc", 2 * (l - 2) + g + 1, 10)
                        if l < LV - 1:
                            for h in range(4):
                                last = pe.matmul(banks[2 + g][:, h * P:(h + 1) * P], DT[g][:, h, :],
                                                 XX[g][:, h, :], start=True, stop=True)
                            last.then_inc(ev["d"], 1)
                        for h in range(4):
                            last = pe.matmul(banks[6 + g][:, h * P:(h + 1) * P], XX[g][:, h, :],
                                             DT[g][:, h, :], start=True, stop=True)
                        last.then_inc(ev["t"], 1)
                for h in range(HEADS):
                    last = pe.matmul(banks[4][:, h * HD:(h + 1) * HD], KM[:, h, 0, :],
                                     VT[:, h * HD:(h + 1) * HD], start=True, stop=True)
                last.then_inc(ev["x0"], 1)
                now("x0c")
                now("tc", 10, 10)
                for g in range(2):
                    for h in range(4):
                        last = pe.matmul(banks[g][:, h * P:(h + 1) * P], DT[g][:, h, :],
                                         RH[:, :, 4 * g + h, :], start=True, stop=True)
                    last.then_inc(ev["w"], 1)
                now("wc", 2, 2)
                for h in range(HEADS):
                    last = pe.matmul(banks[5][64 * (h % 2):64 * (h % 2) + 64, (h // 2) * P:(h // 2 + 1) * P],
                                     WW[:, 0, h, :], BM[:, h, 1, :], start=True, stop=True)
                last.then_inc(ev["qt"], 1)
                for c in range(2):
                    for p in range(4):
                        last = pe.matmul(banks[2 + c][:, p * P:(p + 1) * P], WW[:, 0, 2 * p:2 * p + 2, :],
                                         BH[:, c, p, :], start=True, stop=True)
                    last.then_inc(ev["g"], 1)
                    for p in range(4):
                        pe.matmul(banks[6 + c][:, p * P:(p + 1) * P], BH[:, c, p, :],
                                  WW[:, 1, 2 * p:2 * p + 2, :], start=True, stop=False)
                        last = pe.matmul(banks[6 + c][:, p * P:(p + 1) * P], KH[:, c, p, :],
                                         VT[:, p * P:(p + 1) * P], start=False, stop=True)
                    last.then_inc(ev["h"], 1)
                for e in range(2):
                    for p in range(4):
                        h = 2 * p + e
                        o = banks[4][64 * e:64 * e + 64, p * P:(p + 1) * P]
                        pe.matmul(o, WW[:, 1, h, :], BM[:, h, 1, :], start=(p == 0), stop=False,
                                  skip_group_check=True)
                        pe.matmul(o, VT[:, h * HD:(h + 1) * HD], KM[:, h, 1, :], start=False, stop=False,
                                  skip_group_check=True)
                now("qtc")
                for c in range(2):
                    if c == 0:
                        before("stc", 2)
                    else:
                        now("stc", 1, 2)
                    for p in range(4):
                        o = banks[4][:, p * P + CH * c:p * P + CH * c + CH]
                        last = pe.matmul(o, S[c][:, p, :], QT[:, p, CH * c:CH * c + CH], start=False, stop=True,
                                         skip_group_check=True)
                    if c == 1:
                        last.then_inc(ev["y"], 1)
                    now("gc", c + 1, 2)
                    for p in range(4):
                        last = pe.matmul(banks[c][:, p * P:(p + 1) * P], GT[:, c, p, :], S[c][:, p, :],
                                         start=True, stop=True)
                    last.then_inc(ev["st"], 1)
                now("qks", 2, 2)
                now("hc", 2, 2)
                for g in range(2):
                    for e in range(2):
                        b = (2, 3, 6, 7)[2 * g + e]
                        for j in range(2):
                            rows = slice(64 * e, 64 * e + 64)
                            last = pe.matmul(banks[b][:, 256 * j:256 * j + 256], qs[rows, 2 * g + j, :],
                                             ks[rows, g, :], start=True, stop=True)
                        last.then_inc(ev["sc"], 1)
                now("yc")
                pe.matmul(banks[5][:, :], mean2[:, :], Y[:, :, :].rearrange("p a b -> p (a b)"), start=True,
                          stop=True).then_inc(ev["m"], 1)
                now("sq")
                pe.matmul(banks[5][:, :], mean2[:, :], Yq[:, :, :].rearrange("p a b -> p (a b)"), start=True,
                          stop=True).then_inc(ev["va"], 1)
                now("vac")
                now("scm", 4, 4)
                now("ex", 9, 9)
                for j in range(4):
                    for h in (2 * j, 2 * j + 1):
                        for k in range(2):
                            last = pe.transpose(banks[2 + j][:, (h % 2) * 256 + k * P:(h % 2) * 256 + (k + 1) * P],
                                                SC[:, h, k * P:(k + 1) * P], ident[:, :])
                    last.then_inc(ev["pt"], 1)
                for h in range(HEADS):
                    now("ptc", h // 2 + 1, 4)
                    for k in range(2):
                        last = pe.matmul(banks[6][:, h * HD:(h + 1) * HD], PT[:, h, k, :],
                                         vtok[:, bass.ds(n + k, 1), 64 * (h // 4):64 * (h // 4) + 64]
                                         .rearrange("p o d -> p (o d)"), start=(k == 0), stop=(k == 1))
                last.then_inc(ev["o"], 1)
                now("oc")
                for p in range(4):
                    last = pe.transpose(banks[7][:, p * P:(p + 1) * P], ON[:, p * P:(p + 1) * P], ident[:, :])
                last.then_inc(ev["ot"], 1)

        @block.vector
        def _(dve):
            per = 12
            chain = Tally(p_dve)
            dve.wait_ge(ev["ready"], 1)
            dve.wait_ge(ev["sink_in"], 16)
            with dve.Fori(0, NT) as n:
                now, before = waits(dve, n)
                chain.enter(n, per)
                step = stepper(dve, chain)
                before("gramK", 4)
                dve.tensor_copy(Bs[:, :, :], AI[:, :, cols(n)]).then_inc(ev["bks"], 1)
                dve.tensor_copy(Ks[:, :, :], PM[:, 4:8, cols(n)]).then_inc(ev["bks"], 1)

                def mask(bank, dst, name, g, e):
                    dve.tensor_tensor(dst[:, 4 * g + e:4 * g + e + 3:2, :, :].rearrange("p h u t -> p h (u t)"),
                                      banks[bank][:, :].rearrange("p (h u) -> p h u", h=2),
                                      masks[:, :, :].rearrange("p u t -> p (u t)").unsqueeze(1)
                                      .broadcast_to([P, 2, 2 * P]), ALU.mult).then_inc(ev[name], 1)
                before("y")
                for g in range(2):
                    for e in range(2):
                        now("gramB", 2 * g + e + 1, 4)
                        mask(2 * g + e, BM, "maskB", g, e)
                for g in range(2):
                    now("maskB", 2 * g + 2, 4)
                    before("w", 2)
                    step(dve.tensor_tensor(DT[g][:, :, :], BM[:, 4 * g:4 * g + 4, 0, :],
                                           lvl[:, 0, :].unsqueeze(1).broadcast_to([P, 4, P]), ALU.mult))
                    dve.tensor_tensor(DT[g][:, :, :], DT[g][:, :, :],
                                      ident[:, :].unsqueeze(1).broadcast_to([P, 4, P]), ALU.add)\
                        .then_inc(ev["dt0"], 1)
                for g in range(2):
                    for e in range(2):
                        now("gramK", 2 * g + e + 1, 4)
                        mask(2 + 2 * g + e, KM, "maskK", g, e)
                for l in range(1, LV):
                    for g in range(2):
                        now("xx", 2 * (l - 1) + g + 1, 10)
                        dve.tensor_tensor(XX[g][:, :, :], four(banks[g][:, :]),
                                          ident[:, :].unsqueeze(1).broadcast_to([P, 4, P]), ALU.add)\
                            .then_inc(ev["xxc"], 1)
                now("qt")
                dve.tensor_tensor(QT[:, :, :], four(banks[5][:, :]), AR[:, 1, :, :], ALU.add)\
                    .then_inc(ev["qtc"], 1)
                dg = diag2[:, :].unsqueeze(1).broadcast_to([P, 4, P])
                for c in range(2):
                    now("g", c + 1, 2)
                    now("dpl", c + 1, 2)
                    step(dve.tensor_tensor(GT[:, c, :, :], four(banks[2 + c][:, :]), dg, ALU.mult))
                    dve.tensor_tensor(GT[:, c, :, :], GT[:, c, :, :], dPL[:, c, :, :], ALU.add)\
                        .then_inc(ev["gc"], 1)
                    now("h", c + 1, 2)
                    dve.tensor_tensor(HS[:, c, :, :], four(banks[6 + c][:, :]), dg, ALU.mult)\
                        .then_inc(ev["hc"], 1)
                for c in range(2):
                    now("st", c + 1, 2)
                    now("hc", c + 1, 2)
                    if c == 0:
                        before("y")
                    dve.tensor_tensor(S[1 - c][:, :, :], four(banks[c][:, :]), HS[:, c, :, :], ALU.add)\
                        .then_inc(ev["stc"], 1)
                now("m")
                dve.tensor_tensor(Yc[:, :, :], Y[:, :, :], four(banks[5][:, :]), ALU.subtract)\
                    .then_inc(ev["mc"], 1)
                now("va")
                dve.tensor_scalar(Yv[:, :, :], four(banks[5][:, :]), GN_EPS, None, ALU.add).then_inc(ev["vac"], 1)
                for g in range(2):
                    for e in range(2):
                        now("sc", 2 * g + e + 1, 4)
                        b = (2, 3, 6, 7)[2 * g + e]
                        last = dve.tensor_tensor(
                            SC[:, 4 * g + e:4 * g + e + 3:2, :], banks[b][:, :].rearrange("p (h k) -> p h k", h=2),
                            window[:, bass.ds((n + 3) // 4, 1), :].broadcast_to([P, 2, 2 * P]), ALU.add)
                        last.then_inc(ev["scm"], 1)
                now("scm", 4, 4)
                step(dve.tensor_reduce(mx[:, :], SC[:, :, :], AX.X, ALU.max))
                step(dve.tensor_tensor(mx[:, :], mx[:, :], sinks[:, :], ALU.max))
                dve.tensor_scalar(nm[:, :], mx[:, :], -1.0, None, ALU.mult)
                dve.tensor_tensor(es[:, :], sinks[:, :], mx[:, :], ALU.subtract).then_inc(ev["mx"], 1)
                now("root")
                lx = [par[:, r:r + 4].unsqueeze(2).broadcast_to([P, 4, P]) for r in (R_LXG, R_LXB)]
                step(dve.reciprocal(Yv[:, :, :], Yv[:, :, :]))
                step(dve.tensor_tensor(Yc[:, :, :], Yc[:, :, :], Yv[:, :, :], ALU.mult))
                step(dve.tensor_tensor(Yc[:, :, :], Yc[:, :, :], lx[0], ALU.mult))
                step(dve.tensor_tensor(Yc[:, :, :], Yc[:, :, :], lx[1], ALU.add))
                step(dve.tensor_tensor(Yc[:, :, :], Yc[:, :, :], BO[:, :, cols(n)], ALU.add))
                dve.tensor_tensor(yT[:, 4:8, cols(n)], Yc[:, :, :], GG[:, :, cols(n)], ALU.mult)\
                    .then_inc(ev["gn"], 1)
                now("ex", 9, 9)
                step(dve.tensor_tensor(rs[:, :], rs[:, :], es[:, :], ALU.add))
                dve.reciprocal(rs[:, :], rs[:, :]).then_inc(ev["rsum"], 1)
                now("rsum")
                now("o")
                before("ot")
                dve.tensor_tensor(ON[:, :].rearrange("p (h d) -> p h d", h=HEADS),
                                  banks[6][:, :].rearrange("p (h d) -> p h d", h=HEADS),
                                  rs[:, :].unsqueeze(2).broadcast_to([P, HEADS, HD]), ALU.mult)\
                    .then_inc(ev["oc"], 1)
                chain.leave(NT)


TB = 64


class Norm:

    def __init__(self, nc, sb, prefix):
        self.nc = nc
        self.stats = [sb(f"{prefix}stats{i}", [P, 2, 6]) for i in range(2)]
        self.mv = [sb(f"{prefix}mv{i}", [P, 2]) for i in range(2)]
        self.sd = [sb(f"{prefix}sd{i}", [P, 1]) for i in range(2)]

    def moments(self, dve, step, t, tile):
        for h in range(2):
            last = dve.bn_stats(out=self.stats[t % 2][:, h, :], in_=tile[:, 512 * h:512 * h + 512])
        step(last)
        step(dve.bn_aggr(out=self.mv[t % 2][:, :], in_=self.stats[t % 2][:, :, :].rearrange("p a b -> p (a b)")))
        return dve.tensor_scalar(self.sd[t % 2][:, :], self.mv[t % 2][:, 1:2], LN_EPS, None, ALU.add)

    def root(self, act, t):
        return act.activation(self.sd[t % 2][:, :], self.sd[t % 2][:, :], ACT.Sqrt)

    def scaled(self, dve, step, t, tile):
        step(dve.reciprocal(self.sd[t % 2][:, :], self.sd[t % 2][:, :]))
        return dve.tensor_scalar(tile, tile, self.mv[t % 2][:, 0:1], self.sd[t % 2][:, :], ALU.subtract, ALU.mult)


def emit_mix_out(nc, banks, sem, v):
    x, w_out, ln1_g, ln1_b, ident, mod, gt1, yT, x1, h2, hh, hl = (
        v[n] for n in ("x", "w_out", "ln1_g", "ln1_b", "ident", "mod", "gt1", "yT", "x1", "h2", "hh", "hl"))
    ctx = ExitStack()
    with ctx:
        def sb(name, shape, dt=F32):
            return ctx.enter_context(nc.sbuf_tensor(name, shape, dt))

        wo = [sb(f"wo{k}", [P, D]) for k in range(KD)]
        xs = sb("xs", [P, NT, D])
        lg, lb = sb("lg", [P, D]), sb("lb", [P, D])
        norm = Norm(nc, sb, "n1_")
        wo_in = [sem(f"wo_in{k}") for k in range(KD)]
        xs_in, ln_in = sem("xs_in"), sem("ln_in")
        y_up, y_used, var_up, root_up = sem("y_up"), sem("y_used"), sem("var_up"), sem("root_up")
        centred, gained, x1_up = sem("centred"), sem("gained"), sem("x1_up")
        xt_up, h_up, hh_up, hl_up = sem("x1t_up"), sem("h2_up"), sem("hh_up"), sem("hl_up")
        p_dve = sem("p_dve3")
        block = ctx.enter_context(nc.Block())

        @block.sync
        def _(sp):
            wv = w_out[0].rearrange("(k p) n -> k p n", p=P)
            for k in range(KD):
                sp.dma_start(wo[k][:, :], wv[k]).then_inc(wo_in[k], 16)
            sp.dma_start(xs[:, :, :], x[0].rearrange("(t p) d -> p t d", p=P)).then_inc(xs_in, 16)
            for dst, src in ((lg, ln1_g), (lb, ln1_b)):
                sp.dma_start(dst[:, :], src.rearrange("o n -> (o n)").partition_broadcast(P)).then_inc(ln_in, 16)
            sp.wait_ge(ln_in, 32)

        @block.tensor
        def _(pe):
            def turn(t):
                pe.wait_ge(x1_up, t + 1)
                for h in range(2):
                    for k in range(4):
                        last = pe.transpose(banks[4 + 2 * (t % 2) + h][:, k * P:(k + 1) * P],
                                            x1[:, t, (4 * h + k) * P:(4 * h + k + 1) * P], ident[:, :])
                    last.then_inc(xt_up, 1)
            for t in range(NT):
                if t >= 2:
                    pe.wait_ge(y_used, 2 * (t - 1))
                for h in range(2):
                    for k in range(KD):
                        if t == 0 and h == 0:
                            pe.wait_ge(wo_in[k], 16)
                        last = pe.matmul(banks[2 * (t % 2) + h][:, :], yT[:, k, t * P:(t + 1) * P],
                                         wo[k][:, 512 * h:512 * h + 512], start=(k == 0), stop=(k == KD - 1))
                    last.then_inc(y_up, 1)
                if t >= 1:
                    if t >= 3:
                        pe.wait_ge(h_up, 8 * (t - 2))
                    turn(t - 1)
            pe.wait_ge(h_up, 8 * (NT - 2))
            turn(NT - 1)

        def split(dve, t):
            cols = slice(t * P, (t + 1) * P)
            dve.wait_ge(h_up, 8 * (t + 1))
            dve.tensor_copy(hh[:, :, cols], h2[:, :, cols]).then_inc(hh_up, 1)
            dve.wait_ge(hh_up, t + 1)
            dve.tensor_tensor(hl[:, :, cols], h2[:, :, cols], hh[:, :, cols].bitcast(F32), ALU.subtract)\
                .then_inc(hl_up, 1)

        @block.vector
        def _(dve):
            step = stepper(dve, Tally(p_dve))
            def head(t):
                for h in range(2):
                    half = slice(512 * h, 512 * h + 512)
                    dve.wait_ge(y_up, 2 * t + h + 1)
                    ins = dve.tensor_tensor(x1[:, t, half], banks[2 * (t % 2) + h][:, :], gt1[:, half], ALU.mult)
                    ins.then_inc(y_used, 1)
                dve.wait_ge(xs_in, 16)
                dve.wait_ge(y_used, 2 * t + 2)
                step(dve.scalar_tensor_tensor(out=x1[:, t, :], in0=xs[:, t, :], scalar=ALPHA, in1=x1[:, t, :],
                                              op0=ALU.mult, op1=ALU.add))
                norm.moments(dve, step, t, x1[:, t, :]).then_inc(var_up, 1)

            def tail(t):
                dve.wait_ge(root_up, t + 1)
                norm.scaled(dve, step, t, x1[:, t, :]).then_inc(centred, 1)
                dve.wait_ge(gained, t + 1)
                dve.tensor_tensor(x1[:, t, :], x1[:, t, :], lb[:, :], ALU.add).then_inc(x1_up, 1)
            dve.wait_ge(ln_in, 32)
            for t in range(NT):
                head(t)
                tail(t)
                if t >= 1:
                    split(dve, t - 1)
            split(dve, NT - 1)

        @block.gpsimd
        def _(pool):
            pool.wait_ge(ln_in, 32)
            for t in range(NT):
                pool.wait_ge(centred, t + 1)
                pool.tensor_tensor(x1[:, t, :], x1[:, t, :], lg[:, :], ALU.mult).then_inc(gained, 1)

        @block.scalar
        def _(act):
            for t in range(NT):
                act.wait_ge(var_up, t + 1)
                norm.root(act, t).then_inc(root_up, 1)
                for k in range(KD):
                    act.wait_ge(xt_up, 2 * t + k // 4 + 1)
                    act.activation(h2[:, k, t * P:(t + 1) * P],
                                   banks[4 + 2 * (t % 2) + k // 4][:, (k % 4) * P:(k % 4 + 1) * P], ACT.Identity,
                                   bias=mod[:, 16 + k:17 + k], scale=mod[:, 24 + k:25 + k]).then_inc(h_up, 1)


class ExpertScores:

    def __init__(self, nc, sb, sem, prefix, banks, ident, hh, hl, ring, peer_u):
        self.nc, self.banks, self.ident, self.hh, self.hl, self.ring = nc, banks, ident, hh, hl, ring
        self.u = [sb(f"{prefix}u{s}", [P, D]) for s in range(4)]
        self.uraw = sb(prefix + "uraw", [P, KD, P])
        self.uh = [sb(f"{prefix}uh{s}", [P, KD, P], F32R) for s in range(2)]
        self.ul = [sb(f"{prefix}ul{s}", [P, KD, P], F32R) for s in range(2)]
        self.u_in = [sem(f"{prefix}u_in{s}") for s in range(4)]
        self.turned, self.uh_up, self.uraw_up, self.ul_up, self.a_up, self.gelu_up = (
            sem(prefix + n) for n in ("turned", "uh_up", "uraw_up", "ul_up", "a_up", "gelu_up"))
        self.src = peer_u[0].rearrange("(i j) d -> i j d", j=NKEYS)

    def load(self, sp, i, s, tile):
        sp.dma_start(self.u[s][:, :], self.src[:, tile, :]).then_inc(self.u_in[s], 16)

    def turn(self, pe, i, s):
        pe.wait_ge(self.u_in[s], 16 * i + 16)
        for h in range(2):
            pe.wait_ge(self.uraw_up, 8 * i + max(2 * s + h - 1, 0))
            for k in range(4):
                last = pe.transpose(self.banks[2 + h][:, k * P:(k + 1) * P],
                                    self.u[s][:, (4 * h + k) * P:(4 * h + k + 1) * P], self.ident[:, :])
            last.then_inc(self.turned, 1)

    def product(self, pe, i, s):
        pe.wait_ge(self.uh_up, 8 * i + 2 * s + 2)
        pe.wait_ge(self.gelu_up, 4 * i + max(s - 1, 0))
        bank = self.banks[s % 2]
        for k in range(KD):
            pe.matmul(bank[:, :], self.uh[s % 2][:, k, :], self.hh[:, k, :], start=(k == 0), stop=False)
            pe.matmul(bank[:, :], self.uh[s % 2][:, k, :], self.hl[:, k, :], start=False, stop=False)
        pe.wait_ge(self.ul_up, 4 * i + s + 1)
        for k in range(KD):
            last = pe.matmul(bank[:, :], self.ul[s % 2][:, k, :], self.hh[:, k, :], start=False,
                             stop=(k == KD - 1))
        last.then_inc(self.a_up, 1)

    def evacuate(self, act, i, s):
        act.wait_ge(self.a_up, 4 * i + max(s - 1, 0))
        for h in range(2):
            act.wait_ge(self.turned, 8 * i + 2 * s + h + 1)
            act.activation(self.uh[s % 2][:, 4 * h:4 * h + 4, :],
                           self.banks[2 + h][:, :].rearrange("p (k e) -> p k e", k=4), ACT.Copy)\
                .then_inc(self.uh_up, 1)
            if h == 0:
                act.wait_ge(self.ul_up, 4 * i + s)
            act.activation(self.uraw[:, 4 * h:4 * h + 4, :],
                           self.banks[2 + h][:, :].rearrange("p (k e) -> p k e", k=4), ACT.Copy)\
                .then_inc(self.uraw_up, 1)

    def remainder(self, pool, i, s):
        pool.wait_ge(self.uraw_up, 8 * i + 2 * s + 2)
        pool.wait_ge(self.uh_up, 8 * i + 2 * s + 2)
        pool.wait_ge(self.a_up, 4 * i + max(s - 1, 0))
        pool.tensor_tensor(self.ul[s % 2][:, :, :], self.uraw[:, :, :], self.uh[s % 2][:, :, :].bitcast(F32),
                           ALU.subtract).then_inc(self.ul_up, 1)

    def gelu(self, act, i, s, slot):
        act.wait_ge(self.a_up, 4 * i + s + 1)
        act.activation(self.ring[:, slot, :], self.banks[s % 2][:, :], ACT.Gelu).then_inc(self.gelu_up, 1)


def emit_routing(nc, banks, sem, v):
    peer_wq, peer_subkeys, peer_u, ident, h2, hh, hl, ring, FV, IS, JS = (
        v[n] for n in ("peer_wq", "peer_subkeys", "peer_u", "ident", "h2", "hh", "hl", "ring", "FV", "IS", "JS"))
    ctx = ExitStack()
    with ctx:
        def sb(name, shape, dt=F32):
            return ctx.enter_context(nc.sbuf_tensor(name, shape, dt))

        wq = [sb(f"wq{c}", [P, KD, P]) for c in range(2)]
        sk = [sb(f"sk{c}", [P, P]) for c in range(2)]
        skT = [sb(f"skT{c}", [P, P]) for c in range(2)]
        q2 = [sb(f"q2{c}", [P, T]) for c in range(2)]
        SS = sb("SS", [P, HEADS, 2, NT, NKEYS])
        st = sb("st", [P, 8, NKEYS])
        st2 = sb("st2", [P, 8, NKEYS])
        cand, cand2 = (m[:, :, :].rearrange("p (t a) (c b) -> p t (a c) b", t=NT, b=TOPK) for m in (st, st2))
        sv = sb("sv", [P, 8, TOPK])
        si = sb("si", [P, 8, TOPK], U32)
        sif = sb("sif", [P, 8, TOPK])
        fv = sb("fv", [P, NT, TOPK])
        fp = sb("fp", [P, NT, TOPK], U32)
        fa = [sb(f"fa{c}", [P, NT * TOPK], U32) for c in range(2)]
        ff = [sb(f"ff{c}", [P, NT * TOPK]) for c in range(2)]
        iota16 = sb("iota16", [P, TOPK])
        gatepost = sb("gatepost", [P, 1])
        scores = ExpertScores(nc, sb, sem, "r_", banks, ident, hh, hl, ring, peer_u)
        wq_in = [sem(f"wq_in{c}") for c in range(2)]
        sk_in = [sem(f"sk_in{c}") for c in range(2)]
        q_up, q_out, k_up, k_out, s_up, s_out = (sem(n) for n in ("q_up", "q_out", "k_up", "k_out", "s_up", "s_out"))
        iota_up, p_dve = sem("iota_up"), sem("p_dve4")
        block = ctx.enter_context(nc.Block())

        @block.sync
        def _(sp):
            wv = peer_wq[0].rearrange("(k p) n -> p k n", p=P)
            kv = peer_subkeys[0].rearrange("h c n d -> n (h c) d")
            with sp.Fori(0, HEADS) as h:
                for c in range(2):
                    sp.wait_ge(q_up, 2 * h)
                    sp.dma_start(wq[c][:, :, :], wv[:, :, bass.ds((2 * h + c) * P, P)]).then_inc(wq_in[c], 16)
                    sp.wait_ge(k_up, 2 * h)
                    sp.dma_start(sk[c][:, :], kv[:, bass.ds(2 * h + c, 1), :].rearrange("n o d -> n (o d)"))\
                        .then_inc(sk_in[c], 16)
            with sp.Fori(0, AHEAD) as i:
                for s in range(4):
                    sp.wait_ge(scores.turned, 8 * i)
                    scores.load(sp, i, s, bass.ds(4 * i + s, 1))

        @block.gpsimd
        def _(pool):
            pool.iota(iota16[:, :], pattern=[[1, TOPK]], base=0, channel_multiplier=0,
                      allow_small_or_imprecise_dtypes=True).then_inc(iota_up, 1)
            with pool.Fori(0, AHEAD) as i:
                for s in range(4):
                    scores.remainder(pool, i, s)

        @block.tensor
        def _(pe):
            with pe.Fori(0, HEADS) as h:
                for c in range(2):
                    pe.wait_ge(wq_in[c], 16 * h + 16)
                    pe.wait_ge(q_out, 2 * h)
                    for k in range(KD):
                        last = pe.matmul(banks[c][:, :], wq[c][:, k, :], h2[:, k, :], start=(k == 0),
                                         stop=(k == KD - 1))
                    last.then_inc(q_up, 1)
                    pe.wait_ge(sk_in[c], 16 * h + 16)
                    pe.wait_ge(k_out, 2 * h)
                    pe.transpose(banks[2 + c][:, 0:P], sk[c][:, :], ident[:, :]).then_inc(k_up, 1)
                for c in range(2):
                    pe.wait_ge(q_out, 2 * h + (c + 1))
                    pe.wait_ge(k_out, 2 * h + (c + 1))
                    pe.wait_ge(s_out, 2 * h)
                    for t in range(NT):
                        last = pe.matmul(banks[4 + c][:, t * P:(t + 1) * P], q2[c][:, t * P:(t + 1) * P],
                                         skT[c][:, :], start=True, stop=True)
                    last.then_inc(s_up, 1)
            pe.wait_ge(q_out, 2 * HEADS)
            pe.wait_ge(k_out, 2 * HEADS)
            with pe.Fori(0, AHEAD) as i:
                scores.turn(pe, i, 0)
                for s in range(4):
                    if s < 3:
                        scores.turn(pe, i, s + 1)
                    scores.product(pe, i, s)

        @block.scalar
        def _(act):
            with act.Fori(0, HEADS) as h:
                for c in range(2):
                    act.wait_ge(q_up, 2 * h + (c + 1))
                    act.wait_ge(s_up, 2 * h)
                    act.activation(q2[c][:, :], banks[c][:, :], ACT.Copy).then_inc(q_out, 1)
                    act.wait_ge(k_up, 2 * h + (c + 1))
                    act.activation(skT[c][:, :], banks[2 + c][:, 0:P], ACT.Copy).then_inc(k_out, 1)
                for c in range(2):
                    act.wait_ge(s_up, 2 * h + (c + 1))
                    act.activation(SS[:, bass.ds(h, 1), c, :, :].rearrange("p o t n -> p (o t n)"),
                                   banks[4 + c][:, :], ACT.Copy).then_inc(s_out, 1)
            with act.Fori(0, AHEAD) as i:
                scores.evacuate(act, i, 0)
                for s in range(4):
                    if s < 3:
                        scores.evacuate(act, i, s + 1)
                    scores.gelu(act, i, s, bass.ds(4 * i + s, 1))

        @block.vector
        def _(dve):
            per = 16
            chain = Tally(p_dve)
            dve.wait_ge(iota_up, 1)
            with dve.Fori(0, HEADS) as h:
                chain.enter(h, per)
                step = stepper(dve, chain)

                def settled(ins):
                    step(ins)
                    dve.tensor_copy(gatepost[:, :], iota16[:, 0:1])

                def best16(src, spare, vals, places, n):
                    for u in range(n):
                        last = dve.max(vals[:, u, 0:8], src[u])
                    settled(last)
                    for u in range(n):
                        last = dve.max_index(places[:, u, 0:8], vals[:, u, 0:8], src[u])
                    for u in range(n):
                        last = dve.match_replace(spare[u], vals[:, u, 0:8], src[u], -3.0e38)
                    settled(last)
                    for u in range(n):
                        last = dve.max(vals[:, u, 8:16], spare[u])
                    settled(last)
                    for u in range(n):
                        last = dve.max_index(places[:, u, 8:16], vals[:, u, 8:16], spare[u])
                    settled(last)
                dve.wait_ge(s_out, 2 * h + 2)
                settled(dve.tensor_copy(st[:, :, :], SS[:, bass.ds(h, 1), :, :, :]
                                        .rearrange("p o c t n -> p (o c t) n")))
                best16([st[:, u, :] for u in range(8)], [st2[:, u, :] for u in range(8)], sv, si, 8)
                dve.tensor_copy(sif[:, :, :], si[:, :, :])
                settled(dve.tensor_tensor(cand[:, :, :, :], sv[:, 0:4, :].unsqueeze(3).broadcast_to([P, NT, TOPK, TOPK]),
                                       sv[:, 4:8, :].unsqueeze(2).broadcast_to([P, NT, TOPK, TOPK]), ALU.add))
                flat = [[m[:, t, :, :].rearrange("p a b -> p (a b)") for t in range(NT)] for m in (cand, cand2)]
                best16(flat[0], flat[1], fv, fp, NT)
                dve.tensor_copy(FV[:, :, bass.ds(h, 1), :].rearrange("p t o k -> p t (o k)"), fv[:, :, :])
                fpf = fp[:, :, :].rearrange("p t k -> p (t k)")
                dve.tensor_scalar(fa[0][:, :], fpf, 4, None, ALU.logical_shift_right)
                step(dve.tensor_scalar(fa[1][:, :], fpf, 15, None, ALU.bitwise_and))
                dve.tensor_copy(ff[0][:, :], fa[0][:, :])
                step(dve.tensor_copy(ff[1][:, :], fa[1][:, :]))
                for c, work, dst in ((0, cand, IS), (1, cand2, JS)):
                    one = work[:, :, :, :].rearrange("p t k a -> p (t k) a")
                    last = dve.tensor_tensor(one, ff[c][:, :].unsqueeze(2).broadcast_to([P, NT * TOPK, TOPK]),
                                      iota16[:, :].unsqueeze(1).broadcast_to([P, NT * TOPK, TOPK]), ALU.is_equal)
                step(last)
                emit_pick(dve, step, cand, cand2, sif, IS, JS, h)
                assert chain.local == per, chain.local
                chain.leave(HEADS)


def emit_pick(dve, step, cand, cand2, sif, IS, JS, h):
    step(dve.tensor_tensor(cand[:, :, :, :], cand[:, :, :, :],
                           sif[:, 0:4, :].unsqueeze(2).broadcast_to([P, NT, TOPK, TOPK]), ALU.mult))
    step(dve.tensor_tensor(cand2[:, :, :, :], cand2[:, :, :, :],
                           sif[:, 4:8, :].unsqueeze(2).broadcast_to([P, NT, TOPK, TOPK]), ALU.mult))
    for work, dst in ((cand, IS), (cand2, JS)):
        last = dve.tensor_reduce(dst[:, :, bass.ds(h, 1), :].rearrange("p t o k -> p t (o k)"),
                                 work[:, :, :, :], AX.X, ALU.add)
    step(last)


def emit_gates(nc, banks, sem, v):
    ident, FV, IS, JS, gates = (v[n] for n in ("ident", "FV", "IS", "JS", "gates"))
    ctx = ExitStack()
    with ctx:
        def sb(name, shape, dt=F32):
            return ctx.enter_context(nc.sbuf_tensor(name, shape, dt))

        tot = sb("tot", [P, NT, HEADS])
        turned = [sb(f"turned{j}", [P, T]) for j in range(3)]
        iota = sb("iota", [P, P])
        OI = [sb(f"OI{k}", [P, P]) for k in range(8)]
        OJ = [sb(f"OJ{k}", [P, P]) for k in range(8)]
        stage = [sb(f"stage{b}", [P, NKEYS, TB]) for b in range(2)]
        iota_up, less_up, exp_up, gate_up, t_up, t_out = (
            sem(n) for n in ("iota_up", "less_up", "exp_up5", "gate_up5", "t_up5", "t_out5"))
        hot, spread, staged, p_dve = sem("hot"), sem("spread"), sem("staged"), sem("p_dve5")
        sent = [sem(f"sent{b}") for b in range(2)]
        block = ctx.enter_context(nc.Block())
        BL = T // TB
        PB = TB // 4

        @block.gpsimd
        def _(pool):
            pool.iota(iota[:, :], pattern=[[1, P]], base=0, channel_multiplier=0,
                      allow_small_or_imprecise_dtypes=True).then_inc(iota_up, 1)

        @block.sync
        def _(sp):
            with sp.Fori(0, BL // 2) as i:
                for b in range(2):
                    sp.wait_ge(staged, 2 * PB * i + PB * (b + 1))
                    sp.dma_start(gates[:, bass.ds(2 * i + b, 1), :, :].rearrange("p o j t -> p (o j t)"),
                                 stage[b][:, :, :].rearrange("p j t -> p (j t)")).then_inc(sent[b], 16)
            for b in range(2):
                sp.wait_ge(sent[b], 16 * (BL // 2))

        @block.scalar
        def _(act):
            act.wait_ge(less_up, 1)
            act.activation(FV[:, :, :, :], FV[:, :, :, :], ACT.Exp).then_inc(exp_up, 1)
            for j in range(3):
                act.wait_ge(t_up, j + 1)
                act.activation(turned[j][:, :], banks[j][:, :], ACT.Copy).then_inc(t_out, 1)
            with act.Fori(0, BL // 2) as i:
                for b in range(2):
                    act.wait_ge(sent[b], 16 * i)
                    with act.Fori(0, PB // 2) as g:
                        for q in range(2):
                            act.wait_ge(spread, (2 * i + b) * PB + 2 * g + (q + 1))
                            act.activation(stage[b][:, :, bass.ds(8 * g + 4 * q, 4)],
                                           banks[4 + q][:, :].rearrange("p (t j) -> p j t", t=4), ACT.Copy)\
                                .then_inc(staged, 1)

        @block.tensor
        def _(pe):
            for j, src in enumerate((IS, JS, FV)):
                if j == 2:
                    pe.wait_ge(gate_up, 1)
                for t in range(NT):
                    last = pe.transpose(banks[j][:, t * P:(t + 1) * P],
                                        src[:, t, :, :].rearrange("p h k -> p (h k)"), ident[:, :])
                last.then_inc(t_up, 1)
            with pe.Fori(0, T // 8) as g:
                for q in range(2):
                    pe.wait_ge(hot, 2 * g + (q + 1))
                    pe.wait_ge(staged, 2 * g + (q - 1) if q else 2 * g)
                    for k in range(4):
                        last = pe.matmul(banks[4 + q][:, k * P:(k + 1) * P], OI[4 * q + k][:, :],
                                         OJ[4 * q + k][:, :], start=True, stop=True)
                    last.then_inc(spread, 1)

        @block.vector
        def _(dve):
            step = stepper(dve, Tally(p_dve))
            top = FV[:, :, :, :].rearrange("p t h k -> p (t h) k")
            heads = NT * HEADS
            step(dve.tensor_copy(tot[:, :, :], FV[:, :, :, 0]))
            flat = tot[:, :, :].rearrange("p t h -> p (t h)")
            dve.tensor_tensor(top, top, flat.unsqueeze(2).broadcast_to([P, heads, TOPK]), ALU.subtract)\
                .then_inc(less_up, 1)
            dve.wait_ge(exp_up, 1)
            step(dve.tensor_reduce(flat, top, AX.X, ALU.add))
            step(dve.reciprocal(flat, flat))
            dve.tensor_tensor(top, top, flat.unsqueeze(2).broadcast_to([P, heads, TOPK]), ALU.mult)\
                .then_inc(gate_up, 1)
            dve.wait_ge(iota_up, 1)
            dve.wait_ge(t_out, 3)
            with dve.Fori(0, T // 8) as g:
                for q in range(2):
                    dve.wait_ge(spread, 2 * g)
                    for k in range(4):
                        at = bass.ds(8 * g + 4 * q + k, 1)
                        dve.tensor_scalar(OI[4 * q + k][:, :], iota[:, :], turned[0][:, at], None, ALU.is_equal)
                        last = dve.tensor_scalar(OJ[4 * q + k][:, :], iota[:, :], turned[1][:, at],
                                                 turned[2][:, at], ALU.is_equal, ALU.mult)
                    last.then_inc(hot, 1)


def emit_experts(nc, bank, banks, sem, v):
    peer_u, peer_v, ln2_g, ln2_b, ident, hh, hl, ring, gates, x1, gt2, out = (
        v[n] for n in ("peer_u", "peer_v", "ln2_g", "ln2_b", "ident", "hh", "hl", "ring", "gates", "x1", "gt2", "out"))
    acc = v["acc"]
    ctx = ExitStack()
    with ctx:
        def sb(name, shape, dt=F32):
            return ctx.enter_context(nc.sbuf_tensor(name, shape, dt))

        scores = ExpertScores(nc, sb, sem, "e_", banks, ident, hh, hl, ring, peer_u)
        vraw = [sb(f"vraw{s}", [P, D]) for s in range(4)]
        vh = [sb(f"vh{q}", [P, 2, D], F32R) for q in range(2)]
        vl = [sb(f"vl{q}", [P, 2, D], F32R) for q in range(2)]
        gt = [sb(f"gtile{q}", [P, T // TB, 2, TB]) for q in range(2)]
        w = [sb(f"w{b}", [P, 2, P]) for b in range(2)]
        wh = [sb(f"wh{t}", [P, 2, P], F32R) for t in range(NT)]
        wl = [sb(f"wl{t}", [P, 2, P], F32R) for t in range(NT)]
        v_in = [sem(f"v_in{s}") for s in range(4)]
        g_in = [sem(f"g_in{q}") for q in range(2)]
        vh_up, vl_up, w_up, wh_up, wl_up, y_up, y_added, zeroed = (
            sem(n) for n in ("vh_up", "vl_up", "w_up", "wh_up", "wl_up", "y_up6", "y_added", "zeroed"))
        IT = NKEYS // 4
        MAIN = IT - AHEAD
        vsrc = peer_v[0].rearrange("(i j) d -> i j d", j=NKEYS)

        lg, lb = (ring[:, 2 * j:2 * j + 2, :].rearrange("p a b -> p (a b)") for j in range(2))
        norm = Norm(nc, sb, "n2_")
        ln_in, var_up, root_up, centred, gained, x2_up, p_dve, p_y = (
            sem(n) for n in ("ln_in6", "var_up6", "root_up6", "centred6", "gained6", "x2_up", "p_dve6", "p_y"))
        out_sent = sem("out_sent")

        block = ctx.enter_context(nc.Block())

        def load_v(sp, s, turn):
            sp.dma_start(vraw[s][:, :], vsrc[:, bass.ds(4 * turn + s, 1), :].rearrange("i o d -> i (o d)"))\
                .then_inc(v_in[s], 16)

        def load_g(sp, q, turn):
            sp.dma_start(gt[q][:, :, :, :], gates[:, :, bass.ds(4 * turn + 2 * q, 2), :]).then_inc(g_in[q], 16)

        @block.sync
        def _(sp):
            for s in range(4):
                scores.load(sp, 0, s, 4 * AHEAD + s)
            for s in range(4):
                sp.dma_start(vraw[s][:, :], vsrc[:, s, :]).then_inc(v_in[s], 16)
            for q in range(2):
                sp.dma_start(gt[q][:, :, :, :], gates[:, :, 2 * q:2 * q + 2, :]).then_inc(g_in[q], 16)

            def loads(i, with_u):
                def u(s):
                    if with_u:
                        sp.wait_ge(scores.turned, 8 * i + 2 * s + 2)
                        scores.load(sp, i, s, bass.ds(4 * ((i + AHEAD + 1) % IT) + s, 1))
                for s in (0, 1):
                    sp.wait_ge(vl_up, 4 * i + (s + 1))
                    sp.wait_ge(vh_up, 4 * i + (s + 1))
                    load_v(sp, s, (i + 1) % IT)
                sp.wait_ge(wl_up, 8 * i + 4)
                sp.wait_ge(w_up, 8 * i + 4)
                load_g(sp, 0, (i + 1) % IT)
                u(0)
                for s in (2, 3):
                    sp.wait_ge(vl_up, 4 * i + (s + 1))
                    sp.wait_ge(vh_up, 4 * i + (s + 1))
                    load_v(sp, s, (i + 1) % IT)
                u(1)
                sp.wait_ge(w_up, 8 * i + 8)
                load_g(sp, 1, (i + 1) % IT)
                u(2)
                u(3)
            with sp.Fori(0, MAIN) as i:
                loads(i, True)
            with sp.Fori(MAIN, IT) as i:
                loads(i, False)
            sp.wait_ge(w_up, 8 * IT + 4)
            for dst, src in ((lg, ln2_g), (lb, ln2_b)):
                sp.dma_start(dst, src.rearrange("o n -> (o n)").partition_broadcast(P)).then_inc(ln_in, 16)
            for t in range(NT):
                sp.wait_ge(x2_up, t + 1)
                sp.dma_start(out[0, t * P:(t + 1) * P, :], acc[:, t, :]).then_inc(out_sent, 16)
            sp.wait_ge(out_sent, 16 * NT)
            for s in range(4):
                sp.wait_ge(v_in[s], 16 * (IT + 1))
                sp.wait_ge(scores.u_in[s], 16 * (MAIN + 1))
            for q in range(2):
                sp.wait_ge(g_in[q], 16 * (IT + 1))

        def v_ready(eng, i, q, ahead):
            for s in (2 * q, 2 * q + 1):
                eng.wait_ge(v_in[s], 16 * i + (32 if ahead else 16))

        @block.gpsimd
        def _(pool):
            pool.memset(acc[:, :, :], 0.0).then_inc(zeroed, 1)

            def rest(i, q, n, done):
                v_ready(pool, i, q, ahead=(done is not None and q == 0))
                if done is not None:
                    pool.wait_ge(y_up, done)
                for k in range(2):
                    pool.wait_ge(vh_up, 2 * n + (k + 1))
                    pool.tensor_tensor(vl[q][:, k, :], vraw[2 * q + k][:, :], vh[q][:, k, :].bitcast(F32),
                                       ALU.subtract).then_inc(vl_up, 1)
            rest(0, 0, 0, None)

            def turn(i, with_u):
                if with_u:
                    scores.remainder(pool, i, 0)
                rest(i, 1, 2 * i + 1, 8 * i)
                if with_u:
                    scores.remainder(pool, i, 1)
                    scores.remainder(pool, i, 2)
                rest(i, 0, 2 * i + 2, 8 * i + 4)
                if with_u:
                    scores.remainder(pool, i, 3)
            with pool.Fori(0, MAIN) as i:
                turn(i, True)
            with pool.Fori(MAIN, IT) as i:
                turn(i, False)
            for t in range(NT):
                if t == 0:
                    pool.wait_ge(ln_in, 32)
                pool.wait_ge(centred, t + 1)
                pool.tensor_tensor(acc[:, t, :], acc[:, t, :], lg[:, :], ALU.mult).then_inc(gained, 1)

        @block.scalar
        def _(act):
            def rounded(i, q, done):
                v_ready(act, i, q, ahead=(done is not None and q == 0))
                if done is not None:
                    act.wait_ge(y_up, done)
                for k in range(2):
                    act.activation(vh[q][:, k, :], vraw[2 * q + k][:, :], ACT.Copy).then_inc(vh_up, 1)
            rounded(0, 0, None)

            def turn(i, with_u):
                def gelu(s):
                    if with_u:
                        act.wait_ge(w_up, 8 * i + (0, 0, 4, 4)[s] + 4)
                        scores.gelu(act, i, s, bass.ds(4 * (i % AHEAD) + s, 1))
                if with_u:
                    scores.evacuate(act, i, 0)
                rounded(i, 1, 8 * i)
                if with_u:
                    scores.evacuate(act, i, 1)
                    gelu(0)
                    scores.evacuate(act, i, 2)
                    gelu(1)
                rounded(i, 0, 8 * i + 4)
                if with_u:
                    scores.evacuate(act, i, 3)
                    gelu(2)
                    gelu(3)
            with act.Fori(0, MAIN) as i:
                turn(i, True)
            with act.Fori(MAIN, IT) as i:
                turn(i, False)
            for t in range(NT):
                act.wait_ge(var_up, t + 1)
                norm.root(act, t).then_inc(root_up, 1)

        @block.tensor
        def _(pe):
            def unit(i, q, t):
                u = 4 * q + t
                pe.wait_ge(wl_up, 8 * i + (u + 1))
                pe.wait_ge(wh_up, 8 * i + (u + 1))
                if t == 0:
                    pe.wait_ge(vl_up, 4 * i + (2 * q + 2))
                pe.wait_ge(y_added, 8 * i + max(u - 1, 0))
                for h in range(2):
                    b = banks[4 + 2 * (u % 2) + h]
                    half = slice(512 * h, 512 * h + 512)
                    for k in range(2):
                        pe.matmul(b[:, :], wh[t][:, k, :], vh[q][:, k, half], start=(k == 0), stop=False)
                        pe.matmul(b[:, :], wh[t][:, k, :], vl[q][:, k, half], start=False, stop=False)
                        last = pe.matmul(b[:, :], wl[t][:, k, :], vh[q][:, k, half], start=False, stop=(k == 1))
                last.then_inc(y_up, 1)

            def turn(i, with_u):
                for s in range(4):
                    if with_u:
                        scores.turn(pe, i, s)
                    unit(i, s // 2, 2 * (s % 2))
                    unit(i, s // 2, 2 * (s % 2) + 1)
                    if with_u:
                        scores.product(pe, i, s)
            with pe.Fori(0, MAIN) as i:
                turn(i, True)
            with pe.Fori(MAIN, IT) as i:
                turn(i, False)

        @block.vector
        def _(dve):
            def gated(n, i, q, t, slot, turn_of_gates):
                if t == 0:
                    dve.wait_ge(g_in[q], 16 * turn_of_gates + 16)
                dve.tensor_tensor(w[t % 2][:, :, :].rearrange("p j (b t) -> p j b t", b=2),
                                  ring[:, slot, t * P:(t + 1) * P].rearrange("p j (b t) -> p j b t", b=2),
                                  gt[q][:, 2 * t:2 * t + 2, :, :].rearrange("p b j t -> p j b t"), ALU.mult)\
                    .then_inc(w_up, 1)
                dve.wait_ge(w_up, n + (t + 1))
                dve.tensor_copy(wh[t][:, :, :], w[t % 2][:, :, :]).then_inc(wh_up, 1)
                dve.wait_ge(wh_up, n + (t + 1))
                dve.tensor_tensor(wl[t][:, :, :], w[t % 2][:, :, :], wh[t][:, :, :].bitcast(F32), ALU.subtract)\
                    .then_inc(wl_up, 1)

            dve.wait_ge(zeroed, 1)
            for t in range(NT):
                gated(0, 0, 0, t, slice(0, 2), 0)

            def turn(i):
                for q in range(2):
                    for t in range(NT):
                        u = 4 * q + t
                        dve.wait_ge(y_up, 8 * i + (u + 1))
                        b = bank[:, 512 * (4 + 2 * (u % 2)):512 * (6 + 2 * (u % 2))]
                        dve.wait_ge(y_added, 8 * i + max(u - 3, 0))
                        dve.tensor_tensor(acc[:, t, :], acc[:, t, :], b, ALU.add).then_inc(y_added, 1)
                        if q == 0:
                            gated(8 * i + 4, i, 1, t, bass.ds(4 * (i % AHEAD) + 2, 2), i)
                        else:
                            gated(8 * i + 8, i, 0, t, bass.ds(4 * ((i + 1) % AHEAD), 2), i + 1)
            with dve.Fori(0, MAIN) as i:
                turn(i)
            with dve.Fori(MAIN, IT) as i:
                turn(i)
            step = stepper(dve, Tally(p_dve))
            dve.wait_ge(y_added, 8 * IT)
            for t in range(NT):
                step(dve.tensor_tensor(acc[:, t, :], acc[:, t, :], gt2[:, :], ALU.mult))
                step(dve.scalar_tensor_tensor(out=acc[:, t, :], in0=x1[:, t, :], scalar=ALPHA, in1=acc[:, t, :],
                                              op0=ALU.mult, op1=ALU.add))
                norm.moments(dve, step, t, acc[:, t, :]).then_inc(var_up, 1)
                dve.wait_ge(root_up, t + 1)
                norm.scaled(dve, step, t, acc[:, t, :]).then_inc(centred, 1)
                dve.wait_ge(gained, t + 1)
                dve.tensor_tensor(acc[:, t, :], acc[:, t, :], lb[:, :], ALU.add).then_inc(x2_up, 1)


_INS = ["x", "c", "ada_w", "ada_b", "w_in", "attn_sink", "shift_mu", "decay_w0", "decay_w2", "iclr_a0", "iclr_a2",
        "gate_g2", "k_k", "k_a", "r_k", "lnx_g", "lnx_b", "w_out", "ln1_g", "ln1_b", "peer_wq", "peer_subkeys",
        "peer_u", "peer_v", "ln2_g", "ln2_b"]


def kernel(**inputs):
    import numpy as np
    import concourse.bacc as bacc
    from concourse.bass_utils import run_bass_kernel_spmd

    nc = bacc.Bacc("TRN2", target_bir_lowering=False, num_devices=1)
    arrays, args = {}, []
    for name in _INS:
        a = np.ascontiguousarray(inputs[name])
        arrays["in_" + name] = a
        args.append(nc.dram_tensor("in_" + name, a.shape, mybir.dt.from_np(a.dtype), kind="ExternalInput").ap())
    args.append(nc.dram_tensor("out_x", (1, T, D), F32, kind="ExternalOutput").ap())
    hybrid_layer(nc, *args)
    r = run_bass_kernel_spmd(nc, [arrays], core_ids=[0])
    return r.results[0]["out_x"]
```

```python
import concourse.bass as bass
from concourse import mybir
from contextlib import ExitStack
import math

D = 1024
T = 512
P = 128
KD = D // P
NT = T // P
HD = 64
HEADS = 8
PAIRS = HEADS // 2
ATTN_COLS = 768
RW_TILES = 14
CH = 64
NKEYS = 128
TOPK = 16
AHEAD = 6
START = 8
LN_EPS = 1e-5
GN_EPS = 64e-5
ALPHA = 2.0 ** 0.25
KAPPA = math.exp(-0.5)
NEG = -1.0e30

F32 = mybir.dt.float32
F32R = mybir.dt.float32r
U32 = mybir.dt.uint32
ALU = mybir.AluOpType
ACT = mybir.ActivationFunctionType
AX = mybir.AxisListType

R_C, R_ADAB, R_MU, R_W0, R_A0, R_KK, R_KA, R_RK, R_LXG, R_LXB = 0, 8, 56, 70, 74, 78, 82, 86, 90, 94
N_ROWS = 98


class Tally:

    def __init__(self, sem):
        self.sem, self.base, self.local, self.loop = sem, START, 0, None

    def value(self):
        turns = 0 if self.loop is None else self.loop[0] * self.loop[1]
        return turns + (self.base + self.local)

    def inc(self, ins):
        ins.then_inc(self.sem, 1)
        self.local += 1
        return ins

    def enter(self, i, per):
        self.base, self.local, self.loop = self.base + self.local, 0, (i, per)

    def leave(self, turns):
        assert self.local == self.loop[1], (self.local, self.loop[1])
        self.base, self.local, self.loop = self.base + turns * self.local, 0, None


def stepper(eng, tally):
    def step(ins):
        tally.inc(ins)
        eng.wait_ge(tally.sem, tally.value())
    return step


def hybrid_layer(nc, x, c, ada_w, ada_b, w_in, attn_sink, shift_mu, decay_w0, decay_w2, iclr_a0, iclr_a2,
                 gate_g2, k_k, k_a, r_k, lnx_g, lnx_b, w_out, ln1_g, ln1_b, peer_wq, peer_subkeys,
                 peer_u, peer_v, ln2_g, ln2_b, out):
    ctx = ExitStack()
    with ctx:
        held, phase = [], [1]
        starters = (nc.sync, nc.scalar, nc.vector, nc.gpsimd, nc.tensor)

        def sem(name):
            held.append(nc.alloc_semaphore(f"{name}_{phase[0]}"))
            starters[len(held) % len(starters)].sem_inc(held[-1], START)
            return held[-1]

        def fresh():
            nc.clear_and_free_semaphores(held)
            nc.all_engine_barrier()
            held.clear()
            phase[0] += 1

        def keep(name, shape, dt=F32):
            return ctx.enter_context(nc.sbuf_tensor(name, shape, dt))

        bank = ctx.enter_context(nc.psum_tensor("bank", [P, 8 * 512], F32))
        banks = [bank[:, 512 * i:512 * i + 512] for i in range(8)]

        ident = keep("ident", [P, P])
        par = keep("par", [P, N_ROWS])
        mod = keep("mod", [P, 32])
        gt2 = keep("gt2", [P, D])
        wide = keep("wide", [P, KD, T])

        gt1 = keep("gt1", [P, D])

        x1_kept = nc.dram_tensor("x1_kept", [NT, P, D], F32, kind="Internal").ap()
        gates = nc.dram_tensor("gates", [P, T // TB, NKEYS, TB], F32, kind="Internal").ap()
        mix = ExitStack()
        mix.__enter__()

        def mk(name, shape, dt=F32):
            return mix.enter_context(nc.sbuf_tensor(name, shape, dt))

        diag2 = mk("diag2", [P, P])
        qT = mk("qT", [P, 4, T])
        kT = mk("kT", [P, 2, P + T])
        vtok = mk("vtok", [P, 1 + NT, P])
        PM = mk("PM", [P, RW_TILES, T])
        yT = wide
        SW = yT[:, 0:4, :]
        CS = yT[:, 4:8, :]
        AI = mk("AI", [P, PAIRS, T])
        GG = mk("GG", [P, PAIRS, T])
        KN = mk("KN", [P, PAIRS, T])
        BO = mk("BO", [P, PAIRS, T])
        PL = mk("PL", [P, PAIRS, T // CH])

        emit_projections(nc, banks, sem, locals())
        fresh()
        emit_mixing(nc, banks, sem, locals())
        fresh()
        mix.close()

        hh = keep("hh", [P, KD, T], F32R)
        hl = keep("hl", [P, KD, T], F32R)
        ring = keep("ring", [P, 4 * AHEAD, T])
        h2 = wide
        emit_mix_out(nc, banks, sem, locals())
        fresh()
        emit_routing(nc, banks, sem, locals())
        fresh()
        acc = wide[:, :, :].rearrange("p (t h) d -> p t (h d)", t=NT)
        emit_experts(nc, bank, banks, sem, locals())


def emit_projections(nc, banks, sem, v):
    (x, c, ada_w, ada_b, w_in, shift_mu, decay_w0, decay_w2, iclr_a0, iclr_a2, gate_g2, k_k, k_a, r_k, lnx_g,
     lnx_b) = (v[n] for n in ("x", "c", "ada_w", "ada_b", "w_in", "shift_mu", "decay_w0", "decay_w2", "iclr_a0",
                              "iclr_a2", "gate_g2", "k_k", "k_a", "r_k", "lnx_g", "lnx_b"))
    (ident, par, mod, gt1, gt2, diag2, qT, kT, vtok, PM, SW, CS, AI, GG, KN, BO, PL) = (
        v[n] for n in ("ident", "par", "mod", "gt1", "gt2", "diag2", "qT", "kT", "vtok", "PM", "SW", "CS", "AI",
                       "GG", "KN", "BO", "PL"))
    ctx = ExitStack()
    with ctx:
        def sb(name, shape, dt=F32):
            return ctx.enter_context(nc.sbuf_tensor(name, shape, dt))

        rows = sb("rows", [P, P])
        csT = sb("csT", [P, KD])
        csw = sb("csw", [P, KD, P])
        omu = sb("omu", [P, RW_TILES])
        xin = [sb(f"xin{i}", [P, D]) for i in range(2)]
        hT = sb("hT", [P, KD, T])
        ada = [sb(f"ada{i}", [P, KD, 512]) for i in range(2)]
        wt = [sb(f"wt{i}", [P, KD, P]) for i in range(2)]
        w2a2 = sb("w2a2", [P, 512])
        g2 = sb("g2", [P, 512])
        PD = sb("PD", [P, PAIRS, T])
        keepm = sb("keepm", [P, T])
        tmp = [sb(f"tmp{i}", [P, T]) for i in range(4)]

        rows_in, lora_in = sem("rows_in"), sem("lora_in")
        x_in = [sem(f"x_in{i}") for i in range(2)]
        ada_in = [sem(f"ada_in{i}") for i in range(2)]
        wt_in = [sem(f"wt_in{i}") for i in range(2)]
        gb_in = sem("gb_in")
        consts, rows_up, par_up, silu_up = sem("consts"), sem("rows_up"), sem("par_up"), sem("silu_up")
        cs_up = sem("cs_up")
        xt_up, xt_used = sem("xt_up"), sem("xt_used")
        cols_up, cols_used = sem("cols_up"), sem("cols_used")
        ada_used, h_up = sem("ada_used"), sem("h_up")
        proj_up, proj_scaled, proj_mixed = sem("proj_up"), sem("proj_scaled"), sem("proj_mixed")
        lora_act, z_up, z_used = sem("lora_act"), sem("z_up"), sem("z_used")
        p_dve, p_act, p_pool = sem("p_dve"), sem("p_act"), sem("p_pool")
        gate_up, gate_used = sem("gate_up"), sem("gate_used")
        sq_up, ss_up, ss_max, ss_root = sem("sq_up"), sem("ss_up"), sem("ss_max"), sem("ss_root")
        kp_up, rk_up, rks_up, bsum_up, bo_up = sem("kp_up"), sem("rk_up"), sem("rks_up"), sem("bsum_up"), sem("bo_up")
        cs_scan, csm_up, exp_up, nk_up = sem("cs_scan"), sem("csm_up"), sem("exp_up"), sem("nk_up")

        wv = w_in.rearrange("o (k p) n -> p (o k) n", p=P)
        av = ada_w.rearrange("o (k p) n -> p (o k) n", p=P)
        xv = x.rearrange("o (t p) d -> p (o t) d", p=P)

        def ada_piece(m, half):
            return av[:, :, m * D + half * 512:m * D + half * 512 + 512]

        pieces = [(m, half) for m in (0, 1, 2, 3, 4, 5) for half in (0, 1)]

        nc.all_engine_barrier()
        block = ctx.enter_context(nc.Block())

        @block.sync
        def _(sp):
            for name, src, n in (("c", c, 8), ("ada_b", ada_b, 48), ("mu", shift_mu, 14), ("w0", decay_w0, 4),
                                 ("a0", iclr_a0, 4), ("kk", k_k, 4), ("ka", k_a, 4), ("rk", r_k, 4),
                                 ("lxg", lnx_g, 4), ("lxb", lnx_b, 4)):
                at = {"c": R_C, "ada_b": R_ADAB, "mu": R_MU, "w0": R_W0, "a0": R_A0, "kk": R_KK, "ka": R_KA,
                      "rk": R_RK, "lxg": R_LXG, "lxb": R_LXB}[name]
                flat = src.rearrange("o h d -> (o h d)") if name == "rk" else src.rearrange("o n -> (o n)")
                sp.dma_start(rows[at:at + n, :], flat.rearrange("(n p) -> n p", p=P)).then_inc(rows_in, 16)
            for t in range(NT):
                if t >= 2:
                    sp.wait_ge(xt_up, START + 2 * (t - 1))
                sp.dma_start(xin[t % 2][:, :], xv[:, t, :]).then_inc(x_in[t % 2], 16)
            for n in range(4):
                if n >= 2:
                    sp.wait_ge(ada_used, START + n - 1)
                sp.dma_start(ada[n % 2][:, :, :], ada_piece(*pieces[n])).then_inc(ada_in[n % 2], 16)
            sp.dma_start(w2a2[0:64, :], decay_w2[0, :, :]).then_inc(lora_in, 16)
            sp.dma_start(w2a2[64:128, :], iclr_a2[0, :, :]).then_inc(lora_in, 16)
            sp.dma_start(g2[:, :], gate_g2[0, :, :]).then_inc(lora_in, 16)
            for n in range(2):
                sp.dma_start(wt[n][:, :, :], wv[:, :, ATTN_COLS + (12 + n) * P:ATTN_COLS + (13 + n) * P])\
                    .then_inc(wt_in[n], 16)
            with sp.Fori(0, 6) as i:
                for n in range(2):
                    sp.wait_ge(proj_up, START + 2 * i + (n + 1))
                    sp.dma_start(wt[n][:, :, :], wv[:, :, bass.ds((i * 2 + n) * P + ATTN_COLS, P)])\
                        .then_inc(wt_in[n], 16)
            with sp.Fori(0, 2) as i:
                for n in range(2):
                    sp.wait_ge(proj_up, START + 2 * i + (13 + n))
                    sp.dma_start(wt[n][:, :, :], wv[:, :, bass.ds((i * 2 + n) * P, P)]).then_inc(wt_in[n], 16)
            for n in range(2):
                sp.wait_ge(proj_up, START + 17 + n)
                for d in range(2):
                    sp.dma_start(wt[n][:, :, 64 * d:64 * d + 64], wv[:, :, 512 + 64 * n:576 + 64 * n])\
                        .then_inc(wt_in[n], 16)
            sp.wait_ge(proj_up, START + 19)
            sp.dma_start(wt[0][:, :, :], wv[:, :, 640:768]).then_inc(wt_in[0], 16)
            for n in range(4, 12):
                sp.wait_ge(ada_used, START + n - 1)
                sp.dma_start(ada[n % 2][:, :, :], ada_piece(*pieces[n])).then_inc(ada_in[n % 2], 16)
            flat = ada_b.rearrange("o n -> (o n)")
            for dst, m in ((gt1, 2), (gt2, 5)):
                sp.dma_start(dst[:, :], flat[m * D:(m + 1) * D].partition_broadcast(P)).then_inc(gb_in, 16)
            sp.wait_ge(gb_in, START + 32)

        @block.gpsimd
        def _(pool):
            step = stepper(pool, Tally(p_pool))
            step(pool.memset(ident[:, :], 0.0))
            pool.affine_select(out=ident[:, :], in_=ident[:, :], compare_op=ALU.not_equal, fill=1.0, base=0,
                               pattern=[[-1, P]], channel_multiplier=1).then_inc(consts, 1)
            step(pool.memset(diag2[:, :], 1.0))
            d2 = diag2[:, :].rearrange("p (b w) -> p b w", b=2)
            step(pool.affine_select(out=d2, in_=d2, compare_op=ALU.is_ge, fill=0.0, base=0,
                                    pattern=[[-CH, 2], [0, CH]], channel_multiplier=1))
            pool.affine_select(out=d2, in_=d2, compare_op=ALU.is_ge, fill=0.0, base=CH - 1,
                               pattern=[[CH, 2], [0, CH]], channel_multiplier=-1).then_inc(consts, 1)
            step(pool.memset(keepm[:, :], 1.0))
            pool.memset(keepm[:, ::CH], 0.0).then_inc(consts, 1)
            pool.memset(kT[:, :, 0:P], 0.0).then_inc(consts, 1)
            pool.memset(vtok[:, 0, :], 0.0).then_inc(consts, 1)

            for p in range(PAIRS):
                pool.wait_ge(kp_up, START + p + 1)
                if p >= 2:
                    pool.wait_ge(ss_up, START + p - 1)
                pool.tensor_tensor(tmp[p % 2][:, :], KN[:, p, :], KN[:, p, :], ALU.mult).then_inc(sq_up, 1)
            for p in range(PAIRS):
                pool.wait_ge(cs_scan, START + p + 1)
                pool.tensor_tensor(SW[:, p, :], CS[:, p, :], SW[:, p, :], ALU.subtract).then_inc(csm_up, 1)
            for p in range(PAIRS):
                pool.wait_ge(kp_up, START + PAIRS + p + 1)
                if p >= 2:
                    pool.wait_ge(bsum_up, START + p - 1)
                pool.tensor_tensor(tmp[2 + p % 2][:, :], PM[:, p, :], PM[:, 4 + p, :], ALU.mult).then_inc(rk_up, 1)
            for p in range(PAIRS):
                pool.wait_ge(exp_up, START + 3 * PAIRS)
                pool.wait_ge(nk_up, START + 2 * p + 2)
                pool.tensor_tensor(AI[:, p, :], AI[:, p, :], CS[:, p, :], ALU.mult).then_inc(p_pool, 1)
            for p in range(PAIRS):
                pool.wait_ge(rk_up, START + p + 1)
                pool.tensor_tensor(PM[:, 4 + p, :], PM[:, 4 + p, :], CS[:, p, :], ALU.mult).then_inc(p_pool, 1)

        @block.scalar
        def _(act):
            act.wait_ge(rows_up, START + 1)
            act.activation(par[:, :], banks[7][:, 0:N_ROWS], ACT.Copy).then_inc(par_up, 1)
            act.wait_ge(par_up, START + 1)
            act.activation(csT[:, :], par[:, R_C:R_C + KD], ACT.Sigmoid).then_inc(silu_up, 1)
            for t in range(NT):
                for h in range(2):
                    act.wait_ge(xt_up, START + 2 * t + h + 1)
                    act.activation(hT[:, 4 * h:4 * h + 4, t * P:(t + 1) * P],
                                   banks[2 + (2 * t + h) % 4][:, :].rearrange("p (k t) -> p k t", k=4), ACT.Copy)\
                        .then_inc(xt_used, 1)
            act.wait_ge(silu_up, START + 3)
            for n in range(2):
                act.wait_ge(proj_up, START + n + 1)
                act.activation(PM[:, 12 + n, :], banks[n][:, :], ACT.Copy, scale=omu[:, 12 + n:13 + n])\
                    .then_inc(proj_scaled, 1)
            act.wait_ge(proj_mixed, START + 2)
            act.activation(PM[0:64, 12, :], PM[0:64, 12, :], ACT.Tanh).then_inc(lora_act, 1)
            act.activation(PM[:, 13, :], PM[:, 13, :], ACT.Sigmoid).then_inc(lora_act, 1)
            for p in range(PAIRS):
                for j, (dst, row) in enumerate(((SW, R_W0), (AI, R_A0), (GG, None))):
                    n = 3 * p + j
                    act.wait_ge(z_up, START + n + 1)
                    src = banks[2 + n % 2][:, :]
                    if row is None:
                        act.activation(dst[:, p, :], src, ACT.Copy).then_inc(z_used, 1)
                    else:
                        act.activation(dst[:, p, :], src, ACT.Sigmoid, bias=par[:, row + p:row + p + 1])\
                            .then_inc(z_used, 1)
            with act.Fori(0, 6) as i:
                for n in range(2):
                    act.wait_ge(proj_up, START + 2 * i + (3 + n))
                    act.activation(PM[:, bass.ds(2 * i + n, 1), :].rearrange("p o t -> p (o t)"), banks[n][:, :],
                                   ACT.Copy, scale=omu[:, bass.ds(2 * i + n, 1)]).then_inc(proj_scaled, 1)
            with act.Fori(0, 2) as i:
                for n in range(2):
                    act.wait_ge(proj_up, START + 2 * i + (15 + n))
                    act.activation(qT[:, bass.ds(2 * i + n, 1), :].rearrange("p o t -> p (o t)"), banks[n][:, :],
                                   ACT.Copy, scale=HD ** -0.5).then_inc(proj_scaled, 1)
            for n in range(2):
                act.wait_ge(proj_up, START + 19 + n)
                act.activation(kT[:, n, P:], banks[n][:, :], ACT.Copy).then_inc(proj_scaled, 1)
            act.wait_ge(proj_up, START + 21)
            act.activation(vtok[:, 1:, :], banks[0][:, :].rearrange("p (t n) -> p t n", t=NT), ACT.Copy)\
                .then_inc(proj_scaled, 1)
            for p in range(PAIRS):
                act.wait_ge(ss_max, START + p + 1)
                act.activation(PD[:, p, :], PD[:, p, :], ACT.Sqrt).then_inc(ss_root, 1)
            act.wait_ge(cs_scan, START + PAIRS)
            act.wait_ge(csm_up, START + PAIRS)
            act.activation(SW[:, :, :], SW[:, :, :], ACT.Exp, scale=-KAPPA).then_inc(exp_up, PAIRS)
            act.wait_ge(nk_up, START + 2 * PAIRS)
            act.activation(PD[:, :, :], CS[:, :, :], ACT.Exp, scale=-KAPPA).then_inc(exp_up, PAIRS)
            act.wait_ge(exp_up, START + 2 * PAIRS)
            act.activation(CS[:, :, :], CS[:, :, :], ACT.Exp, scale=KAPPA).then_inc(exp_up, PAIRS)

        @block.tensor
        def _(pe):
            pe.wait_ge(rows_in, START + 160)
            pe.wait_ge(consts, START + 1)
            pe.transpose(banks[7][:, 0:N_ROWS], rows[0:N_ROWS, :], ident[0:N_ROWS, 0:N_ROWS]).then_inc(rows_up, 1)
            for t in range(NT):
                pe.wait_ge(x_in[t % 2], START + 16 * (t // 2 + 1))
                for h in range(2):
                    n = 2 * t + h
                    if n >= 4:
                        pe.wait_ge(xt_used, START + n - 3)
                    for k in range(4):
                        last = pe.transpose(banks[2 + n % 4][:, k * P:(k + 1) * P],
                                            xin[t % 2][:, (4 * h + k) * P:(4 * h + k + 1) * P], ident[:, :])
                    last.then_inc(xt_up, 1)
            pe.wait_ge(silu_up, START + 2)
            def columns(n, col):
                pe.wait_ge(ada_in[n % 2], START + 16 * (n // 2 + 1))
                for j in range(4):
                    for k in range(KD):
                        last = pe.matmul(banks[6][:, col + j:col + j + 1], ada[n % 2][:, k, j * P:(j + 1) * P],
                                         csT[:, k:k + 1], start=(k == 0), stop=(k == KD - 1))
                last.then_inc(ada_used, 1)
            for n in range(4):
                columns(n, 4 * n)
            pe.wait_ge(h_up, START + KD)
            def project(slot, w):
                for k in range(KD):
                    last = pe.matmul(banks[slot][:, :], wt[slot][:, k, :], hT[:, k, :], start=(k == 0),
                                     stop=(k == KD - 1))
                last.then_inc(proj_up, 1)
            for n in range(2):
                pe.wait_ge(wt_in[n], START + 16)
                project(n, n)
            pe.wait_ge(lora_in, START + 48)
            pe.wait_ge(lora_act, START + 2)
            for p in range(PAIRS):
                for j in range(3):
                    n = 3 * p + j
                    if n >= 2:
                        pe.wait_ge(z_used, START + n - 1)
                    cols = slice(p * P, (p + 1) * P)
                    w, r = ((w2a2[0:64, cols], PM[0:64, 12, :]), (w2a2[64:128, cols], PM[64:128, 12, :]),
                            (g2[:, cols], PM[:, 13, :]))[j]
                    pe.matmul(banks[2 + n % 2][:, :], w, r, start=True, stop=True).then_inc(z_up, 1)
            with pe.Fori(0, 6) as i:
                for n in range(2):
                    pe.wait_ge(wt_in[n], START + 16 * i + 32)
                    pe.wait_ge(proj_mixed, START + 2 * i + (n + 1))
                    project(n, None)
            with pe.Fori(0, 2) as i:
                for n in range(2):
                    pe.wait_ge(wt_in[n], START + 16 * i + 128)
                    pe.wait_ge(proj_scaled, START + 2 * i + (13 + n))
                    pe.wait_ge(proj_mixed, START + 14)
                    project(n, None)
            for p in range(PAIRS):
                if p == 0:
                    pe.wait_ge(consts, START + 5)
                pe.wait_ge(sq_up, START + p + 1)
                if p >= 2:
                    pe.wait_ge(ss_max, START + p - 1)
                pe.matmul(banks[4 + p % 2][:, :], diag2[:, :], tmp[p % 2][:, :], start=True, stop=True)\
                    .then_inc(ss_up, 1)
            for n in range(2):
                pe.wait_ge(wt_in[n], START + 16 * 9 + 32)
                pe.wait_ge(proj_scaled, START + 17 + n)
                project(n, None)
            pe.wait_ge(wt_in[0], START + 16 * 9 + 48)
            pe.wait_ge(proj_scaled, START + 19)
            for t in range(NT):
                for k in range(KD):
                    last = pe.matmul(banks[0][:, t * P:(t + 1) * P], hT[:, k, t * P:(t + 1) * P], wt[0][:, k, :],
                                     start=(k == 0), stop=(k == KD - 1))
            last.then_inc(proj_up, 1)
            for p in range(PAIRS):
                pe.wait_ge(rks_up, START + p + 1)
                pe.wait_ge(ss_max, START + PAIRS)
                if p >= 2:
                    pe.wait_ge(bo_up, START + p - 1)
                pe.matmul(banks[4 + p % 2][:, :], diag2[:, :], tmp[2 + p % 2][:, :], start=True, stop=True)\
                    .then_inc(bsum_up, 1)
            def gate(n, bank):
                pe.wait_ge(ada_in[n % 2], START + 16 * (n // 2 + 1))
                for k in range(KD):
                    last = pe.matmul(banks[bank][:, :], csw[:, k, :], ada[n % 2][:, k, :], start=(k == 0),
                                     stop=(k == KD - 1))
                last.then_inc(ada_used, 1)
            pe.wait_ge(cols_used, START + 1)
            gate(4, 2)
            gate(5, 3)
            for n in range(6, 10):
                columns(n, 4 * n - 8)
            pe.wait_ge(gate_used, START + 2)
            gate(10, 2)
            gate(11, 3)

        @block.vector
        def _(dve):
            tally = Tally(p_dve)
            step = stepper(dve, tally)
            dve.wait_ge(par_up, START + 1)
            dve.wait_ge(silu_up, START + 1)
            dve.tensor_tensor(csT[:, :], csT[:, :], par[:, R_C:R_C + KD], ALU.mult).then_inc(silu_up, 1)
            dve.tensor_scalar(omu[:, :], par[:, R_MU:R_MU + RW_TILES], -1.0, 1.0, ALU.mult, ALU.add)\
                .then_inc(silu_up, 1)
            dve.wait_ge(silu_up, START + 3)
            step(dve.tensor_copy(csw[:, :, :], csT[:, :].unsqueeze(2).broadcast_to([P, KD, P])))
            dve.wait_ge(ada_used, START + 4)
            dve.tensor_tensor(mod[:, 0:16], banks[6][:, 0:16], par[:, R_ADAB:R_ADAB + 16], ALU.add)\
                .then_inc(cols_used, 1)
            dve.wait_ge(cols_used, START + 1)
            step(dve.tensor_scalar(mod[:, 8:16], mod[:, 8:16], 1.0, None, ALU.add))
            dve.wait_ge(xt_used, START + 8)
            for k in range(KD):
                dve.tensor_scalar(hT[:, k, :], hT[:, k, :], mod[:, 8 + k:9 + k], mod[:, k:k + 1],
                                  ALU.mult, ALU.add).then_inc(h_up, 1)
            for n in range(2):
                dve.wait_ge(proj_scaled, START + n + 1)
                dve.scalar_tensor_tensor(out=PM[:, 12 + n, 1:], in0=banks[n][:, 0:T - 1],
                                         scalar=par[:, R_MU + 12 + n:R_MU + 13 + n], in1=PM[:, 12 + n, 1:],
                                         op0=ALU.mult, op1=ALU.add).then_inc(proj_mixed, 1)
            with dve.Fori(0, 6) as i:
                for n in range(2):
                    dve.wait_ge(proj_scaled, START + 2 * i + (3 + n))
                    pm = PM[:, bass.ds(2 * i + n, 1), 1:].rearrange("p o t -> p (o t)")
                    dve.scalar_tensor_tensor(out=pm, in0=banks[n][:, 0:T - 1],
                                             scalar=par[:, bass.ds(2 * i + (R_MU + n), 1)], in1=pm,
                                             op0=ALU.mult, op1=ALU.add).then_inc(proj_mixed, 1)
            dve.wait_ge(consts, START + 5)
            dve.wait_ge(z_used, START + 12)
            dve.wait_ge(proj_mixed, START + 14)
            for p in range(PAIRS):
                dve.tensor_scalar(KN[:, p, :], PM[:, 4 + p, :], par[:, R_KK + p:R_KK + p + 1], None, ALU.mult)\
                    .then_inc(kp_up, 1)
            for p in range(PAIRS):
                dve.tensor_tensor_scan(out=CS[:, p, :], data0=keepm[:, :], data1=SW[:, p, :], initial=0.0,
                                       op0=ALU.mult, op1=ALU.add).then_inc(cs_scan, 1)
            for p in range(PAIRS):
                step(dve.tensor_scalar(BO[:, p, :], AI[:, p, :], -1.0, par[:, R_KA + p:R_KA + p + 1], ALU.add,
                                       ALU.mult))
                dve.scalar_tensor_tensor(out=PM[:, 4 + p, :], in0=BO[:, p, :], scalar=1.0, in1=PM[:, 4 + p, :],
                                         op0=ALU.add, op1=ALU.mult).then_inc(kp_up, 1)
            for p in range(PAIRS):
                dve.wait_ge(ss_up, START + p + 1)
                dve.tensor_scalar(PD[:, p, :], banks[4 + p % 2][:, :], 1e-24, None, ALU.max).then_inc(ss_max, 1)
            for p in range(PAIRS):
                dve.wait_ge(ss_root, START + p + 1)
                step(dve.reciprocal(PD[:, p, :], PD[:, p, :]))
                dve.scalar_tensor_tensor(out=KN[:, p, :], in0=KN[:, p, :], scalar=-1.0, in1=PD[:, p, :],
                                         op0=ALU.mult, op1=ALU.mult).then_inc(nk_up, 1)
                dve.wait_ge(nk_up, START + 2 * p + 1)
                dve.scalar_tensor_tensor(out=AI[:, p, :], in0=KN[:, p, :], scalar=-1.0, in1=AI[:, p, :],
                                         op0=ALU.mult, op1=ALU.mult).then_inc(nk_up, 1)
            for p in range(PAIRS):
                dve.wait_ge(rk_up, START + p + 1)
                dve.tensor_scalar(tmp[2 + p % 2][:, :], tmp[2 + p % 2][:, :], par[:, R_RK + p:R_RK + p + 1], None,
                                  ALU.mult).then_inc(rks_up, 1)
            for p in range(PAIRS):
                dve.wait_ge(bsum_up, START + p + 1)
                dve.tensor_tensor(BO[:, p, :], banks[4 + p % 2][:, :], PM[:, 8 + p, :], ALU.mult).then_inc(bo_up, 1)
            dve.wait_ge(exp_up, START + 2 * PAIRS)
            dve.tensor_copy(PL[:, :, :], PD[:, :, CH - 1::CH])
            dve.wait_ge(rk_up, START + PAIRS)
            dve.wait_ge(nk_up, START + 2 * PAIRS)
            for p in range(PAIRS):
                dve.tensor_tensor(PM[:, p, :], PM[:, p, :], PD[:, p, :], ALU.mult)
                dve.tensor_tensor(KN[:, p, :], KN[:, p, :], SW[:, p, :], ALU.mult)
            dve.wait_ge(gb_in, START + 32)
            for m, gt in ((0, gt1), (1, gt2)):
                dve.wait_ge(ada_used, START + (6 if m == 0 else 12))
                for h in range(2):
                    dve.tensor_tensor(gt[:, h * 512:(h + 1) * 512], banks[2 + h][:, :], gt[:, h * 512:(h + 1) * 512],
                                      ALU.add).then_inc(gate_used, 1)
                if m == 0:
                    dve.wait_ge(ada_used, START + 10)
                    step(dve.tensor_tensor(mod[:, 16:32], banks[6][:, 16:32],
                                           par[:, R_ADAB + 24:R_ADAB + 40], ALU.add))
                    dve.tensor_scalar(mod[:, 24:32], mod[:, 24:32], 1.0, None, ALU.add)


def emit_mixing(nc, banks, sem, v):
    attn_sink = v["attn_sink"]
    (ident, par, diag2, qT, kT, vtok, PM, AI, GG, KN, BO, PL, yT) = (
        v[n] for n in ("ident", "par", "diag2", "qT", "kT", "vtok", "PM", "AI", "GG", "KN", "BO", "PL", "yT"))
    ctx = ExitStack()
    with ctx:
        def sb(name, shape, dt=F32):
            return ctx.enter_context(nc.sbuf_tensor(name, shape, dt))

        LV = 6
        masks = sb("masks", [P, 2, P])
        lvl = sb("lvl", [P, LV, P])
        window = sb("window", [P, 2, 2 * P])
        mean2 = sb("mean2", [P, P])
        sinks = sb("sinks", [P, HEADS])
        AR = sb("AR", [P, 2, 4, P])
        Bs, Ks, Vs = (sb(n, [P, 4, P]) for n in ("Bs", "Ks", "Vs"))
        BHs, KHs = (sb(n, [P, 4, P]) for n in ("BHs", "KHs"))
        RH = sb("RH", [P, 2, HEADS, HD])
        VT = sb("VT", [P, HEADS * HD])
        BH, KH = (sb(n, [P, 2, 4, P]) for n in ("BH", "KH"))
        BM, KM = (sb(n, [P, HEADS, 2, P]) for n in ("BM", "KM"))
        PT = sb("PT", [P, HEADS, 2, P])
        NL = [[PT[:, 4 * g + 2 * b:4 * g + 2 * b + 2, :, :].rearrange("p a b c -> p (a b) c") for b in range(2)]
              for g in range(2)]
        DD, DT, XX = ([sb(f"{n}{g}", [P, 4, P]) for g in range(2)] for n in ("DD", "DT", "XX"))
        WW = sb("WW", [P, 2, HEADS, HD])
        QT = sb("QT", [P, 4, P])
        GT, HS = (sb(n, [P, 2, 4, P]) for n in ("GT", "HS"))
        dPL = sb("dPL", [P, 2, 4, P])
        S = [sb(f"S{c}", [P, 4, P]) for c in range(2)]
        Y, Yc, Yq, Yv = (sb(n, [P, 4, P]) for n in ("Y", "Yc", "Yq", "Yv"))
        qs = sb("qs", [P, 4, P])
        ks = sb("ks", [P, 2, 2 * P])
        SC = KM[:, :, :, :].rearrange("p h u k -> p h (u k)")
        mx, nm, es, rs = (sb(n, [P, HEADS]) for n in ("mx", "nm", "es", "rs"))
        ON = sb("ON", [P, HEADS * HD])
        gatepost = sb("gatepost3", [P, 1])

        names = ("ready sink_in ar bks vs bhs gramB maskB gramK maskK tr trA trV trB trK nl dt0 dd0 dd0c xx xxc d dc "
                 "t tc x0 x0c w wc qt qtc g gc h hc y yc st stc m mc sq va vac root rstd gn dpl "
                 "qks sc scm mx ex rsum pt ptc o oc ot otc").split()
        ev = {n: sem("mix_" + n) for n in names}
        p_dve, p_act, p_pool = sem("mix_dve"), sem("mix_act"), sem("mix_pool")
        nc.all_engine_barrier()
        block = ctx.enter_context(nc.Block())

        def waits(eng, n):
            def now(name, k=1, per=1):
                eng.wait_ge(ev[name], START + n * per + k)

            def before(name, per=1):
                eng.wait_ge(ev[name], START + n * per)
            return now, before

        def cols(n):
            return bass.ds(n * P, P)

        def four(ap):
            return ap.rearrange("p (a b) -> p a b", a=4)

        @block.sync
        def _(sp):
            sp.dma_start(sinks[:, :], attn_sink.rearrange("o n -> (o n)").partition_broadcast(P))\
                .then_inc(ev["sink_in"], 16)
            sp.wait_ge(ev["sink_in"], START + 16)

        @block.gpsimd
        def _(pool):
            step = stepper(pool, Tally(p_pool))
            step(pool.memset(masks[:, :, :], 1.0))
            for k in range(2):
                m = masks[:, k, :].rearrange("p (b w) -> p b w", b=2)
                step(pool.affine_select(out=m, in_=m, compare_op=ALU.is_ge, fill=0.0, base=k - 1,
                                        pattern=[[CH, 2], [1, CH]], channel_multiplier=-1))
                step(pool.affine_select(out=m, in_=m, compare_op=ALU.is_ge, fill=0.0, base=0,
                                        pattern=[[-CH, 2], [0, CH]], channel_multiplier=1))
            step(pool.memset(lvl[:, :, :], 1.0))
            for l in range(LV):
                w = 1 << l
                nb = P // (2 * w)
                m = lvl[:, l, :].rearrange("p (b u w) -> p b u w", u=2, w=w)
                for base, pattern, cm in ((0, [[-2 * w, nb], [0, 2], [0, w]], 1),
                                          (w - 1, [[2 * w, nb], [0, 2], [0, w]], -1),
                                          (-1, [[0, nb], [1, 2], [0, w]], 0)):
                    step(pool.affine_select(out=m, in_=m, compare_op=ALU.is_ge, fill=0.0, base=base,
                                            pattern=pattern, channel_multiplier=cm))
            step(pool.memset(window[:, :, :], 0.0))
            for base, pattern, cm in ((P, [[0, 2], [-1, 2 * P]], 1), (-1, [[0, 2], [1, 2 * P]], -1)):
                step(pool.affine_select(out=window[:, :, :], in_=window[:, :, :], compare_op=ALU.is_ge, fill=NEG,
                                        base=base, pattern=pattern, channel_multiplier=cm))
            step(pool.memset(window[:, 0, 0:P], NEG))
            for s in S:
                step(pool.memset(s[:, :, :], 0.0))
            pool.tensor_scalar(mean2[:, :], diag2[:, :], 1.0 / HD, None, ALU.mult).then_inc(ev["ready"], 1)
            with pool.Fori(0, NT) as n:
                now, before = waits(pool, n)
                before("tr", 4)
                pool.tensor_copy(Vs[:, :, :], PM[:, 8:12, cols(n)]).then_inc(ev["vs"], 1)
                decay = PL[:, :, bass.ds(2 * n, 2)].unsqueeze(3).broadcast_to([P, 4, 2, CH])
                for src, dst in ((AI[:, :, cols(n)], BHs), (PM[:, 4:8, cols(n)], KHs)):
                    pool.tensor_tensor(dst[:, :, :].rearrange("p a (c w) -> p a c w", c=2),
                                       src.rearrange("p a (c w) -> p a c w", c=2), decay, ALU.mult)\
                        .then_inc(ev["bhs"], 1)
                for l in range(1, LV):
                    for g in range(2):
                        if l == 1:
                            now("maskB", 2 * g + 2, 4)
                            before("xx", 10)
                            before("o")
                        if l >= 3:
                            now("xx", 2 * (l - 3) + g + 1, 10)
                        pool.tensor_tensor(NL[g][l % 2][:, :, :], BM[:, 4 * g:4 * g + 4, 0, :],
                                           lvl[:, l, :].unsqueeze(1).broadcast_to([P, 4, P]), ALU.mult)\
                            .then_inc(ev["nl"], 1)
                before("gc", 2)
                pool.tensor_tensor(gatepost[:, :], masks[:, 0, 0:1], masks[:, 0, 0:1], ALU.mult)
                for c in range(2):
                    pool.tensor_tensor(dPL[:, c, :, :], ident[:, :].unsqueeze(1).broadcast_to([P, 4, P]),
                                       PL[:, :, bass.ds(2 * n + c, 1)].broadcast_to([P, 4, P]), ALU.mult)\
                        .then_inc(ev["dpl"], 1)

        @block.scalar
        def _(act):
            with act.Fori(0, NT) as n:
                now, before = waits(act, n)
                before("gramK", 4)
                before("qtc")
                act.activation(AR[:, 0, :, :], KN[:, :, cols(n)], ACT.Copy).then_inc(ev["ar"], 1)
                act.activation(AR[:, 1, :, :], PM[:, 0:4, cols(n)], ACT.Copy).then_inc(ev["ar"], 1)
                before("sc", 4)
                act.activation(qs[:, :, :], qT[:, :, cols(n)], ACT.Copy).then_inc(ev["qks"], 1)
                act.activation(ks[:, :, :], kT[:, :, bass.ds(n * P, 2 * P)], ACT.Copy).then_inc(ev["qks"], 1)
                now("tr", 1, 4)
                before("w", 2)
                act.activation(RH[:, 0, :, :].rearrange("p h d -> p (h d)"), banks[4][:, :], ACT.Copy)\
                    .then_inc(ev["trA"], 1)
                now("tr", 2, 4)
                before("st", 2)
                act.activation(VT[:, :], banks[5][:, :], ACT.Copy).then_inc(ev["trV"], 1)
                for j, (dst, name) in enumerate(((BH, "trB"), (KH, "trK"))):
                    now("tr", 3 + j, 4)
                    for c in range(2):
                        act.activation(dst[:, c, :, :], four(banks[6 + j][:, :]), ACT.Copy,
                                       scale=diag2[:, CH * c:CH * c + 1]).then_inc(ev[name], 1)
                for g in range(2):
                    now("dd0", g + 1, 2)
                    act.activation(DD[g][:, :, :], four(banks[g][:, :]), ACT.Copy).then_inc(ev["dd0c"], 1)
                for l in range(1, LV):
                    for g in range(2):
                        if l < LV - 1:
                            now("d", 2 * (l - 1) + g + 1, 8)
                            act.activation(DD[g][:, :, :], four(banks[2 + g][:, :]), ACT.Copy)\
                                .then_inc(ev["dc"], 1)
                        now("t", 2 * (l - 1) + g + 1, 10)
                        act.activation(DT[g][:, :, :], four(banks[6 + g][:, :]), ACT.Copy).then_inc(ev["tc"], 1)
                now("x0")
                act.activation(RH[:, 1, :, :].rearrange("p h d -> p (h d)"), banks[4][:, :], ACT.Copy)\
                    .then_inc(ev["x0c"], 1)
                for g in range(2):
                    now("w", g + 1, 2)
                    act.activation(WW[:, :, 4 * g:4 * g + 4, :],
                                   banks[g][:, :].rearrange("p (h u d) -> p u h d", u=2, d=HD), ACT.Copy)\
                        .then_inc(ev["wc"], 1)
                now("y")
                before("m")
                act.activation(Y[:, :, :], four(banks[4][:, :]), ACT.Copy).then_inc(ev["yc"], 1)
                now("mc")
                act.activation(Yq[:, :, :], Yc[:, :, :], ACT.Square).then_inc(ev["sq"], 1)
                now("vac")
                act.activation(Yv[:, :, :], Yv[:, :, :], ACT.Sqrt).then_inc(ev["root"], 1)
                now("mx")
                before("rsum")
                act.activation(es[:, :], es[:, :], ACT.Exp).then_inc(ev["ex"], 1)
                for h in range(HEADS):
                    act.activation(SC[:, h, :], SC[:, h, :], ACT.Exp, bias=nm[:, h:h + 1],
                                   accum_out=rs[:, h:h + 1]).then_inc(ev["ex"], 1)
                for j in range(4):
                    now("pt", j + 1, 4)
                    act.activation(PT[:, 2 * j:2 * j + 2, :, :].rearrange("p h k q -> p (h k q)"),
                                   banks[2 + j][:, :], ACT.Copy).then_inc(ev["ptc"], 1)
                now("ot")
                act.activation(yT[:, 0:4, cols(n)], four(banks[7][:, :]), ACT.Copy).then_inc(ev["otc"], 1)

        @block.tensor
        def _(pe):
            pe.wait_ge(ev["ready"], START + 1)
            with pe.Fori(0, NT) as n:
                now, before = waits(pe, n)

                def grams(src, first, name):
                    for g in range(2):
                        for e in range(2):
                            for j in range(2):
                                p = 2 * g + j
                                rows = slice(64 * e, 64 * e + 64)
                                last = pe.matmul(banks[first + 2 * g + e][:, 256 * j:256 * j + 256],
                                                 src[rows, p, :], AR[rows, :, p, :], start=True, stop=True)
                            last.then_inc(ev[name], 1)
                now("ar", 2, 2)
                now("bks", 2, 2)
                before("gn")
                before("otc")
                grams(Bs, 0, "gramB")
                now("vs")
                now("bhs", 2, 2)
                for b, src in ((4, AR[:, 0]), (5, Vs), (6, BHs), (7, KHs)):
                    for p in range(4):
                        last = pe.transpose(banks[b][:, p * P:(p + 1) * P],
                                            src[:, p, :], ident[:, :])
                    last.then_inc(ev["tr"], 1)
                for g in range(2):
                    now("dt0", g + 1, 2)
                    for h in range(4):
                        last = pe.transpose(banks[g][:, h * P:(h + 1) * P], DT[g][:, h, :], ident[:, :])
                    last.then_inc(ev["dd0"], 1)
                now("maskB", 4, 4)
                now("trV")
                grams(Ks, 2, "gramK")
                for l in range(1, LV):
                    for g in range(2):
                        now("nl", 2 * (l - 1) + g + 1, 10)
                        if l == 1:
                            now("dd0c", g + 1, 2)
                        else:
                            now("dc", 2 * (l - 2) + g + 1, 8)
                        for h in range(4):
                            last = pe.matmul(banks[g][:, h * P:(h + 1) * P], NL[g][l % 2][:, h, :],
                                             DD[g][:, h, :], start=True, stop=True)
                        last.then_inc(ev["xx"], 1)
                    for g in range(2):
                        now("xxc", 2 * (l - 1) + g + 1, 10)
                        if l == 1:
                            now("maskK", 4, 4)
                            now("trK", 2, 2)
                        else:
                            now("tc", 2 * (l - 2) + g + 1, 10)
                        if l < LV - 1:
                            for h in range(4):
                                last = pe.matmul(banks[2 + g][:, h * P:(h + 1) * P], DT[g][:, h, :],
                                                 XX[g][:, h, :], start=True, stop=True)
                            last.then_inc(ev["d"], 1)
                        for h in range(4):
                            last = pe.matmul(banks[6 + g][:, h * P:(h + 1) * P], XX[g][:, h, :],
                                             DT[g][:, h, :], start=True, stop=True)
                        last.then_inc(ev["t"], 1)
                for h in range(HEADS):
                    last = pe.matmul(banks[4][:, h * HD:(h + 1) * HD], KM[:, h, 0, :],
                                     VT[:, h * HD:(h + 1) * HD], start=True, stop=True)
                last.then_inc(ev["x0"], 1)
                now("x0c")
                now("tc", 10, 10)
                for g in range(2):
                    for h in range(4):
                        last = pe.matmul(banks[g][:, h * P:(h + 1) * P], DT[g][:, h, :],
                                         RH[:, :, 4 * g + h, :], start=True, stop=True)
                    last.then_inc(ev["w"], 1)
                now("wc", 2, 2)
                for h in range(HEADS):
                    last = pe.matmul(banks[5][64 * (h % 2):64 * (h % 2) + 64, (h // 2) * P:(h // 2 + 1) * P],
                                     WW[:, 0, h, :], BM[:, h, 1, :], start=True, stop=True)
                last.then_inc(ev["qt"], 1)
                for c in range(2):
                    for p in range(4):
                        last = pe.matmul(banks[2 + c][:, p * P:(p + 1) * P], WW[:, 0, 2 * p:2 * p + 2, :],
                                         BH[:, c, p, :], start=True, stop=True)
                    last.then_inc(ev["g"], 1)
                    for p in range(4):
                        pe.matmul(banks[6 + c][:, p * P:(p + 1) * P], BH[:, c, p, :],
                                  WW[:, 1, 2 * p:2 * p + 2, :], start=True, stop=False)
                        last = pe.matmul(banks[6 + c][:, p * P:(p + 1) * P], KH[:, c, p, :],
                                         VT[:, p * P:(p + 1) * P], start=False, stop=True)
                    last.then_inc(ev["h"], 1)
                for e in range(2):
                    for p in range(4):
                        h = 2 * p + e
                        o = banks[4][64 * e:64 * e + 64, p * P:(p + 1) * P]
                        pe.matmul(o, WW[:, 1, h, :], BM[:, h, 1, :], start=(p == 0), stop=False,
                                  skip_group_check=True)
                        pe.matmul(o, VT[:, h * HD:(h + 1) * HD], KM[:, h, 1, :], start=False, stop=False,
                                  skip_group_check=True)
                now("qtc")
                for c in range(2):
                    if c == 0:
                        before("stc", 2)
                    else:
                        now("stc", 1, 2)
                    for p in range(4):
                        o = banks[4][:, p * P + CH * c:p * P + CH * c + CH]
                        last = pe.matmul(o, S[c][:, p, :], QT[:, p, CH * c:CH * c + CH], start=False, stop=True,
                                         skip_group_check=True)
                    if c == 1:
                        last.then_inc(ev["y"], 1)
                    now("gc", c + 1, 2)
                    for p in range(4):
                        last = pe.matmul(banks[c][:, p * P:(p + 1) * P], GT[:, c, p, :], S[c][:, p, :],
                                         start=True, stop=True)
                    last.then_inc(ev["st"], 1)
                now("qks", 2, 2)
                now("hc", 2, 2)
                for g in range(2):
                    for e in range(2):
                        b = (2, 3, 6, 7)[2 * g + e]
                        for j in range(2):
                            rows = slice(64 * e, 64 * e + 64)
                            last = pe.matmul(banks[b][:, 256 * j:256 * j + 256], qs[rows, 2 * g + j, :],
                                             ks[rows, g, :], start=True, stop=True)
                        last.then_inc(ev["sc"], 1)
                now("yc")
                pe.matmul(banks[5][:, :], mean2[:, :], Y[:, :, :].rearrange("p a b -> p (a b)"), start=True,
                          stop=True).then_inc(ev["m"], 1)
                now("sq")
                pe.matmul(banks[5][:, :], mean2[:, :], Yq[:, :, :].rearrange("p a b -> p (a b)"), start=True,
                          stop=True).then_inc(ev["va"], 1)
                now("vac")
                now("scm", 4, 4)
                now("ex", 9, 9)
                for j in range(4):
                    for h in (2 * j, 2 * j + 1):
                        for k in range(2):
                            last = pe.transpose(banks[2 + j][:, (h % 2) * 256 + k * P:(h % 2) * 256 + (k + 1) * P],
                                                SC[:, h, k * P:(k + 1) * P], ident[:, :])
                    last.then_inc(ev["pt"], 1)
                for h in range(HEADS):
                    now("ptc", h // 2 + 1, 4)
                    for k in range(2):
                        last = pe.matmul(banks[6][:, h * HD:(h + 1) * HD], PT[:, h, k, :],
                                         vtok[:, bass.ds(n + k, 1), 64 * (h // 4):64 * (h // 4) + 64]
                                         .rearrange("p o d -> p (o d)"), start=(k == 0), stop=(k == 1))
                last.then_inc(ev["o"], 1)
                now("oc")
                for p in range(4):
                    last = pe.transpose(banks[7][:, p * P:(p + 1) * P], ON[:, p * P:(p + 1) * P], ident[:, :])
                last.then_inc(ev["ot"], 1)

        @block.vector
        def _(dve):
            per = 12
            chain = Tally(p_dve)
            dve.wait_ge(ev["ready"], START + 1)
            dve.wait_ge(ev["sink_in"], START + 16)
            with dve.Fori(0, NT) as n:
                now, before = waits(dve, n)
                chain.enter(n, per)
                step = stepper(dve, chain)
                before("gramK", 4)
                dve.tensor_copy(Bs[:, :, :], AI[:, :, cols(n)]).then_inc(ev["bks"], 1)
                dve.tensor_copy(Ks[:, :, :], PM[:, 4:8, cols(n)]).then_inc(ev["bks"], 1)

                def mask(bank, dst, name, g, e):
                    dve.tensor_tensor(dst[:, 4 * g + e:4 * g + e + 3:2, :, :].rearrange("p h u t -> p h (u t)"),
                                      banks[bank][:, :].rearrange("p (h u) -> p h u", h=2),
                                      masks[:, :, :].rearrange("p u t -> p (u t)").unsqueeze(1)
                                      .broadcast_to([P, 2, 2 * P]), ALU.mult).then_inc(ev[name], 1)
                before("y")
                for g in range(2):
                    for e in range(2):
                        now("gramB", 2 * g + e + 1, 4)
                        mask(2 * g + e, BM, "maskB", g, e)
                for g in range(2):
                    now("maskB", 2 * g + 2, 4)
                    before("w", 2)
                    step(dve.tensor_tensor(DT[g][:, :, :], BM[:, 4 * g:4 * g + 4, 0, :],
                                           lvl[:, 0, :].unsqueeze(1).broadcast_to([P, 4, P]), ALU.mult))
                    dve.tensor_tensor(DT[g][:, :, :], DT[g][:, :, :],
                                      ident[:, :].unsqueeze(1).broadcast_to([P, 4, P]), ALU.add)\
                        .then_inc(ev["dt0"], 1)
                for g in range(2):
                    for e in range(2):
                        now("gramK", 2 * g + e + 1, 4)
                        mask(2 + 2 * g + e, KM, "maskK", g, e)
                for l in range(1, LV):
                    for g in range(2):
                        now("xx", 2 * (l - 1) + g + 1, 10)
                        dve.tensor_tensor(XX[g][:, :, :], four(banks[g][:, :]),
                                          ident[:, :].unsqueeze(1).broadcast_to([P, 4, P]), ALU.add)\
                            .then_inc(ev["xxc"], 1)
                now("qt")
                dve.tensor_tensor(QT[:, :, :], four(banks[5][:, :]), AR[:, 1, :, :], ALU.add)\
                    .then_inc(ev["qtc"], 1)
                dg = diag2[:, :].unsqueeze(1).broadcast_to([P, 4, P])
                for c in range(2):
                    now("g", c + 1, 2)
                    now("dpl", c + 1, 2)
                    step(dve.tensor_tensor(GT[:, c, :, :], four(banks[2 + c][:, :]), dg, ALU.mult))
                    dve.tensor_tensor(GT[:, c, :, :], GT[:, c, :, :], dPL[:, c, :, :], ALU.add)\
                        .then_inc(ev["gc"], 1)
                    now("h", c + 1, 2)
                    dve.tensor_tensor(HS[:, c, :, :], four(banks[6 + c][:, :]), dg, ALU.mult)\
                        .then_inc(ev["hc"], 1)
                for c in range(2):
                    now("st", c + 1, 2)
                    now("hc", c + 1, 2)
                    if c == 0:
                        before("y")
                    dve.tensor_tensor(S[1 - c][:, :, :], four(banks[c][:, :]), HS[:, c, :, :], ALU.add)\
                        .then_inc(ev["stc"], 1)
                now("m")
                dve.tensor_tensor(Yc[:, :, :], Y[:, :, :], four(banks[5][:, :]), ALU.subtract)\
                    .then_inc(ev["mc"], 1)
                now("va")
                dve.tensor_scalar(Yv[:, :, :], four(banks[5][:, :]), GN_EPS, None, ALU.add).then_inc(ev["vac"], 1)
                for g in range(2):
                    for e in range(2):
                        now("sc", 2 * g + e + 1, 4)
                        b = (2, 3, 6, 7)[2 * g + e]
                        last = dve.tensor_tensor(
                            SC[:, 4 * g + e:4 * g + e + 3:2, :], banks[b][:, :].rearrange("p (h k) -> p h k", h=2),
                            window[:, bass.ds((n + 3) // 4, 1), :].broadcast_to([P, 2, 2 * P]), ALU.add)
                        last.then_inc(ev["scm"], 1)
                now("scm", 4, 4)
                step(dve.tensor_reduce(mx[:, :], SC[:, :, :], AX.X, ALU.max))
                step(dve.tensor_tensor(mx[:, :], mx[:, :], sinks[:, :], ALU.max))
                dve.tensor_scalar(nm[:, :], mx[:, :], -1.0, None, ALU.mult)
                dve.tensor_tensor(es[:, :], sinks[:, :], mx[:, :], ALU.subtract).then_inc(ev["mx"], 1)
                now("root")
                lx = [par[:, r:r + 4].unsqueeze(2).broadcast_to([P, 4, P]) for r in (R_LXG, R_LXB)]
                step(dve.reciprocal(Yv[:, :, :], Yv[:, :, :]))
                step(dve.tensor_tensor(Yc[:, :, :], Yc[:, :, :], Yv[:, :, :], ALU.mult))
                step(dve.tensor_tensor(Yc[:, :, :], Yc[:, :, :], lx[0], ALU.mult))
                step(dve.tensor_tensor(Yc[:, :, :], Yc[:, :, :], lx[1], ALU.add))
                step(dve.tensor_tensor(Yc[:, :, :], Yc[:, :, :], BO[:, :, cols(n)], ALU.add))
                dve.tensor_tensor(yT[:, 4:8, cols(n)], Yc[:, :, :], GG[:, :, cols(n)], ALU.mult)\
                    .then_inc(ev["gn"], 1)
                now("ex", 9, 9)
                step(dve.tensor_tensor(rs[:, :], rs[:, :], es[:, :], ALU.add))
                dve.reciprocal(rs[:, :], rs[:, :]).then_inc(ev["rsum"], 1)
                now("rsum")
                now("o")
                before("ot")
                dve.tensor_tensor(ON[:, :].rearrange("p (h d) -> p h d", h=HEADS),
                                  banks[6][:, :].rearrange("p (h d) -> p h d", h=HEADS),
                                  rs[:, :].unsqueeze(2).broadcast_to([P, HEADS, HD]), ALU.mult)\
                    .then_inc(ev["oc"], 1)
                chain.leave(NT)


TB = 32


class Norm:

    def __init__(self, nc, sb, prefix):
        self.nc = nc
        self.stats = [sb(f"{prefix}stats{i}", [P, 2, 6]) for i in range(2)]
        self.mv = [sb(f"{prefix}mv{i}", [P, 2]) for i in range(2)]
        self.sd = [sb(f"{prefix}sd{i}", [P, 1]) for i in range(2)]

    def moments(self, dve, step, t, tile):
        for h in range(2):
            last = dve.bn_stats(out=self.stats[t % 2][:, h, :], in_=tile[:, 512 * h:512 * h + 512])
        step(last)
        step(dve.bn_aggr(out=self.mv[t % 2][:, :], in_=self.stats[t % 2][:, :, :].rearrange("p a b -> p (a b)")))
        return dve.tensor_scalar(self.sd[t % 2][:, :], self.mv[t % 2][:, 1:2], LN_EPS, None, ALU.add)

    def root(self, act, t):
        return act.activation(self.sd[t % 2][:, :], self.sd[t % 2][:, :], ACT.Sqrt)

    def scaled(self, dve, step, t, tile):
        step(dve.reciprocal(self.sd[t % 2][:, :], self.sd[t % 2][:, :]))
        return dve.tensor_scalar(tile, tile, self.mv[t % 2][:, 0:1], self.sd[t % 2][:, :], ALU.subtract, ALU.mult)


def emit_mix_out(nc, banks, sem, v):
    x, w_out, ln1_g, ln1_b, ident, mod, gt1, yT, x1_kept, h2, hh, hl = (
        v[n] for n in ("x", "w_out", "ln1_g", "ln1_b", "ident", "mod", "gt1", "yT", "x1_kept", "h2", "hh", "hl"))
    ctx = ExitStack()
    with ctx:
        def sb(name, shape, dt=F32):
            return ctx.enter_context(nc.sbuf_tensor(name, shape, dt))

        wo = [sb(f"wo{k}", [P, D]) for k in range(KD)]
        xs = sb("xs", [P, NT, D])
        x1 = sb("x1", [P, NT, D])
        lg, lb = sb("lg", [P, D]), sb("lb", [P, D])
        norm = Norm(nc, sb, "n1_")
        wo_in = [sem(f"wo_in{k}") for k in range(KD)]
        xs_in, ln_in = sem("xs_in"), sem("ln_in")
        y_up, y_used, var_up, root_up = sem("y_up"), sem("y_used"), sem("var_up"), sem("root_up")
        centred, gained, x1_up = sem("centred"), sem("gained"), sem("x1_up")
        xt_up, h_up, hh_up, hl_up = sem("x1t_up"), sem("h2_up"), sem("hh_up"), sem("hl_up")
        p_dve, kept = sem("p_dve3"), sem("x1_kept3")
        nc.all_engine_barrier()
        block = ctx.enter_context(nc.Block())

        @block.sync
        def _(sp):
            wv = w_out[0].rearrange("(k p) n -> k p n", p=P)
            for k in range(KD):
                sp.dma_start(wo[k][:, :], wv[k]).then_inc(wo_in[k], 16)
            sp.dma_start(xs[:, :, :], x[0].rearrange("(t p) d -> p t d", p=P)).then_inc(xs_in, 16)
            for dst, src in ((lg, ln1_g), (lb, ln1_b)):
                sp.dma_start(dst[:, :], src.rearrange("o n -> (o n)").partition_broadcast(P)).then_inc(ln_in, 16)
            for t in range(NT):
                sp.wait_ge(x1_up, START + t + 1)
                sp.dma_start(x1_kept[t], x1[:, t, :]).then_inc(kept, 16)
            sp.wait_ge(ln_in, START + 32)
            sp.wait_ge(kept, START + 16 * NT)

        @block.tensor
        def _(pe):
            def turn(t):
                pe.wait_ge(x1_up, START + t + 1)
                for h in range(2):
                    for k in range(4):
                        last = pe.transpose(banks[4 + 2 * (t % 2) + h][:, k * P:(k + 1) * P],
                                            x1[:, t, (4 * h + k) * P:(4 * h + k + 1) * P], ident[:, :])
                    last.then_inc(xt_up, 1)
            for t in range(NT):
                if t >= 2:
                    pe.wait_ge(y_used, START + 2 * (t - 1))
                for h in range(2):
                    for k in range(KD):
                        if t == 0 and h == 0:
                            pe.wait_ge(wo_in[k], START + 16)
                        last = pe.matmul(banks[2 * (t % 2) + h][:, :], yT[:, k, t * P:(t + 1) * P],
                                         wo[k][:, 512 * h:512 * h + 512], start=(k == 0), stop=(k == KD - 1))
                    last.then_inc(y_up, 1)
                if t >= 1:
                    if t >= 3:
                        pe.wait_ge(h_up, START + 8 * (t - 2))
                    turn(t - 1)
            pe.wait_ge(h_up, START + 8 * (NT - 2))
            turn(NT - 1)

        def split(dve, t):
            cols = slice(t * P, (t + 1) * P)
            dve.wait_ge(h_up, START + 8 * (t + 1))
            dve.tensor_copy(hh[:, :, cols], h2[:, :, cols]).then_inc(hh_up, 1)
            dve.wait_ge(hh_up, START + t + 1)
            dve.tensor_tensor(hl[:, :, cols], h2[:, :, cols], hh[:, :, cols].bitcast(F32), ALU.subtract)\
                .then_inc(hl_up, 1)

        @block.vector
        def _(dve):
            step = stepper(dve, Tally(p_dve))
            def head(t):
                for h in range(2):
                    half = slice(512 * h, 512 * h + 512)
                    dve.wait_ge(y_up, START + 2 * t + h + 1)
                    ins = dve.tensor_tensor(x1[:, t, half], banks[2 * (t % 2) + h][:, :], gt1[:, half], ALU.mult)
                    ins.then_inc(y_used, 1)
                dve.wait_ge(xs_in, START + 16)
                dve.wait_ge(y_used, START + 2 * t + 2)
                step(dve.scalar_tensor_tensor(out=x1[:, t, :], in0=xs[:, t, :], scalar=ALPHA, in1=x1[:, t, :],
                                              op0=ALU.mult, op1=ALU.add))
                norm.moments(dve, step, t, x1[:, t, :]).then_inc(var_up, 1)

            def tail(t):
                dve.wait_ge(root_up, START + t + 1)
                norm.scaled(dve, step, t, x1[:, t, :]).then_inc(centred, 1)
                dve.wait_ge(gained, START + t + 1)
                dve.tensor_tensor(x1[:, t, :], x1[:, t, :], lb[:, :], ALU.add).then_inc(x1_up, 1)
            dve.wait_ge(ln_in, START + 32)
            for t in range(NT):
                head(t)
                tail(t)
                if t >= 1:
                    split(dve, t - 1)
            split(dve, NT - 1)

        @block.gpsimd
        def _(pool):
            pool.wait_ge(ln_in, START + 32)
            for t in range(NT):
                pool.wait_ge(centred, START + t + 1)
                pool.tensor_tensor(x1[:, t, :], x1[:, t, :], lg[:, :], ALU.mult).then_inc(gained, 1)

        @block.scalar
        def _(act):
            for t in range(NT):
                act.wait_ge(var_up, START + t + 1)
                norm.root(act, t).then_inc(root_up, 1)
                for k in range(KD):
                    act.wait_ge(xt_up, START + 2 * t + k // 4 + 1)
                    act.activation(h2[:, k, t * P:(t + 1) * P],
                                   banks[4 + 2 * (t % 2) + k // 4][:, (k % 4) * P:(k % 4 + 1) * P], ACT.Identity,
                                   bias=mod[:, 16 + k:17 + k], scale=mod[:, 24 + k:25 + k]).then_inc(h_up, 1)


class ExpertScores:

    def __init__(self, nc, sb, sem, prefix, banks, ident, hh, hl, ring, peer_u):
        self.nc, self.banks, self.ident, self.hh, self.hl, self.ring = nc, banks, ident, hh, hl, ring
        self.u = [sb(f"{prefix}u{s}", [P, D]) for s in range(4)]
        self.uraw = sb(prefix + "uraw", [P, KD, P])
        self.uh = [sb(f"{prefix}uh{s}", [P, KD, P], F32R) for s in range(2)]
        self.ul = [sb(f"{prefix}ul{s}", [P, KD, P], F32R) for s in range(2)]
        self.u_in = [sem(f"{prefix}u_in{s}") for s in range(4)]
        self.turned, self.uh_up, self.uraw_up, self.ul_up, self.a_up, self.gelu_up = (
            sem(prefix + n) for n in ("turned", "uh_up", "uraw_up", "ul_up", "a_up", "gelu_up"))
        self.src = peer_u[0].rearrange("(i j) d -> i j d", j=NKEYS)

    def load(self, sp, i, s, tile):
        sp.dma_start(self.u[s][:, :], self.src[:, tile, :]).then_inc(self.u_in[s], 16)

    def turn(self, pe, i, s):
        pe.wait_ge(self.u_in[s], START + 16 * i + 16)
        for h in range(2):
            pe.wait_ge(self.uraw_up, START + 8 * i + (2 * s + h - 1))
            for k in range(4):
                last = pe.transpose(self.banks[2 + h][:, k * P:(k + 1) * P],
                                    self.u[s][:, (4 * h + k) * P:(4 * h + k + 1) * P], self.ident[:, :])
            last.then_inc(self.turned, 1)

    def product(self, pe, i, s, part=None):
        bank, uh, ul = self.banks[s % 2], self.uh[s % 2], self.ul[s % 2]
        if part in (None, 0):
            pe.wait_ge(self.uh_up, START + 8 * i + 2 * s + 2)
            pe.wait_ge(self.gelu_up, START + 4 * i + (s - 1))
        steps = [(uh, k, self.hh) for k in range(KD)] + [(uh, k, self.hl) for k in range(KD)]
        steps = [x for pair in zip(steps[:KD], steps[KD:]) for x in pair] + [(ul, k, self.hh) for k in range(KD)]
        for n in range(3 * KD) if part is None else range(3 * part, 3 * part + 3):
            if n == 2 * KD:
                pe.wait_ge(self.ul_up, START + 4 * i + s + 1)
            u, k, h = steps[n]
            last = pe.matmul(bank[:, :], u[:, k, :], h[:, k, :], start=(n == 0), stop=(n == 3 * KD - 1))
        if part in (None, KD - 1):
            last.then_inc(self.a_up, 1)

    def evacuate(self, act, i, s):
        act.wait_ge(self.a_up, START + 4 * i + (s - 1))
        for h in range(2):
            act.wait_ge(self.turned, START + 8 * i + 2 * s + h + 1)
            act.activation(self.uh[s % 2][:, 4 * h:4 * h + 4, :],
                           self.banks[2 + h][:, :].rearrange("p (k e) -> p k e", k=4), ACT.Copy)\
                .then_inc(self.uh_up, 1)
            if h == 0:
                act.wait_ge(self.ul_up, START + 4 * i + s)
            act.activation(self.uraw[:, 4 * h:4 * h + 4, :],
                           self.banks[2 + h][:, :].rearrange("p (k e) -> p k e", k=4), ACT.Copy)\
                .then_inc(self.uraw_up, 1)

    def remainder(self, pool, i, s):
        pool.wait_ge(self.uraw_up, START + 8 * i + 2 * s + 2)
        pool.wait_ge(self.uh_up, START + 8 * i + 2 * s + 2)
        pool.wait_ge(self.a_up, START + 4 * i + (s - 1))
        pool.tensor_tensor(self.ul[s % 2][:, :, :], self.uraw[:, :, :], self.uh[s % 2][:, :, :].bitcast(F32),
                           ALU.subtract).then_inc(self.ul_up, 1)

    def gelu(self, act, i, s, slot):
        act.wait_ge(self.a_up, START + 4 * i + s + 1)
        act.activation(self.ring[:, slot, :], self.banks[s % 2][:, :], ACT.Gelu).then_inc(self.gelu_up, 1)


def emit_routing(nc, banks, sem, v):
    peer_wq, peer_subkeys, peer_u, ident, h2, hh, hl, ring, gates = (
        v[n] for n in ("peer_wq", "peer_subkeys", "peer_u", "ident", "h2", "hh", "hl", "ring", "gates"))
    ctx = ExitStack()
    with ctx:
        def sb(name, shape, dt=F32):
            return ctx.enter_context(nc.sbuf_tensor(name, shape, dt))

        FV, IS, JS = (sb(n, [P, NT, HEADS, TOPK]) for n in ("FV", "IS", "JS"))
        wq = [sb(f"wq{c}", [P, KD, P]) for c in range(2)]
        sk = [sb(f"sk{c}", [P, P]) for c in range(2)]
        skT = [sb(f"skT{c}", [P, P]) for c in range(2)]
        q2 = [sb(f"q2{c}", [P, T]) for c in range(2)]
        SS = sb("SS", [P, HEADS, 2, NT, NKEYS])
        st = sb("st", [P, 8, NKEYS])
        st2 = sb("st2", [P, 8, NKEYS])
        cand, cand2 = (m[:, :, :].rearrange("p (t a) (c b) -> p t (a c) b", t=NT, b=TOPK) for m in (st, st2))
        sv = sb("sv", [P, 8, TOPK])
        si = sb("si", [P, 8, TOPK], U32)
        sif = sb("sif", [P, 8, TOPK])
        fv = sb("fv", [P, NT, TOPK])
        fp = sb("fp", [P, NT, TOPK], U32)
        fa = [sb(f"fa{c}", [P, NT * TOPK], U32) for c in range(2)]
        ff = [sb(f"ff{c}", [P, NT * TOPK]) for c in range(2)]
        iota = sb("iota", [P, P])
        iota16 = iota[:, 0:TOPK]
        gatepost = sb("gatepost", [P, 1])
        tot = sb("tot", [P, NT, HEADS])
        SLOTS = 4
        turned = [m.rearrange("p u n -> p (u n)") for m in (st[:, 0:4, :], st[:, 4:8, :], st2[:, 0:4, :])]
        OI, OJ = ([h2[:, SLOTS * j + q, :].rearrange("p (t n) -> p t n", t=4) for q in range(SLOTS)]
                  for j in range(2))
        stage = [SS[:, 4 * b:4 * b + 4, :, :, :].rearrange("p h c t n -> p (h c t n)")
                 .rearrange("p (j t) -> p j t", t=TB) for b in range(2)]
        less_up, exp_up, gate_up, t_up, t_out = (
            sem(n) for n in ("less_up", "exp_up4", "gate_up4", "t_up4", "t_out4"))
        hot, spread, staged, p_soft = sem("hot"), sem("spread"), sem("staged"), sem("p_soft")
        sent = [sem(f"sent{b}") for b in range(2)]
        HT = HEADS // 4
        assert (AHEAD - HT) * 4 == T // TB
        scores = ExpertScores(nc, sb, sem, "r_", banks, ident, hh, hl, ring, peer_u)
        wq_in = [sem(f"wq_in{c}") for c in range(2)]
        sk_in = [sem(f"sk_in{c}") for c in range(2)]
        q_up, q_out, k_up, k_out, s_up, s_out = (sem(n) for n in ("q_up", "q_out", "k_up", "k_out", "s_up", "s_out"))
        iota_up, p_dve = sem("iota_up"), sem("p_dve4")
        nc.all_engine_barrier()
        block = ctx.enter_context(nc.Block())

        @block.sync
        def _(sp):
            wv = peer_wq[0].rearrange("(k p) n -> p k n", p=P)
            kv = peer_subkeys[0].rearrange("h c n d -> n (h c) d")
            for c in range(2):
                sp.dma_start(wq[c][:, :, :], wv[:, :, c * P:(c + 1) * P]).then_inc(wq_in[c], 16)
                sp.dma_start(sk[c][:, :], kv[:, c, :]).then_inc(sk_in[c], 16)
            for s in range(4):
                scores.load(sp, 0, s, s)
            with sp.Fori(0, HT) as i:
                for s in range(4):
                    h, nxt = 4 * i + s, (4 * i + (s + 1)) % HEADS
                    for c in range(2):
                        sp.wait_ge(q_up, START + 2 * h + (c + 1))
                        sp.dma_start(wq[c][:, :, :], wv[:, :, bass.ds((2 * nxt + c) * P, P)]).then_inc(wq_in[c], 16)
                        sp.wait_ge(k_up, START + 2 * h + (c + 1))
                        sp.dma_start(sk[c][:, :], kv[:, bass.ds(2 * nxt + c, 1), :].rearrange("n o d -> n (o d)"))\
                            .then_inc(sk_in[c], 16)
                    sp.wait_ge(scores.turned, START + 8 * i + (2 * s + 2))
                    scores.load(sp, i + 1, s, bass.ds(4 * (i + 1) + s, 1))
            with sp.Fori(HT, AHEAD) as i:
                for s in range(4):
                    n = 4 * (i - HT) + s
                    sp.wait_ge(staged, START + (TB // 4) * (n + 1))
                    sp.dma_start(gates[:, bass.ds(n, 1), :, :].rearrange("p o j t -> p (o j t)"),
                                 stage[s % 2].rearrange("p j t -> p (j t)")).then_inc(sent[s % 2], 16)
                    sp.wait_ge(scores.turned, START + 8 * i + (2 * s + 2))
                    scores.load(sp, i + 1, s, bass.ds(4 * (i + 1) + s, 1))
            for b in range(2):
                sp.wait_ge(sent[b], START + 16 * (T // TB // 2))
                sp.wait_ge(wq_in[b], START + 16 * (HEADS + 1))
                sp.wait_ge(sk_in[b], START + 16 * (HEADS + 1))
            for s in range(4):
                sp.wait_ge(scores.u_in[s], START + 16 * (AHEAD + 1))

        @block.gpsimd
        def _(pool):
            pool.iota(iota[:, :], pattern=[[1, P]], base=0, channel_multiplier=0,
                      allow_small_or_imprecise_dtypes=True).then_inc(iota_up, 1)
            with pool.Fori(0, AHEAD) as i:
                for s in range(4):
                    scores.remainder(pool, i, s)

        @block.tensor
        def _(pe):
            with pe.Fori(0, HT) as i:
                scores.turn(pe, i, 0)
                for s in range(4):
                    h = 4 * i + s
                    for c in range(2):
                        pe.wait_ge(wq_in[c], START + 16 * h + 16)
                        pe.wait_ge(q_out, START + 2 * h)
                        for k in range(KD):
                            last = pe.matmul(banks[4 + c][:, :], wq[c][:, k, :], h2[:, k, :], start=(k == 0),
                                             stop=(k == KD - 1))
                        last.then_inc(q_up, 1)
                        pe.wait_ge(sk_in[c], START + 16 * h + 16)
                        pe.wait_ge(k_out, START + 2 * h + c)
                        pe.transpose(banks[6][:, c * P:(c + 1) * P], sk[c][:, :], ident[:, :]).then_inc(k_up, 1)
                    if s < 3:
                        scores.turn(pe, i, s + 1)
                    for c in range(2):
                        pe.wait_ge(q_out, START + 2 * h + (c + 1))
                        pe.wait_ge(k_out, START + 2 * h + (c + 1))
                        pe.wait_ge(s_out, START + 2 * h + c)
                        for t in range(NT):
                            last = pe.matmul(banks[7][:, t * P:(t + 1) * P], q2[c][:, t * P:(t + 1) * P],
                                             skT[c][:, :], start=True, stop=True)
                        last.then_inc(s_up, 1)
                        if c == 0:
                            scores.product(pe, i, s)
            for j, src in enumerate((IS, JS, FV)):
                pe.wait_ge(less_up, START + 1)
                if j == 2:
                    pe.wait_ge(gate_up, START + 1)
                for t in range(NT):
                    last = pe.transpose(banks[4 + j][:, t * P:(t + 1) * P],
                                        src[:, t, :, :].rearrange("p h k -> p (h k)"), ident[:, :])
                last.then_inc(t_up, 1)
            pe.wait_ge(t_out, START + 3)
            with pe.Fori(HT, AHEAD) as i:
                scores.turn(pe, i, 0)
                for s in range(4):
                    for q in range(TB // 4):
                        g = (TB // 4) * (4 * (i - HT) + s) + q
                        pe.wait_ge(hot, START + g + 1)
                        pe.wait_ge(staged, START + (TB // 4) * (4 * (i - HT) + s) + (q - 3))
                        for k in range(4):
                            last = pe.matmul(banks[4 + q % 4][:, k * P:(k + 1) * P], OI[q % SLOTS][:, k, :],
                                             OJ[q % SLOTS][:, k, :], start=True, stop=True)
                        last.then_inc(spread, 1)
                        scores.product(pe, i, s, q)
                        if q == 3 and s < 3:
                            scores.turn(pe, i, s + 1)

        @block.scalar
        def _(act):
            with act.Fori(0, HT) as i:
                scores.evacuate(act, i, 0)
                for s in range(4):
                    h = 4 * i + s
                    for c in range(2):
                        act.wait_ge(q_up, START + 2 * h + (c + 1))
                        act.wait_ge(s_up, START + 2 * h)
                        act.activation(q2[c][:, :], banks[4 + c][:, :], ACT.Copy).then_inc(q_out, 1)
                        act.wait_ge(k_up, START + 2 * h + (c + 1))
                        act.activation(skT[c][:, :], banks[6][:, c * P:(c + 1) * P], ACT.Copy).then_inc(k_out, 1)
                    if s < 3:
                        scores.evacuate(act, i, s + 1)
                    for c in range(2):
                        act.wait_ge(s_up, START + 2 * h + (c + 1))
                        act.activation(SS[:, bass.ds(h, 1), c, :, :].rearrange("p o t n -> p (o t n)"),
                                       banks[7][:, :], ACT.Copy).then_inc(s_out, 1)
                    scores.gelu(act, i, s, bass.ds(4 * i + s, 1))
            act.wait_ge(less_up, START + 1)
            act.activation(FV[:, :, :, :], FV[:, :, :, :], ACT.Exp).then_inc(exp_up, 1)
            for j in range(3):
                act.wait_ge(t_up, START + j + 1)
                act.activation(turned[j][:, :], banks[4 + j][:, :], ACT.Copy).then_inc(t_out, 1)
            with act.Fori(HT, AHEAD) as i:
                scores.evacuate(act, i, 0)
                for s in range(4):
                    act.wait_ge(sent[s % 2], START + 16 * (2 * (i - HT) + s // 2))
                    for q in range(TB // 4):
                        act.wait_ge(spread, START + (TB // 4) * (4 * (i - HT) + s) + (q + 1))
                        act.activation(stage[s % 2][:, :, 4 * q:4 * q + 4],
                                       banks[4 + q % 4][:, :].rearrange("p (t j) -> p j t", t=4), ACT.Copy)\
                            .then_inc(staged, 1)
                        if q == 4 and s < 3:
                            scores.evacuate(act, i, s + 1)
                    scores.gelu(act, i, s, bass.ds(4 * i + s, 1))

        @block.vector
        def _(dve):
            per = 16
            chain = Tally(p_dve)
            dve.wait_ge(iota_up, START + 1)
            with dve.Fori(0, HEADS) as h:
                chain.enter(h, per)
                step = stepper(dve, chain)

                def settled(ins):
                    step(ins)
                    dve.tensor_copy(gatepost[:, :], iota16[:, 0:1])

                def best16(src, spare, vals, places, n):
                    for u in range(n):
                        last = dve.max(vals[:, u, 0:8], src[u])
                    settled(last)
                    for u in range(n):
                        last = dve.max_index(places[:, u, 0:8], vals[:, u, 0:8], src[u])
                    for u in range(n):
                        last = dve.match_replace(spare[u], vals[:, u, 0:8], src[u], -3.0e38)
                    settled(last)
                    for u in range(n):
                        last = dve.max(vals[:, u, 8:16], spare[u])
                    settled(last)
                    for u in range(n):
                        last = dve.max_index(places[:, u, 8:16], vals[:, u, 8:16], spare[u])
                    settled(last)
                dve.wait_ge(s_out, START + 2 * h + 2)
                settled(dve.tensor_copy(st[:, :, :], SS[:, bass.ds(h, 1), :, :, :]
                                        .rearrange("p o c t n -> p (o c t) n")))
                best16([st[:, u, :] for u in range(8)], [st2[:, u, :] for u in range(8)], sv, si, 8)
                dve.tensor_copy(sif[:, :, :], si[:, :, :])
                settled(dve.tensor_tensor(cand[:, :, :, :], sv[:, 0:4, :].unsqueeze(3).broadcast_to([P, NT, TOPK, TOPK]),
                                       sv[:, 4:8, :].unsqueeze(2).broadcast_to([P, NT, TOPK, TOPK]), ALU.add))
                flat = [[m[:, t, :, :].rearrange("p a b -> p (a b)") for t in range(NT)] for m in (cand, cand2)]
                best16(flat[0], flat[1], fv, fp, NT)
                dve.tensor_copy(FV[:, :, bass.ds(h, 1), :].rearrange("p t o k -> p t (o k)"), fv[:, :, :])
                fpf = fp[:, :, :].rearrange("p t k -> p (t k)")
                dve.tensor_scalar(fa[0][:, :], fpf, 4, None, ALU.logical_shift_right)
                step(dve.tensor_scalar(fa[1][:, :], fpf, 15, None, ALU.bitwise_and))
                dve.tensor_copy(ff[0][:, :], fa[0][:, :])
                step(dve.tensor_copy(ff[1][:, :], fa[1][:, :]))
                for c, work, dst in ((0, cand, IS), (1, cand2, JS)):
                    one = work[:, :, :, :].rearrange("p t k a -> p (t k) a")
                    last = dve.tensor_tensor(one, ff[c][:, :].unsqueeze(2).broadcast_to([P, NT * TOPK, TOPK]),
                                      iota16[:, :].unsqueeze(1).broadcast_to([P, NT * TOPK, TOPK]), ALU.is_equal)
                step(last)
                emit_pick(dve, step, cand, cand2, sif, IS, JS, h)
                assert chain.local == per, chain.local
                chain.leave(HEADS)
            soft = stepper(dve, Tally(p_soft))
            top = FV[:, :, :, :].rearrange("p t h k -> p (t h) k")
            heads = NT * HEADS
            soft(dve.tensor_copy(tot[:, :, :], FV[:, :, :, 0]))
            flat = tot[:, :, :].rearrange("p t h -> p (t h)")
            dve.tensor_tensor(top, top, flat.unsqueeze(2).broadcast_to([P, heads, TOPK]), ALU.subtract)\
                .then_inc(less_up, 1)
            dve.wait_ge(exp_up, START + 1)
            soft(dve.tensor_reduce(flat, top, AX.X, ALU.add))
            soft(dve.reciprocal(flat, flat))
            dve.tensor_tensor(top, top, flat.unsqueeze(2).broadcast_to([P, heads, TOPK]), ALU.mult)\
                .then_inc(gate_up, 1)
            dve.wait_ge(t_out, START + 3)
            with dve.Fori(0, T // (4 * SLOTS)) as g:
                for q in range(SLOTS):
                    dve.wait_ge(spread, START + SLOTS * g + (q - 3))
                    dve.tensor_tensor(OI[q], iota[:, :].unsqueeze(1).broadcast_to([P, 4, P]),
                                      turned[0][:, bass.ds(4 * SLOTS * g + 4 * q, 4)].unsqueeze(2)
                                      .broadcast_to([P, 4, P]), ALU.is_equal)
                    for k in range(4):
                        at = bass.ds(4 * SLOTS * g + 4 * q + k, 1)
                        last = dve.tensor_scalar(OJ[q][:, k, :], iota[:, :], turned[1][:, at],
                                                 turned[2][:, at], ALU.is_equal, ALU.mult)
                    last.then_inc(hot, 1)


def emit_pick(dve, step, cand, cand2, sif, IS, JS, h):
    step(dve.tensor_tensor(cand[:, :, :, :], cand[:, :, :, :],
                           sif[:, 0:4, :].unsqueeze(2).broadcast_to([P, NT, TOPK, TOPK]), ALU.mult))
    step(dve.tensor_tensor(cand2[:, :, :, :], cand2[:, :, :, :],
                           sif[:, 4:8, :].unsqueeze(2).broadcast_to([P, NT, TOPK, TOPK]), ALU.mult))
    for work, dst in ((cand, IS), (cand2, JS)):
        last = dve.tensor_reduce(dst[:, :, bass.ds(h, 1), :].rearrange("p t o k -> p t (o k)"),
                                 work[:, :, :, :], AX.X, ALU.add)
    step(last)


def emit_experts(nc, bank, banks, sem, v):
    peer_u, peer_v, ln2_g, ln2_b, ident, hh, hl, ring, gates, x1_kept, gt2, out = (
        v[n] for n in ("peer_u", "peer_v", "ln2_g", "ln2_b", "ident", "hh", "hl", "ring", "gates", "x1_kept", "gt2", "out"))
    acc = v["acc"]
    ctx = ExitStack()
    with ctx:
        def sb(name, shape, dt=F32):
            return ctx.enter_context(nc.sbuf_tensor(name, shape, dt))

        scores = ExpertScores(nc, sb, sem, "e_", banks, ident, hh, hl, ring, peer_u)
        vraw = [v["gt1"]] + [sb(f"vraw{s}", [P, D]) for s in range(1, 4)]
        vh = [sb(f"vh{q}", [P, 2, D], F32R) for q in range(2)]
        vl = [sb(f"vl{q}", [P, 2, D], F32R) for q in range(2)]
        gt = [sb(f"gtile{q}", [P, T // TB, 2, TB]) for q in range(2)]
        w = [sb(f"w{b}", [P, 2, P]) for b in range(2)]
        wh = [sb(f"wh{t}", [P, 2, P], F32R) for t in range(NT)]
        wl = [sb(f"wl{t}", [P, 2, P], F32R) for t in range(NT)]
        v_in = [sem(f"v_in{s}") for s in range(4)]
        g_in = [sem(f"g_in{q}") for q in range(2)]
        vh_up, vl_up, w_up, wh_up, wl_up, y_up, y_added, zeroed = (
            sem(n) for n in ("vh_up", "vl_up", "w_up", "wh_up", "wl_up", "y_up6", "y_added", "zeroed"))
        IT = NKEYS // 4
        MAIN = IT - AHEAD
        vsrc = peer_v[0].rearrange("(i j) d -> i j d", j=NKEYS)

        lg, lb = (ring[:, 2 * j:2 * j + 2, :].rearrange("p a b -> p (a b)") for j in range(2))
        norm = Norm(nc, sb, "n2_")
        ln_in, var_up, root_up, centred, gained, x2_up, p_dve, p_y = (
            sem(n) for n in ("ln_in6", "var_up6", "root_up6", "centred6", "gained6", "x2_up", "p_dve6", "p_y"))
        out_sent, x1_in = sem("out_sent"), [sem(f"x1_in{t}") for t in range(NT)]

        nc.all_engine_barrier()
        block = ctx.enter_context(nc.Block())

        def load_v(sp, s, turn):
            sp.dma_start(vraw[s][:, :], vsrc[:, bass.ds(4 * turn + s, 1), :].rearrange("i o d -> i (o d)"))\
                .then_inc(v_in[s], 16)

        def load_g(sp, q, turn):
            sp.dma_start(gt[q][:, :, :, :], gates[:, :, bass.ds(4 * turn + 2 * q, 2), :]).then_inc(g_in[q], 16)

        @block.sync
        def _(sp):
            for s in range(4):
                scores.load(sp, 0, s, 4 * AHEAD + s)
            for s in range(4):
                sp.dma_start(vraw[s][:, :], vsrc[:, s, :]).then_inc(v_in[s], 16)
            for q in range(2):
                sp.dma_start(gt[q][:, :, :, :], gates[:, :, 2 * q:2 * q + 2, :]).then_inc(g_in[q], 16)

            def loads(i, with_u):
                def u(s):
                    if with_u:
                        sp.wait_ge(scores.turned, START + 8 * i + 2 * s + 2)
                        scores.load(sp, i, s, bass.ds(4 * ((i + AHEAD + 1) % IT) + s, 1))
                for s in (0, 1):
                    sp.wait_ge(vl_up, START + 4 * i + (s + 1))
                    sp.wait_ge(vh_up, START + 4 * i + (s + 1))
                    load_v(sp, s, (i + 1) % IT)
                sp.wait_ge(wl_up, START + 8 * i + 4)
                sp.wait_ge(w_up, START + 8 * i + 4)
                load_g(sp, 0, (i + 1) % IT)
                u(0)
                for s in (2, 3):
                    sp.wait_ge(vl_up, START + 4 * i + (s + 1))
                    sp.wait_ge(vh_up, START + 4 * i + (s + 1))
                    load_v(sp, s, (i + 1) % IT)
                u(1)
                sp.wait_ge(w_up, START + 8 * i + 8)
                load_g(sp, 1, (i + 1) % IT)
                u(2)
                u(3)
            with sp.Fori(0, MAIN) as i:
                loads(i, True)
            with sp.Fori(MAIN, IT) as i:
                loads(i, False)
            for t in range(NT):
                sp.wait_ge(v_in[t], START + 16 * (IT + 1))
                sp.wait_ge(vl_up, START + 4 * IT + 2)
                sp.wait_ge(vh_up, START + 4 * IT + 2)
                sp.dma_start(vraw[t][:, :], x1_kept[t]).then_inc(x1_in[t], 16)
            sp.wait_ge(w_up, START + 8 * IT + 4)
            for dst, src in ((lg, ln2_g), (lb, ln2_b)):
                sp.dma_start(dst, src.rearrange("o n -> (o n)").partition_broadcast(P)).then_inc(ln_in, 16)
            for t in range(NT):
                sp.wait_ge(x2_up, START + t + 1)
                sp.dma_start(out[0, t * P:(t + 1) * P, :], acc[:, t, :]).then_inc(out_sent, 16)
            sp.wait_ge(out_sent, START + 16 * NT)
            for s in range(4):
                sp.wait_ge(v_in[s], START + 16 * (IT + 1))
                sp.wait_ge(scores.u_in[s], START + 16 * (MAIN + 1))
            for q in range(2):
                sp.wait_ge(g_in[q], START + 16 * (IT + 1))

        def v_ready(eng, i, q, ahead):
            for s in (2 * q, 2 * q + 1):
                eng.wait_ge(v_in[s], START + (16 * i + (32 if ahead else 16)))

        @block.gpsimd
        def _(pool):
            pool.memset(acc[:, :, :], 0.0).then_inc(zeroed, 1)

            def rest(i, q, n, done):
                v_ready(pool, i, q, ahead=(done is not None and q == 0))
                if done is not None:
                    pool.wait_ge(y_up, START + done)
                for k in range(2):
                    pool.wait_ge(vh_up, START + 2 * n + (k + 1))
                    pool.tensor_tensor(vl[q][:, k, :], vraw[2 * q + k][:, :], vh[q][:, k, :].bitcast(F32),
                                       ALU.subtract).then_inc(vl_up, 1)
            rest(0, 0, 0, None)

            def turn(i, with_u):
                if with_u:
                    scores.remainder(pool, i, 0)
                rest(i, 1, 2 * i + 1, 8 * i)
                if with_u:
                    scores.remainder(pool, i, 1)
                    scores.remainder(pool, i, 2)
                rest(i, 0, 2 * i + 2, 8 * i + 4)
                if with_u:
                    scores.remainder(pool, i, 3)
            with pool.Fori(0, MAIN) as i:
                turn(i, True)
            with pool.Fori(MAIN, IT) as i:
                turn(i, False)
            for t in range(NT):
                if t == 0:
                    pool.wait_ge(ln_in, START + 32)
                pool.wait_ge(centred, START + t + 1)
                pool.tensor_tensor(acc[:, t, :], acc[:, t, :], lg[:, :], ALU.mult).then_inc(gained, 1)

        @block.scalar
        def _(act):
            def rounded(i, q, done):
                v_ready(act, i, q, ahead=(done is not None and q == 0))
                if done is not None:
                    act.wait_ge(y_up, START + done)
                for k in range(2):
                    act.activation(vh[q][:, k, :], vraw[2 * q + k][:, :], ACT.Copy).then_inc(vh_up, 1)
            rounded(0, 0, None)

            def turn(i, with_u):
                def gelu(s):
                    if with_u:
                        act.wait_ge(w_up, START + 8 * i + (0, 0, 4, 4)[s] + 4)
                        scores.gelu(act, i, s, bass.ds(4 * (i % AHEAD) + s, 1))
                if with_u:
                    scores.evacuate(act, i, 0)
                rounded(i, 1, 8 * i)
                if with_u:
                    scores.evacuate(act, i, 1)
                    gelu(0)
                    scores.evacuate(act, i, 2)
                    gelu(1)
                rounded(i, 0, 8 * i + 4)
                if with_u:
                    scores.evacuate(act, i, 3)
                    gelu(2)
                    gelu(3)
            with act.Fori(0, MAIN) as i:
                turn(i, True)
            with act.Fori(MAIN, IT) as i:
                turn(i, False)
            for t in range(NT):
                act.wait_ge(var_up, START + t + 1)
                norm.root(act, t).then_inc(root_up, 1)

        @block.tensor
        def _(pe):
            def unit(i, q, t):
                u = 4 * q + t
                pe.wait_ge(wl_up, START + 8 * i + (u + 1))
                pe.wait_ge(wh_up, START + 8 * i + (u + 1))
                if t == 0:
                    pe.wait_ge(vl_up, START + 4 * i + (2 * q + 2))
                pe.wait_ge(y_added, START + 8 * i + (u - 1))
                for h in range(2):
                    b = banks[4 + 2 * (u % 2) + h]
                    half = slice(512 * h, 512 * h + 512)
                    for k in range(2):
                        pe.matmul(b[:, :], wh[t][:, k, :], vh[q][:, k, half], start=(k == 0), stop=False)
                        pe.matmul(b[:, :], wh[t][:, k, :], vl[q][:, k, half], start=False, stop=False)
                        last = pe.matmul(b[:, :], wl[t][:, k, :], vh[q][:, k, half], start=False, stop=(k == 1))
                last.then_inc(y_up, 1)

            def turn(i, with_u):
                for s in range(4):
                    if with_u:
                        scores.turn(pe, i, s)
                    unit(i, s // 2, 2 * (s % 2))
                    unit(i, s // 2, 2 * (s % 2) + 1)
                    if with_u:
                        scores.product(pe, i, s)
            with pe.Fori(0, MAIN) as i:
                turn(i, True)
            with pe.Fori(MAIN, IT) as i:
                turn(i, False)

        @block.vector
        def _(dve):
            def gated(n, i, q, t, slot, turn_of_gates):
                if t == 0:
                    dve.wait_ge(g_in[q], START + 16 * turn_of_gates + 16)
                dve.tensor_tensor(w[t % 2][:, :, :].rearrange("p j (b t) -> p j b t", b=P // TB),
                                  ring[:, slot, t * P:(t + 1) * P].rearrange("p j (b t) -> p j b t", b=P // TB),
                                  gt[q][:, (P // TB) * t:(P // TB) * (t + 1), :, :].rearrange("p b j t -> p j b t"), ALU.mult)\
                    .then_inc(w_up, 1)
                dve.wait_ge(w_up, START + n + (t + 1))
                dve.tensor_copy(wh[t][:, :, :], w[t % 2][:, :, :]).then_inc(wh_up, 1)
                dve.wait_ge(wh_up, START + n + (t + 1))
                dve.tensor_tensor(wl[t][:, :, :], w[t % 2][:, :, :], wh[t][:, :, :].bitcast(F32), ALU.subtract)\
                    .then_inc(wl_up, 1)

            dve.wait_ge(zeroed, START + 1)
            for t in range(NT):
                gated(0, 0, 0, t, slice(0, 2), 0)

            def turn(i):
                for q in range(2):
                    for t in range(NT):
                        u = 4 * q + t
                        dve.wait_ge(y_up, START + 8 * i + (u + 1))
                        b = bank[:, 512 * (4 + 2 * (u % 2)):512 * (6 + 2 * (u % 2))]
                        dve.wait_ge(y_added, START + 8 * i + (u - 3))
                        dve.tensor_tensor(acc[:, t, :], acc[:, t, :], b, ALU.add).then_inc(y_added, 1)
                        if q == 0:
                            gated(8 * i + 4, i, 1, t, bass.ds(4 * (i % AHEAD) + 2, 2), i)
                        else:
                            gated(8 * i + 8, i, 0, t, bass.ds(4 * ((i + 1) % AHEAD), 2), i + 1)
            with dve.Fori(0, MAIN) as i:
                turn(i)
            with dve.Fori(MAIN, IT) as i:
                turn(i)
            step = stepper(dve, Tally(p_dve))
            dve.wait_ge(y_added, START + 8 * IT)
            for t in range(NT):
                step(dve.tensor_tensor(acc[:, t, :], acc[:, t, :], gt2[:, :], ALU.mult))
                dve.wait_ge(x1_in[t], START + 16)
                step(dve.scalar_tensor_tensor(out=acc[:, t, :], in0=vraw[t][:, :], scalar=ALPHA, in1=acc[:, t, :],
                                              op0=ALU.mult, op1=ALU.add))
                norm.moments(dve, step, t, acc[:, t, :]).then_inc(var_up, 1)
                dve.wait_ge(root_up, START + t + 1)
                norm.scaled(dve, step, t, acc[:, t, :]).then_inc(centred, 1)
                dve.wait_ge(gained, START + t + 1)
                dve.tensor_tensor(acc[:, t, :], acc[:, t, :], lb[:, :], ALU.add).then_inc(x2_up, 1)


_INS = ["x", "c", "ada_w", "ada_b", "w_in", "attn_sink", "shift_mu", "decay_w0", "decay_w2", "iclr_a0", "iclr_a2",
        "gate_g2", "k_k", "k_a", "r_k", "lnx_g", "lnx_b", "w_out", "ln1_g", "ln1_b", "peer_wq", "peer_subkeys",
        "peer_u", "peer_v", "ln2_g", "ln2_b"]


def kernel(**inputs):
    import numpy as np
    import concourse.bacc as bacc
    from concourse.bass_utils import run_bass_kernel_spmd

    nc = bacc.Bacc("TRN2", target_bir_lowering=False, num_devices=1)
    arrays, args = {}, []
    for name in _INS:
        a = np.ascontiguousarray(inputs[name])
        arrays["in_" + name] = a
        args.append(nc.dram_tensor("in_" + name, a.shape, mybir.dt.from_np(a.dtype), kind="ExternalInput").ap())
    args.append(nc.dram_tensor("out_x", (1, T, D), F32, kind="ExternalOutput").ap())
    hybrid_layer(nc, *args)
    r = run_bass_kernel_spmd(nc, [arrays], core_ids=[0])
    return r.results[0]["out_x"]
```

```python
import concourse.bass as bass
from concourse import mybir
from contextlib import ExitStack
import math

D = 1024
T = 512
P = 128
KD = D // P
NT = T // P
HD = 64
HEADS = 8
PAIRS = HEADS // 2
ATTN_COLS = 768
RW_TILES = 14
CH = 64
NKEYS = 128
TOPK = 16
AHEAD = 6
START = 8
LN_EPS = 1e-5
GN_EPS = 64e-5
ALPHA = 2.0 ** 0.25
KAPPA = math.exp(-0.5)
NEG = -1.0e30

F32 = mybir.dt.float32
F32R = mybir.dt.float32r
U32 = mybir.dt.uint32
ALU = mybir.AluOpType
ACT = mybir.ActivationFunctionType
AX = mybir.AxisListType

R_C, R_ADAB, R_MU, R_W0, R_A0, R_KK, R_KA, R_RK, R_LXG, R_LXB = 0, 8, 56, 70, 74, 78, 82, 86, 90, 94
N_ROWS = 98


class Tally:

    def __init__(self, sem):
        self.sem, self.base, self.local, self.loop = sem, START, 0, None

    def value(self):
        turns = 0 if self.loop is None else self.loop[0] * self.loop[1]
        return turns + (self.base + self.local)

    def inc(self, ins):
        ins.then_inc(self.sem, 1)
        self.local += 1
        return ins

    def enter(self, i, per):
        self.base, self.local, self.loop = self.base + self.local, 0, (i, per)

    def leave(self, turns):
        assert self.local == self.loop[1], (self.local, self.loop[1])
        self.base, self.local, self.loop = self.base + turns * self.local, 0, None


def stepper(eng, tally):
    def step(ins):
        tally.inc(ins)
        eng.wait_ge(tally.sem, tally.value())
    return step


def hybrid_layer(nc, x, c, ada_w, ada_b, w_in, attn_sink, shift_mu, decay_w0, decay_w2, iclr_a0, iclr_a2,
                 gate_g2, k_k, k_a, r_k, lnx_g, lnx_b, w_out, ln1_g, ln1_b, peer_wq, peer_subkeys,
                 peer_u, peer_v, ln2_g, ln2_b, out):
    ctx = ExitStack()
    with ctx:
        held, phase = [], [1]
        starters = (nc.sync, nc.scalar, nc.vector, nc.gpsimd, nc.tensor)

        def sem(name):
            held.append(nc.alloc_semaphore(f"{name}_{phase[0]}"))
            starters[len(held) % len(starters)].sem_inc(held[-1], START)
            return held[-1]

        def fresh():
            nc.clear_and_free_semaphores(held)
            nc.all_engine_barrier()
            held.clear()
            phase[0] += 1

        def keep(name, shape, dt=F32):
            return ctx.enter_context(nc.sbuf_tensor(name, shape, dt))

        bank = ctx.enter_context(nc.psum_tensor("bank", [P, 8 * 512], F32))
        banks = [bank[:, 512 * i:512 * i + 512] for i in range(8)]

        ident = keep("ident", [P, P])
        par = keep("par", [P, N_ROWS])
        mod = keep("mod", [P, 32])
        gt2 = keep("gt2", [P, D])
        wide = keep("wide", [P, KD, T])

        gt1 = keep("gt1", [P, D])

        x1_kept = nc.dram_tensor("x1_kept", [NT, P, D], F32, kind="Internal").ap()
        gates = nc.dram_tensor("gates", [P, T // TB, NKEYS, TB], F32, kind="Internal").ap()
        mix = ExitStack()
        mix.__enter__()

        def mk(name, shape, dt=F32):
            return mix.enter_context(nc.sbuf_tensor(name, shape, dt))

        diag2 = mk("diag2", [P, P])
        qT = mk("qT", [P, 4, T])
        kT = mk("kT", [P, 2, P + T])
        vtok = mk("vtok", [P, 1 + NT, P])
        PM = mk("PM", [P, RW_TILES, T])
        yT = wide
        SW = yT[:, 0:4, :]
        CS = yT[:, 4:8, :]
        AI = mk("AI", [P, PAIRS, T])
        GG = mk("GG", [P, PAIRS, T])
        KN = mk("KN", [P, PAIRS, T])
        BO = mk("BO", [P, PAIRS, T])
        PL = mk("PL", [P, PAIRS, T // CH])

        emit_projections(nc, banks, sem, locals())
        fresh()
        emit_mixing(nc, banks, sem, locals())
        fresh()
        mix.close()

        hh = keep("hh", [P, KD, T], F32R)
        hl = keep("hl", [P, KD, T], F32R)
        ring = keep("ring", [P, 4 * AHEAD, T])
        urows = [keep(f"urows{s}", [P, D]) for s in range(4)]
        h2 = wide
        asked = ExitStack()
        wq = [asked.enter_context(nc.sbuf_tensor(f"wq{c}", [P, KD, P], F32)) for c in range(2)]
        sk = [asked.enter_context(nc.sbuf_tensor(f"sk{c}", [P, P], F32)) for c in range(2)]
        emit_mix_out(nc, banks, sem, locals())
        fresh()
        emit_routing(nc, banks, sem, locals())
        asked.close()
        fresh()
        acc = wide[:, :, :].rearrange("p (t h) d -> p t (h d)", t=NT)
        emit_experts(nc, bank, banks, sem, locals())


def emit_projections(nc, banks, sem, v):
    (x, c, ada_w, ada_b, w_in, shift_mu, decay_w0, decay_w2, iclr_a0, iclr_a2, gate_g2, k_k, k_a, r_k, lnx_g,
     lnx_b) = (v[n] for n in ("x", "c", "ada_w", "ada_b", "w_in", "shift_mu", "decay_w0", "decay_w2", "iclr_a0",
                              "iclr_a2", "gate_g2", "k_k", "k_a", "r_k", "lnx_g", "lnx_b"))
    (ident, par, mod, gt1, gt2, diag2, qT, kT, vtok, PM, SW, CS, AI, GG, KN, BO, PL) = (
        v[n] for n in ("ident", "par", "mod", "gt1", "gt2", "diag2", "qT", "kT", "vtok", "PM", "SW", "CS", "AI",
                       "GG", "KN", "BO", "PL"))
    ctx = ExitStack()
    with ctx:
        def sb(name, shape, dt=F32):
            return ctx.enter_context(nc.sbuf_tensor(name, shape, dt))

        rows = sb("rows", [P, P])
        csT = sb("csT", [P, KD])
        csw = sb("csw", [P, KD, P])
        ones = sb("ones", [P, 1])
        omu = sb("omu", [P, RW_TILES])
        xin = [sb(f"xin{i}", [P, D]) for i in range(2)]
        hT = sb("hT", [P, KD, T])
        ada = [sb(f"ada{i}", [P, KD, 512]) for i in range(2)]
        wt = [sb(f"wt{i}", [P, KD, P]) for i in range(2)]
        w2a2 = sb("w2a2", [P, 512])
        g2 = sb("g2", [P, 512])
        PD = sb("PD", [P, PAIRS, T])
        asum = [sb(f"asum{i}", [P, 512]) for i in range(2)]
        keepm = sb("keepm", [P, T])
        tmp = [sb(f"tmp{i}", [P, T]) for i in range(4)]

        rows_in, lora_in = sem("rows_in"), sem("lora_in")
        x_in = [sem(f"x_in{i}") for i in range(2)]
        ada_in = [sem(f"ada_in{i}") for i in range(2)]
        wt_in = [sem(f"wt_in{i}") for i in range(2)]
        gb_in = sem("gb_in")
        consts, rows_up, par_up, silu_up = sem("consts"), sem("rows_up"), sem("par_up"), sem("silu_up")
        cs_up = sem("cs_up")
        xt_up, xt_used = sem("xt_up"), sem("xt_used")
        cols_up, cols_used = sem("cols_up"), sem("cols_used")
        ada_summed, ada_used, gates_up, h_up = sem("ada_summed"), sem("ada_used"), sem("gates_up"), sem("h_up")
        proj_up, proj_scaled, proj_mixed = sem("proj_up"), sem("proj_scaled"), sem("proj_mixed")
        lora_act, z_up, z_used = sem("lora_act"), sem("z_up"), sem("z_used")
        p_dve, p_act, p_pool, p_sum = sem("p_dve"), sem("p_act"), sem("p_pool"), sem("p_sum")
        gate_up, gate_used = sem("gate_up"), sem("gate_used")
        sq_up, ss_up, ss_max, ss_root = sem("sq_up"), sem("ss_up"), sem("ss_max"), sem("ss_root")
        kp_up, rk_up, rks_up, bsum_up, bo_up = sem("kp_up"), sem("rk_up"), sem("rks_up"), sem("bsum_up"), sem("bo_up")
        cs_scan, csm_up, exp_up, nk_up = sem("cs_scan"), sem("csm_up"), sem("exp_up"), sem("nk_up")

        wv = w_in.rearrange("o (k p) n -> p (o k) n", p=P)
        av = ada_w.rearrange("o (k p) n -> p (o k) n", p=P)
        xv = x.rearrange("o (t p) d -> p (o t) d", p=P)

        def ada_piece(m, half):
            return av[:, :, m * D + half * 512:m * D + half * 512 + 512]

        pieces = [(m, half) for m in (0, 1, 3, 4, 2, 5) for half in (0, 1)]

        nc.all_engine_barrier()
        block = ctx.enter_context(nc.Block())

        @block.sync
        def _(sp):
            for name, src, n in (("c", c, 8), ("ada_b", ada_b, 48), ("mu", shift_mu, 14), ("w0", decay_w0, 4),
                                 ("a0", iclr_a0, 4), ("kk", k_k, 4), ("ka", k_a, 4), ("rk", r_k, 4),
                                 ("lxg", lnx_g, 4), ("lxb", lnx_b, 4)):
                at = {"c": R_C, "ada_b": R_ADAB, "mu": R_MU, "w0": R_W0, "a0": R_A0, "kk": R_KK, "ka": R_KA,
                      "rk": R_RK, "lxg": R_LXG, "lxb": R_LXB}[name]
                flat = src.rearrange("o h d -> (o h d)") if name == "rk" else src.rearrange("o n -> (o n)")
                sp.dma_start(rows[at:at + n, :], flat.rearrange("(n p) -> n p", p=P)).then_inc(rows_in, 16)
            for t in range(NT):
                if t >= 2:
                    sp.wait_ge(xt_up, START + 2 * (t - 1))
                sp.dma_start(xin[t % 2][:, :], xv[:, t, :]).then_inc(x_in[t % 2], 16)
            for n in range(4):
                if n >= 2:
                    sp.wait_ge(ada_summed, START + n - 1)
                sp.dma_start(ada[n % 2][:, :, :], ada_piece(*pieces[n])).then_inc(ada_in[n % 2], 16)
            sp.dma_start(w2a2[0:64, :], decay_w2[0, :, :]).then_inc(lora_in, 16)
            sp.dma_start(w2a2[64:128, :], iclr_a2[0, :, :]).then_inc(lora_in, 16)
            sp.dma_start(g2[:, :], gate_g2[0, :, :]).then_inc(lora_in, 16)
            for n in range(2):
                sp.dma_start(wt[n][:, :, :], wv[:, :, ATTN_COLS + (12 + n) * P:ATTN_COLS + (13 + n) * P])\
                    .then_inc(wt_in[n], 16)
            flat = ada_b.rearrange("o n -> (o n)")
            for dst, m in ((gt1, 2), (gt2, 5)):
                sp.dma_start(dst[:, :], flat[m * D:(m + 1) * D].partition_broadcast(P)).then_inc(gb_in, 16)

            def weights(i, n):
                sp.wait_ge(proj_up, START + 2 * i + (n + 1))
                sp.dma_start(wt[n][:, :, :], wv[:, :, bass.ds((i * 2 + n) * P + ATTN_COLS, P)])\
                    .then_inc(wt_in[n], 16)

            def ada_load(n):
                sp.wait_ge(ada_summed, START + n - 1)
                sp.dma_start(ada[n % 2][:, :, :], ada_piece(*pieces[n])).then_inc(ada_in[n % 2], 16)
            ada_load(4)
            ada_load(5)
            with sp.Fori(0, 2) as i:
                for n in range(2):
                    weights(i, n)
            for n in range(2):
                weights(2, n)
                ada_load(6 + n)
            with sp.Fori(3, 6) as i:
                for n in range(2):
                    weights(i, n)
            with sp.Fori(0, 2) as i:
                for n in range(2):
                    sp.wait_ge(proj_up, START + 2 * i + (13 + n))
                    sp.dma_start(wt[n][:, :, :], wv[:, :, bass.ds((i * 2 + n) * P, P)]).then_inc(wt_in[n], 16)
            for n in range(2):
                sp.wait_ge(proj_up, START + 17 + n)
                for d in range(2):
                    sp.dma_start(wt[n][:, :, 64 * d:64 * d + 64], wv[:, :, 512 + 64 * n:576 + 64 * n])\
                        .then_inc(wt_in[n], 16)
            sp.wait_ge(proj_up, START + 19)
            sp.dma_start(wt[0][:, :, :], wv[:, :, 640:768]).then_inc(wt_in[0], 16)
            ada_load(8)
            ada_load(9)
            for n in range(10, 12):
                sp.wait_ge(gates_up, START + n - 9)
                sp.dma_start(ada[n % 2][:, :, :], ada_piece(*pieces[n])).then_inc(ada_in[n % 2], 16)
            sp.wait_ge(gb_in, START + 32)

        @block.gpsimd
        def _(pool):
            step = stepper(pool, Tally(p_pool))
            step(pool.memset(ident[:, :], 0.0))
            pool.affine_select(out=ident[:, :], in_=ident[:, :], compare_op=ALU.not_equal, fill=1.0, base=0,
                               pattern=[[-1, P]], channel_multiplier=1).then_inc(consts, 1)
            step(pool.memset(diag2[:, :], 1.0))
            d2 = diag2[:, :].rearrange("p (b w) -> p b w", b=2)
            step(pool.affine_select(out=d2, in_=d2, compare_op=ALU.is_ge, fill=0.0, base=0,
                                    pattern=[[-CH, 2], [0, CH]], channel_multiplier=1))
            pool.affine_select(out=d2, in_=d2, compare_op=ALU.is_ge, fill=0.0, base=CH - 1,
                               pattern=[[CH, 2], [0, CH]], channel_multiplier=-1).then_inc(consts, 1)
            step(pool.memset(keepm[:, :], 1.0))
            pool.memset(keepm[:, ::CH], 0.0).then_inc(consts, 1)
            pool.memset(kT[:, :, 0:P], 0.0).then_inc(consts, 1)
            pool.memset(vtok[:, 0, :], 0.0).then_inc(consts, 1)
            pool.memset(ones[:, :], 1.0).then_inc(consts, 1)

            for p in range(PAIRS):
                pool.wait_ge(kp_up, START + p + 1)
                if p >= 2:
                    pool.wait_ge(ss_up, START + p - 1)
                pool.tensor_tensor(tmp[p % 2][:, :], KN[:, p, :], KN[:, p, :], ALU.mult).then_inc(sq_up, 1)
            for p in range(PAIRS):
                pool.wait_ge(cs_scan, START + p + 1)
                pool.tensor_tensor(SW[:, p, :], CS[:, p, :], SW[:, p, :], ALU.subtract).then_inc(csm_up, 1)
            for p in range(PAIRS):
                pool.wait_ge(kp_up, START + PAIRS + p + 1)
                if p >= 2:
                    pool.wait_ge(bsum_up, START + p - 1)
                pool.tensor_tensor(tmp[2 + p % 2][:, :], PM[:, p, :], PM[:, 4 + p, :], ALU.mult).then_inc(rk_up, 1)
            for p in range(PAIRS):
                pool.wait_ge(exp_up, START + 3 * PAIRS)
                pool.wait_ge(nk_up, START + 2 * p + 2)
                pool.tensor_tensor(AI[:, p, :], AI[:, p, :], CS[:, p, :], ALU.mult).then_inc(p_pool, 1)
            for p in range(PAIRS):
                pool.wait_ge(rk_up, START + p + 1)
                pool.tensor_tensor(PM[:, 4 + p, :], PM[:, 4 + p, :], CS[:, p, :], ALU.mult).then_inc(p_pool, 1)

        @block.scalar
        def _(act):
            act.wait_ge(rows_up, START + 1)
            act.activation(par[:, :], banks[7][:, 0:N_ROWS], ACT.Copy).then_inc(par_up, 1)
            act.wait_ge(par_up, START + 1)
            act.activation(csT[:, :], par[:, R_C:R_C + KD], ACT.Sigmoid).then_inc(silu_up, 1)
            for t in range(NT):
                for h in range(2):
                    act.wait_ge(xt_up, START + 2 * t + h + 1)
                    act.activation(hT[:, 4 * h:4 * h + 4, t * P:(t + 1) * P],
                                   banks[2 + (2 * t + h) % 4][:, :].rearrange("p (k t) -> p k t", k=4), ACT.Copy)\
                        .then_inc(xt_used, 1)
            act.wait_ge(silu_up, START + 3)
            for n in range(2):
                act.wait_ge(proj_up, START + n + 1)
                act.activation(PM[:, 12 + n, :], banks[n][:, :], ACT.Copy, scale=omu[:, 12 + n:13 + n])\
                    .then_inc(proj_scaled, 1)
            act.wait_ge(proj_mixed, START + 2)
            act.activation(PM[0:64, 12, :], PM[0:64, 12, :], ACT.Tanh).then_inc(lora_act, 1)
            act.activation(PM[:, 13, :], PM[:, 13, :], ACT.Sigmoid).then_inc(lora_act, 1)
            for p in range(PAIRS):
                for j, (dst, row) in enumerate(((SW, R_W0), (AI, R_A0), (GG, None))):
                    n = 3 * p + j
                    act.wait_ge(z_up, START + n + 1)
                    src = banks[2 + n % 2][:, :]
                    if row is None:
                        act.activation(dst[:, p, :], src, ACT.Copy).then_inc(z_used, 1)
                    else:
                        act.activation(dst[:, p, :], src, ACT.Sigmoid, bias=par[:, row + p:row + p + 1])\
                            .then_inc(z_used, 1)
            with act.Fori(0, 6) as i:
                for n in range(2):
                    act.wait_ge(proj_up, START + 2 * i + (3 + n))
                    act.activation(PM[:, bass.ds(2 * i + n, 1), :].rearrange("p o t -> p (o t)"), banks[n][:, :],
                                   ACT.Copy, scale=omu[:, bass.ds(2 * i + n, 1)]).then_inc(proj_scaled, 1)
            with act.Fori(0, 2) as i:
                for n in range(2):
                    act.wait_ge(proj_up, START + 2 * i + (15 + n))
                    act.activation(qT[:, bass.ds(2 * i + n, 1), :].rearrange("p o t -> p (o t)"), banks[n][:, :],
                                   ACT.Copy, scale=HD ** -0.5).then_inc(proj_scaled, 1)
            for p in range(PAIRS):
                act.wait_ge(ss_max, START + p + 1)
                act.activation(PD[:, p, :], PD[:, p, :], ACT.Sqrt).then_inc(ss_root, 1)
            for n in range(2):
                act.wait_ge(proj_up, START + 19 + n)
                act.activation(kT[:, n, P:], banks[n][:, :], ACT.Copy).then_inc(proj_scaled, 1)
            act.wait_ge(proj_up, START + 21)
            act.activation(vtok[:, 1:, :], banks[0][:, :].rearrange("p (t n) -> p t n", t=NT), ACT.Copy)\
                .then_inc(proj_scaled, 1)
            act.wait_ge(cs_scan, START + PAIRS)
            act.wait_ge(csm_up, START + PAIRS)
            act.activation(SW[:, :, :], SW[:, :, :], ACT.Exp, scale=-KAPPA).then_inc(exp_up, PAIRS)
            act.wait_ge(nk_up, START + 2 * PAIRS)
            act.activation(PD[:, :, :], CS[:, :, :], ACT.Exp, scale=-KAPPA).then_inc(exp_up, PAIRS)
            act.wait_ge(exp_up, START + 2 * PAIRS)
            act.activation(CS[:, :, :], CS[:, :, :], ACT.Exp, scale=KAPPA).then_inc(exp_up, PAIRS)

        @block.tensor
        def _(pe):
            pe.wait_ge(rows_in, START + 160)
            pe.wait_ge(consts, START + 1)
            pe.transpose(banks[7][:, 0:N_ROWS], rows[0:N_ROWS, :], ident[0:N_ROWS, 0:N_ROWS]).then_inc(rows_up, 1)
            for t in range(NT):
                pe.wait_ge(x_in[t % 2], START + 16 * (t // 2 + 1))
                for h in range(2):
                    n = 2 * t + h
                    if n >= 4:
                        pe.wait_ge(xt_used, START + n - 3)
                    for k in range(4):
                        last = pe.transpose(banks[2 + n % 4][:, k * P:(k + 1) * P],
                                            xin[t % 2][:, (4 * h + k) * P:(4 * h + k + 1) * P], ident[:, :])
                    last.then_inc(xt_up, 1)
            pe.wait_ge(silu_up, START + 2)
            def columns(i, n):
                pe.wait_ge(ada_summed, START + 2 * i + (n + 1))
                for j in range(4):
                    last = pe.matmul(banks[6][:, bass.ds(8 * i + (4 * n + j), 1)], asum[n][:, j * P:(j + 1) * P],
                                     ones[:, :], start=True, stop=True)
                last.then_inc(ada_used, 1)
            pe.wait_ge(consts, START + 6)
            with pe.Fori(0, 2) as i:
                for n in range(2):
                    columns(i, n)
            pe.wait_ge(h_up, START + KD)
            def project(slot, w):
                for k in range(KD):
                    last = pe.matmul(banks[slot][:, :], wt[slot][:, k, :], hT[:, k, :], start=(k == 0),
                                     stop=(k == KD - 1))
                last.then_inc(proj_up, 1)
            for n in range(2):
                pe.wait_ge(wt_in[n], START + 16)
                project(n, n)
            pe.wait_ge(lora_in, START + 48)
            pe.wait_ge(lora_act, START + 2)
            for p in range(PAIRS):
                for j in range(3):
                    n = 3 * p + j
                    if n >= 2:
                        pe.wait_ge(z_used, START + n - 1)
                    cols = slice(p * P, (p + 1) * P)
                    w, r = ((w2a2[0:64, cols], PM[0:64, 12, :]), (w2a2[64:128, cols], PM[64:128, 12, :]),
                            (g2[:, cols], PM[:, 13, :]))[j]
                    pe.matmul(banks[2 + n % 2][:, :], w, r, start=True, stop=True).then_inc(z_up, 1)
            def rwkv_tile(i, n):
                pe.wait_ge(wt_in[n], START + 16 * i + 32)
                pe.wait_ge(proj_mixed, START + 2 * i + (n + 1))
                project(n, None)
            with pe.Fori(0, 2) as i:
                for n in range(2):
                    rwkv_tile(i, n)
            with pe.Fori(2, 4) as i:
                for n in range(2):
                    rwkv_tile(i, n)
                    columns(i, n)
            with pe.Fori(4, 6) as i:
                for n in range(2):
                    rwkv_tile(i, n)
            with pe.Fori(0, 2) as i:
                for n in range(2):
                    pe.wait_ge(wt_in[n], START + 16 * i + 128)
                    pe.wait_ge(proj_scaled, START + 2 * i + (13 + n))
                    pe.wait_ge(proj_mixed, START + 14)
                    project(n, None)
            for p in range(PAIRS):
                if p == 0:
                    pe.wait_ge(consts, START + 5)
                pe.wait_ge(sq_up, START + p + 1)
                if p >= 2:
                    pe.wait_ge(ss_max, START + p - 1)
                pe.matmul(banks[4 + p % 2][:, :], diag2[:, :], tmp[p % 2][:, :], start=True, stop=True)\
                    .then_inc(ss_up, 1)

            def bonus(p):
                pe.wait_ge(rks_up, START + p + 1)
                pe.wait_ge(ss_max, START + PAIRS)
                if p >= 2:
                    pe.wait_ge(bo_up, START + p - 1)
                pe.matmul(banks[4 + p % 2][:, :], diag2[:, :], tmp[2 + p % 2][:, :], start=True, stop=True)\
                    .then_inc(bsum_up, 1)
            for n in range(2):
                pe.wait_ge(wt_in[n], START + 16 * 9 + 32)
                pe.wait_ge(proj_scaled, START + 17 + n)
                project(n, None)
                bonus(n)
            pe.wait_ge(wt_in[0], START + 16 * 9 + 48)
            pe.wait_ge(proj_scaled, START + 19)
            for t in range(NT):
                for k in range(KD):
                    last = pe.matmul(banks[0][:, t * P:(t + 1) * P], hT[:, k, t * P:(t + 1) * P], wt[0][:, k, :],
                                     start=(k == 0), stop=(k == KD - 1))
            last.then_inc(proj_up, 1)

            def gate(n, bank):
                pe.wait_ge(ada_in[n % 2], START + 16 * (n // 2 + 1))
                for k in range(KD):
                    last = pe.matmul(banks[bank][:, :], csw[:, k, :], ada[n % 2][:, k, :], start=(k == 0),
                                     stop=(k == KD - 1))
                last.then_inc(gates_up, 1)
            pe.wait_ge(z_used, START + 12)
            gate(8, 2)
            bonus(2)
            bonus(3)
            gate(9, 3)
            pe.wait_ge(proj_scaled, START + 21)
            gate(10, 0)
            gate(11, 1)

        @block.vector
        def _(dve):
            tally = Tally(p_dve)
            step = stepper(dve, tally)
            dve.wait_ge(par_up, START + 1)
            dve.wait_ge(silu_up, START + 1)
            dve.tensor_tensor(csT[:, :], csT[:, :], par[:, R_C:R_C + KD], ALU.mult).then_inc(silu_up, 1)
            dve.tensor_scalar(omu[:, :], par[:, R_MU:R_MU + RW_TILES], -1.0, 1.0, ALU.mult, ALU.add)\
                .then_inc(silu_up, 1)
            dve.wait_ge(silu_up, START + 3)
            step(dve.tensor_copy(csw[:, :, :], csT[:, :].unsqueeze(2).broadcast_to([P, KD, P])))

            def summed(i, n, marks):
                dve.wait_ge(ada_in[n], START + 16 * i + 16)
                dve.wait_ge(ada_used, START + 2 * i + (n - 1))
                for k in range(KD):
                    if k == 0:
                        ins = dve.tensor_scalar(asum[n][:, :], ada[n][:, k, :], csT[:, k:k + 1], None, ALU.mult)
                    else:
                        ins = dve.scalar_tensor_tensor(out=asum[n][:, :], in0=ada[n][:, k, :],
                                                       scalar=csT[:, k:k + 1], in1=asum[n][:, :],
                                                       op0=ALU.mult, op1=ALU.add)
                    if k < KD - 1:
                        marks(ins)
                    else:
                        ins.then_inc(ada_summed, 1)
            marks = Tally(p_sum)
            with dve.Fori(0, 2) as i:
                marks.enter(i, 2 * (KD - 1))
                for n in range(2):
                    summed(i, n, stepper(dve, marks))
                marks.leave(2)
            dve.wait_ge(ada_used, START + 4)
            dve.tensor_tensor(mod[:, 0:16], banks[6][:, 0:16], par[:, R_ADAB:R_ADAB + 16], ALU.add)\
                .then_inc(cols_used, 1)
            dve.wait_ge(cols_used, START + 1)
            step(dve.tensor_scalar(mod[:, 8:16], mod[:, 8:16], 1.0, None, ALU.add))
            dve.wait_ge(xt_used, START + 8)
            for k in range(KD):
                dve.tensor_scalar(hT[:, k, :], hT[:, k, :], mod[:, 8 + k:9 + k], mod[:, k:k + 1],
                                  ALU.mult, ALU.add).then_inc(h_up, 1)
            for n in range(2):
                dve.wait_ge(proj_scaled, START + n + 1)
                dve.scalar_tensor_tensor(out=PM[:, 12 + n, 1:], in0=banks[n][:, 0:T - 1],
                                         scalar=par[:, R_MU + 12 + n:R_MU + 13 + n], in1=PM[:, 12 + n, 1:],
                                         op0=ALU.mult, op1=ALU.add).then_inc(proj_mixed, 1)
            def mixed(i, n):
                dve.wait_ge(proj_scaled, START + 2 * i + (3 + n))
                pm = PM[:, bass.ds(2 * i + n, 1), 1:].rearrange("p o t -> p (o t)")
                dve.scalar_tensor_tensor(out=pm, in0=banks[n][:, 0:T - 1],
                                         scalar=par[:, bass.ds(2 * i + (R_MU + n), 1)], in1=pm,
                                         op0=ALU.mult, op1=ALU.add).then_inc(proj_mixed, 1)
            for n in range(2):
                mixed(0, n)
            with dve.Fori(1, 3) as i:
                marks.enter(i - 1, 2 * (KD - 1))
                for n in range(2):
                    mixed(i, n)
                    summed(i + 1, n, stepper(dve, marks))
                marks.leave(2)
            with dve.Fori(3, 6) as i:
                for n in range(2):
                    mixed(i, n)
            dve.wait_ge(consts, START + 5)
            dve.wait_ge(z_used, START + 12)
            dve.wait_ge(proj_mixed, START + 14)
            for p in range(PAIRS):
                dve.tensor_scalar(KN[:, p, :], PM[:, 4 + p, :], par[:, R_KK + p:R_KK + p + 1], None, ALU.mult)\
                    .then_inc(kp_up, 1)
            for p in range(PAIRS):
                dve.tensor_tensor_scan(out=CS[:, p, :], data0=keepm[:, :], data1=SW[:, p, :], initial=0.0,
                                       op0=ALU.mult, op1=ALU.add).then_inc(cs_scan, 1)
            for p in range(PAIRS):
                step(dve.tensor_scalar(BO[:, p, :], AI[:, p, :], -1.0, par[:, R_KA + p:R_KA + p + 1], ALU.add,
                                       ALU.mult))
                dve.scalar_tensor_tensor(out=PM[:, 4 + p, :], in0=BO[:, p, :], scalar=1.0, in1=PM[:, 4 + p, :],
                                         op0=ALU.add, op1=ALU.mult).then_inc(kp_up, 1)
            for p in range(PAIRS):
                dve.wait_ge(ss_up, START + p + 1)
                dve.tensor_scalar(PD[:, p, :], banks[4 + p % 2][:, :], 1e-24, None, ALU.max).then_inc(ss_max, 1)

            def bonus_in(p):
                dve.wait_ge(rk_up, START + p + 1)
                dve.tensor_scalar(tmp[2 + p % 2][:, :], tmp[2 + p % 2][:, :], par[:, R_RK + p:R_RK + p + 1], None,
                                  ALU.mult).then_inc(rks_up, 1)

            def bonus_out(p):
                dve.wait_ge(bsum_up, START + p + 1)
                dve.tensor_tensor(BO[:, p, :], banks[4 + p % 2][:, :], PM[:, 8 + p, :], ALU.mult).then_inc(bo_up, 1)
            bonus_in(0)
            bonus_in(1)
            for p in range(PAIRS):
                dve.wait_ge(ss_root, START + p + 1)
                step(dve.reciprocal(PD[:, p, :], PD[:, p, :]))
                dve.scalar_tensor_tensor(out=KN[:, p, :], in0=KN[:, p, :], scalar=-1.0, in1=PD[:, p, :],
                                         op0=ALU.mult, op1=ALU.mult).then_inc(nk_up, 1)
                dve.wait_ge(nk_up, START + 2 * p + 1)
                dve.scalar_tensor_tensor(out=AI[:, p, :], in0=KN[:, p, :], scalar=-1.0, in1=AI[:, p, :],
                                         op0=ALU.mult, op1=ALU.mult).then_inc(nk_up, 1)
            for p in range(2):
                bonus_out(p)
            for p in range(2, PAIRS):
                bonus_in(p)
                bonus_out(p)
            dve.wait_ge(exp_up, START + 2 * PAIRS)
            dve.tensor_copy(PL[:, :, :], PD[:, :, CH - 1::CH])
            dve.wait_ge(rk_up, START + PAIRS)
            dve.wait_ge(nk_up, START + 2 * PAIRS)
            for p in range(PAIRS):
                dve.tensor_tensor(PM[:, p, :], PM[:, p, :], PD[:, p, :], ALU.mult)
                dve.tensor_tensor(KN[:, p, :], KN[:, p, :], SW[:, p, :], ALU.mult)
            dve.wait_ge(gb_in, START + 32)
            for m, gt in ((0, gt1), (1, gt2)):
                dve.wait_ge(gates_up, START + 2 * m + 2)
                for h in range(2):
                    dve.tensor_tensor(gt[:, h * 512:(h + 1) * 512], banks[2 - 2 * m + h][:, :], gt[:, h * 512:(h + 1) * 512],
                                      ALU.add).then_inc(gate_used, 1)
            dve.wait_ge(ada_used, START + 8)
            step(dve.tensor_tensor(mod[:, 16:32], banks[6][:, 16:32], par[:, R_ADAB + 24:R_ADAB + 40], ALU.add))
            dve.tensor_scalar(mod[:, 24:32], mod[:, 24:32], 1.0, None, ALU.add)


def emit_mixing(nc, banks, sem, v):
    attn_sink = v["attn_sink"]
    (ident, par, diag2, qT, kT, vtok, PM, AI, GG, KN, BO, PL, yT) = (
        v[n] for n in ("ident", "par", "diag2", "qT", "kT", "vtok", "PM", "AI", "GG", "KN", "BO", "PL", "yT"))
    ctx = ExitStack()
    with ctx:
        def sb(name, shape, dt=F32):
            return ctx.enter_context(nc.sbuf_tensor(name, shape, dt))

        LV = 6
        masks = sb("masks", [P, 2, P])
        lvl = sb("lvl", [P, LV, P])
        window = sb("window", [P, 2, 2 * P])
        mean2 = sb("mean2", [P, P])
        sinks = sb("sinks", [P, HEADS])
        AR = sb("AR", [P, 2, 4, P])
        Bs, Ks, Vs = (sb(n, [P, 4, P]) for n in ("Bs", "Ks", "Vs"))
        BHs, KHs = (sb(n, [P, 4, P]) for n in ("BHs", "KHs"))
        RH = sb("RH", [P, 2, HEADS, HD])
        vwin = RH[:, 0, 0:4, :].rearrange("p (k a) d -> p k (a d)", k=2)
        VT = sb("VT", [P, HEADS * HD])
        BH, KH = (sb(n, [P, 2, 4, P]) for n in ("BH", "KH"))
        BM, KM = (sb(n, [P, HEADS, 2, P]) for n in ("BM", "KM"))
        PT = sb("PT", [P, HEADS, 2, P])
        NL = [[PT[:, 4 * g + 2 * b:4 * g + 2 * b + 2, :, :].rearrange("p a b c -> p (a b) c") for b in range(2)]
              for g in range(2)]
        DD, DT, XX = ([sb(f"{n}{g}", [P, 4, P]) for g in range(2)] for n in ("DD", "DT", "XX"))
        WW = sb("WW", [P, 2, HEADS, HD])
        QT = sb("QT", [P, 4, P])
        GT, HS = (sb(n, [P, 2, 4, P]) for n in ("GT", "HS"))
        dPL = sb("dPL", [P, 2, 4, P])
        S = [sb(f"S{c}", [P, 4, P]) for c in range(2)]
        Y, Yc, Yq, Yv = (sb(n, [P, 4, P]) for n in ("Y", "Yc", "Yq", "Yv"))
        qs = sb("qs", [P, 4, P])
        ks = sb("ks", [P, 2, 2 * P])
        SC = KM[:, :, :, :].rearrange("p h u k -> p h (u k)")
        mx, nm, es, rs = (sb(n, [P, HEADS]) for n in ("mx", "nm", "es", "rs"))
        ON = sb("ON", [P, HEADS * HD])
        gatepost = sb("gatepost3", [P, 1])

        names = ("ready sink_in ar bks vs bhs gramB maskB gramK maskK tr trA trV trB trK nl dt0 dd0 dd0c xx xxc d dc "
                 "t tc x0 x0c w wc qt qtc g gc h hc y yc st stc m mc sq va vac root rstd gn dpl "
                 "qks sc scm mx ex rsum pt ptc o oc ot otc").split()
        ev = {n: sem("mix_" + n) for n in names}
        p_dve, p_act, p_pool = sem("mix_dve"), sem("mix_act"), sem("mix_pool")
        nc.all_engine_barrier()
        block = ctx.enter_context(nc.Block())

        def waits(eng, n):
            def now(name, k=1, per=1):
                eng.wait_ge(ev[name], START + n * per + k)

            def before(name, per=1):
                eng.wait_ge(ev[name], START + n * per)
            return now, before

        def cols(n):
            return bass.ds(n * P, P)

        def four(ap):
            return ap.rearrange("p (a b) -> p a b", a=4)

        @block.sync
        def _(sp):
            sp.dma_start(sinks[:, :], attn_sink.rearrange("o n -> (o n)").partition_broadcast(P))\
                .then_inc(ev["sink_in"], 16)
            sp.wait_ge(ev["sink_in"], START + 16)

        @block.gpsimd
        def _(pool):
            step = stepper(pool, Tally(p_pool))
            step(pool.memset(masks[:, :, :], 1.0))
            for k in range(2):
                m = masks[:, k, :].rearrange("p (b w) -> p b w", b=2)
                step(pool.affine_select(out=m, in_=m, compare_op=ALU.is_ge, fill=0.0, base=k - 1,
                                        pattern=[[CH, 2], [1, CH]], channel_multiplier=-1))
                step(pool.affine_select(out=m, in_=m, compare_op=ALU.is_ge, fill=0.0, base=0,
                                        pattern=[[-CH, 2], [0, CH]], channel_multiplier=1))
            step(pool.memset(lvl[:, :, :], 1.0))
            for l in range(LV):
                w = 1 << l
                nb = P // (2 * w)
                m = lvl[:, l, :].rearrange("p (b u w) -> p b u w", u=2, w=w)
                for base, pattern, cm in ((0, [[-2 * w, nb], [0, 2], [0, w]], 1),
                                          (w - 1, [[2 * w, nb], [0, 2], [0, w]], -1),
                                          (-1, [[0, nb], [1, 2], [0, w]], 0)):
                    step(pool.affine_select(out=m, in_=m, compare_op=ALU.is_ge, fill=0.0, base=base,
                                            pattern=pattern, channel_multiplier=cm))
            step(pool.memset(window[:, :, :], 0.0))
            for base, pattern, cm in ((P, [[0, 2], [-1, 2 * P]], 1), (-1, [[0, 2], [1, 2 * P]], -1)):
                step(pool.affine_select(out=window[:, :, :], in_=window[:, :, :], compare_op=ALU.is_ge, fill=NEG,
                                        base=base, pattern=pattern, channel_multiplier=cm))
            step(pool.memset(window[:, 0, 0:P], NEG))
            for s in S:
                step(pool.memset(s[:, :, :], 0.0))
            pool.tensor_scalar(mean2[:, :], diag2[:, :], 1.0 / HD, None, ALU.mult).then_inc(ev["ready"], 1)
            with pool.Fori(0, NT) as n:
                now, before = waits(pool, n)
                before("tr", 4)
                pool.tensor_copy(Vs[:, :, :], PM[:, 8:12, cols(n)]).then_inc(ev["vs"], 1)
                decay = PL[:, :, bass.ds(2 * n, 2)].unsqueeze(3).broadcast_to([P, 4, 2, CH])
                for src, dst in ((AI[:, :, cols(n)], BHs), (PM[:, 4:8, cols(n)], KHs)):
                    pool.tensor_tensor(dst[:, :, :].rearrange("p a (c w) -> p a c w", c=2),
                                       src.rearrange("p a (c w) -> p a c w", c=2), decay, ALU.mult)\
                        .then_inc(ev["bhs"], 1)
                for l in range(1, LV):
                    for g in range(2):
                        if l == 1:
                            now("maskB", 2 * g + 2, 4)
                            before("xx", 10)
                            before("o")
                        if l >= 3:
                            now("xx", 2 * (l - 3) + g + 1, 10)
                        pool.tensor_tensor(NL[g][l % 2][:, :, :], BM[:, 4 * g:4 * g + 4, 0, :],
                                           lvl[:, l, :].unsqueeze(1).broadcast_to([P, 4, P]), ALU.mult)\
                            .then_inc(ev["nl"], 1)
                before("gc", 2)
                pool.tensor_tensor(gatepost[:, :], masks[:, 0, 0:1], masks[:, 0, 0:1], ALU.mult)
                for c in range(2):
                    pool.tensor_tensor(dPL[:, c, :, :], ident[:, :].unsqueeze(1).broadcast_to([P, 4, P]),
                                       PL[:, :, bass.ds(2 * n + c, 1)].broadcast_to([P, 4, P]), ALU.mult)\
                        .then_inc(ev["dpl"], 1)

        @block.scalar
        def _(act):
            def rows_of_tile(n):
                act.activation(AR[:, 0, :, :], KN[:, :, cols(n)], ACT.Copy).then_inc(ev["ar"], 1)
                act.activation(AR[:, 1, :, :], PM[:, 0:4, cols(n)], ACT.Copy).then_inc(ev["ar"], 1)
            rows_of_tile(0)
            with act.Fori(0, NT) as n:
                now, before = waits(act, n)
                before("sc", 4)
                act.activation(qs[:, :, :], qT[:, :, cols(n)], ACT.Copy).then_inc(ev["qks"], 1)
                act.activation(ks[:, :, :], kT[:, :, bass.ds(n * P, 2 * P)], ACT.Copy).then_inc(ev["qks"], 1)
                now("tr", 1, 4)
                before("w", 2)
                act.activation(RH[:, 0, :, :].rearrange("p h d -> p (h d)"), banks[4][:, :], ACT.Copy)\
                    .then_inc(ev["trA"], 1)
                now("tr", 2, 4)
                before("st", 2)
                act.activation(VT[:, :], banks[5][:, :], ACT.Copy).then_inc(ev["trV"], 1)
                for j, (dst, name) in enumerate(((BH, "trB"), (KH, "trK"))):
                    now("tr", 3 + j, 4)
                    for c in range(2):
                        act.activation(dst[:, c, :, :], four(banks[6 + j][:, :]), ACT.Copy,
                                       scale=diag2[:, CH * c:CH * c + 1]).then_inc(ev[name], 1)
                for g in range(2):
                    now("dd0", g + 1, 2)
                    act.activation(DD[g][:, :, :], four(banks[g][:, :]), ACT.Copy).then_inc(ev["dd0c"], 1)
                for l in range(1, LV):
                    for g in range(2):
                        if l < LV - 1:
                            now("d", 2 * (l - 1) + g + 1, 8)
                            act.activation(DD[g][:, :, :], four(banks[2 + g][:, :]), ACT.Copy)\
                                .then_inc(ev["dc"], 1)
                        now("t", 2 * (l - 1) + g + 1, 10)
                        act.activation(DT[g][:, :, :], four(banks[6 + g][:, :]), ACT.Copy).then_inc(ev["tc"], 1)
                now("x0")
                act.activation(RH[:, 1, :, :].rearrange("p h d -> p (h d)"), banks[4][:, :], ACT.Copy)\
                    .then_inc(ev["x0c"], 1)
                for g in range(2):
                    now("w", g + 1, 2)
                    act.activation(WW[:, :, 4 * g:4 * g + 4, :],
                                   banks[g][:, :].rearrange("p (h u d) -> p u h d", u=2, d=HD), ACT.Copy)\
                        .then_inc(ev["wc"], 1)
                act.activation(vwin, vtok[:, bass.ds(n, 2), :], ACT.Copy).then_inc(ev["qks"], 1)
                now("y")
                before("m")
                act.activation(Y[:, :, :], four(banks[4][:, :]), ACT.Copy).then_inc(ev["yc"], 1)
                now("mc")
                act.activation(Yq[:, :, :], Yc[:, :, :], ACT.Square).then_inc(ev["sq"], 1)
                now("vac")
                act.activation(Yv[:, :, :], Yv[:, :, :], ACT.Sqrt).then_inc(ev["root"], 1)
                now("mx")
                before("rsum")
                act.activation(es[:, :], es[:, :], ACT.Exp).then_inc(ev["ex"], 1)
                for h in range(HEADS):
                    act.activation(SC[:, h, :], SC[:, h, :], ACT.Exp, bias=nm[:, h:h + 1],
                                   accum_out=rs[:, h:h + 1]).then_inc(ev["ex"], 1)
                for j in range(4):
                    now("pt", j + 1, 4)
                    act.activation(PT[:, 2 * j:2 * j + 2, :, :].rearrange("p h k q -> p (h k q)"),
                                   banks[2 + j][:, :], ACT.Copy).then_inc(ev["ptc"], 1)
                now("gramK", 4, 4)
                now("qtc")
                rows_of_tile((n + 1) % NT)
                now("ot")
                act.activation(yT[:, 0:4, cols(n)], four(banks[7][:, :]), ACT.Copy).then_inc(ev["otc"], 1)

        @block.tensor
        def _(pe):
            pe.wait_ge(ev["ready"], START + 1)
            with pe.Fori(0, NT) as n:
                now, before = waits(pe, n)

                def grams(src, first, name):
                    for g in range(2):
                        for e in range(2):
                            for j in range(2):
                                p = 2 * g + j
                                rows = slice(64 * e, 64 * e + 64)
                                last = pe.matmul(banks[first + 2 * g + e][:, 256 * j:256 * j + 256],
                                                 src[rows, p, :], AR[rows, :, p, :], start=True, stop=True)
                            last.then_inc(ev[name], 1)
                now("ar", 2, 2)
                now("bks", 2, 2)
                before("gn")
                grams(Bs, 0, "gramB")
                before("otc")
                now("vs")
                now("bhs", 2, 2)
                for b, src in ((4, AR[:, 0]), (5, Vs), (6, BHs), (7, KHs)):
                    for p in range(4):
                        last = pe.transpose(banks[b][:, p * P:(p + 1) * P],
                                            src[:, p, :], ident[:, :])
                    last.then_inc(ev["tr"], 1)
                for g in range(2):
                    now("dt0", g + 1, 2)
                    for h in range(4):
                        last = pe.transpose(banks[g][:, h * P:(h + 1) * P], DT[g][:, h, :], ident[:, :])
                    last.then_inc(ev["dd0"], 1)
                now("maskB", 4, 4)
                now("trV")
                grams(Ks, 2, "gramK")
                for l in range(1, LV):
                    for g in range(2):
                        now("nl", 2 * (l - 1) + g + 1, 10)
                        if l == 1:
                            now("dd0c", g + 1, 2)
                        else:
                            now("dc", 2 * (l - 2) + g + 1, 8)
                        for h in range(4):
                            last = pe.matmul(banks[g][:, h * P:(h + 1) * P], NL[g][l % 2][:, h, :],
                                             DD[g][:, h, :], start=True, stop=True)
                        last.then_inc(ev["xx"], 1)
                    for g in range(2):
                        now("xxc", 2 * (l - 1) + g + 1, 10)
                        if l == 1:
                            now("maskK", 4, 4)
                            now("trK", 2, 2)
                        else:
                            now("tc", 2 * (l - 2) + g + 1, 10)
                        if l < LV - 1:
                            for h in range(4):
                                last = pe.matmul(banks[2 + g][:, h * P:(h + 1) * P], DT[g][:, h, :],
                                                 XX[g][:, h, :], start=True, stop=True)
                            last.then_inc(ev["d"], 1)
                        for h in range(4):
                            last = pe.matmul(banks[6 + g][:, h * P:(h + 1) * P], XX[g][:, h, :],
                                             DT[g][:, h, :], start=True, stop=True)
                        last.then_inc(ev["t"], 1)
                for h in range(HEADS):
                    last = pe.matmul(banks[4][:, h * HD:(h + 1) * HD], KM[:, h, 0, :],
                                     VT[:, h * HD:(h + 1) * HD], start=True, stop=True)
                last.then_inc(ev["x0"], 1)
                now("x0c")
                now("tc", 10, 10)
                for g in range(2):
                    for h in range(4):
                        last = pe.matmul(banks[g][:, h * P:(h + 1) * P], DT[g][:, h, :],
                                         RH[:, :, 4 * g + h, :], start=True, stop=True)
                    last.then_inc(ev["w"], 1)
                now("wc", 2, 2)
                for h in range(HEADS):
                    last = pe.matmul(banks[5][64 * (h % 2):64 * (h % 2) + 64, (h // 2) * P:(h // 2 + 1) * P],
                                     WW[:, 0, h, :], BM[:, h, 1, :], start=True, stop=True)
                last.then_inc(ev["qt"], 1)
                for c in range(2):
                    for p in range(4):
                        last = pe.matmul(banks[2 + c][:, p * P:(p + 1) * P], WW[:, 0, 2 * p:2 * p + 2, :],
                                         BH[:, c, p, :], start=True, stop=True)
                    last.then_inc(ev["g"], 1)
                    for p in range(4):
                        pe.matmul(banks[6 + c][:, p * P:(p + 1) * P], BH[:, c, p, :],
                                  WW[:, 1, 2 * p:2 * p + 2, :], start=True, stop=False)
                        last = pe.matmul(banks[6 + c][:, p * P:(p + 1) * P], KH[:, c, p, :],
                                         VT[:, p * P:(p + 1) * P], start=False, stop=True)
                    last.then_inc(ev["h"], 1)
                for e in range(2):
                    for p in range(4):
                        h = 2 * p + e
                        o = banks[4][64 * e:64 * e + 64, p * P:(p + 1) * P]
                        pe.matmul(o, WW[:, 1, h, :], BM[:, h, 1, :], start=(p == 0), stop=False,
                                  skip_group_check=True)
                        pe.matmul(o, VT[:, h * HD:(h + 1) * HD], KM[:, h, 1, :], start=False, stop=False,
                                  skip_group_check=True)
                now("qtc")
                for c in range(2):
                    if c == 0:
                        before("stc", 2)
                    else:
                        now("stc", 1, 2)
                    for p in range(4):
                        o = banks[4][:, p * P + CH * c:p * P + CH * c + CH]
                        last = pe.matmul(o, S[c][:, p, :], QT[:, p, CH * c:CH * c + CH], start=False, stop=True,
                                         skip_group_check=True)
                    if c == 1:
                        last.then_inc(ev["y"], 1)
                    now("gc", c + 1, 2)
                    for p in range(4):
                        last = pe.matmul(banks[c][:, p * P:(p + 1) * P], GT[:, c, p, :], S[c][:, p, :],
                                         start=True, stop=True)
                    last.then_inc(ev["st"], 1)
                now("qks", 3, 3)
                now("hc", 2, 2)
                for g in range(2):
                    for e in range(2):
                        b = (2, 3, 6, 7)[2 * g + e]
                        for j in range(2):
                            rows = slice(64 * e, 64 * e + 64)
                            last = pe.matmul(banks[b][:, 256 * j:256 * j + 256], qs[rows, 2 * g + j, :],
                                             ks[rows, g, :], start=True, stop=True)
                        last.then_inc(ev["sc"], 1)
                now("yc")
                pe.matmul(banks[5][:, :], mean2[:, :], Y[:, :, :].rearrange("p a b -> p (a b)"), start=True,
                          stop=True).then_inc(ev["m"], 1)
                now("sq")
                pe.matmul(banks[5][:, :], mean2[:, :], Yq[:, :, :].rearrange("p a b -> p (a b)"), start=True,
                          stop=True).then_inc(ev["va"], 1)
                now("vac")
                now("scm", 4, 4)
                now("ex", 9, 9)
                for j in range(4):
                    for h in (2 * j, 2 * j + 1):
                        for k in range(2):
                            last = pe.transpose(banks[2 + j][:, (h % 2) * 256 + k * P:(h % 2) * 256 + (k + 1) * P],
                                                SC[:, h, k * P:(k + 1) * P], ident[:, :])
                    last.then_inc(ev["pt"], 1)
                for h in range(HEADS):
                    now("ptc", h // 2 + 1, 4)
                    for k in range(2):
                        last = pe.matmul(banks[6][:, h * HD:(h + 1) * HD], PT[:, h, k, :],
                                         vwin[:, k, 64 * (h // 4):64 * (h // 4) + 64], start=(k == 0),
                                         stop=(k == 1))
                last.then_inc(ev["o"], 1)
                now("oc")
                for p in range(4):
                    last = pe.transpose(banks[7][:, p * P:(p + 1) * P], ON[:, p * P:(p + 1) * P], ident[:, :])
                last.then_inc(ev["ot"], 1)

        @block.vector
        def _(dve):
            per = 12
            chain = Tally(p_dve)
            dve.wait_ge(ev["ready"], START + 1)
            dve.wait_ge(ev["sink_in"], START + 16)

            def rows_of_tile(n):
                dve.tensor_copy(Bs[:, :, :], AI[:, :, cols(n)]).then_inc(ev["bks"], 1)
                dve.tensor_copy(Ks[:, :, :], PM[:, 4:8, cols(n)]).then_inc(ev["bks"], 1)
            rows_of_tile(0)
            with dve.Fori(0, NT) as n:
                now, before = waits(dve, n)
                chain.enter(n, per)
                step = stepper(dve, chain)
                def mask(bank, dst, name, g, e):
                    dve.tensor_tensor(dst[:, 4 * g + e:4 * g + e + 3:2, :, :].rearrange("p h u t -> p h (u t)"),
                                      banks[bank][:, :].rearrange("p (h u) -> p h u", h=2),
                                      masks[:, :, :].rearrange("p u t -> p (u t)").unsqueeze(1)
                                      .broadcast_to([P, 2, 2 * P]), ALU.mult).then_inc(ev[name], 1)
                before("y")
                for g in range(2):
                    for e in range(2):
                        now("gramB", 2 * g + e + 1, 4)
                        mask(2 * g + e, BM, "maskB", g, e)
                for g in range(2):
                    now("maskB", 2 * g + 2, 4)
                    before("w", 2)
                    step(dve.tensor_tensor(DT[g][:, :, :], BM[:, 4 * g:4 * g + 4, 0, :],
                                           lvl[:, 0, :].unsqueeze(1).broadcast_to([P, 4, P]), ALU.mult))
                    dve.tensor_tensor(DT[g][:, :, :], DT[g][:, :, :],
                                      ident[:, :].unsqueeze(1).broadcast_to([P, 4, P]), ALU.add)\
                        .then_inc(ev["dt0"], 1)
                for g in range(2):
                    for e in range(2):
                        now("gramK", 2 * g + e + 1, 4)
                        mask(2 + 2 * g + e, KM, "maskK", g, e)
                for l in range(1, LV):
                    for g in range(2):
                        now("xx", 2 * (l - 1) + g + 1, 10)
                        dve.tensor_tensor(XX[g][:, :, :], four(banks[g][:, :]),
                                          ident[:, :].unsqueeze(1).broadcast_to([P, 4, P]), ALU.add)\
                            .then_inc(ev["xxc"], 1)
                now("qt")
                dve.tensor_tensor(QT[:, :, :], four(banks[5][:, :]), AR[:, 1, :, :], ALU.add)\
                    .then_inc(ev["qtc"], 1)
                dg = diag2[:, :].unsqueeze(1).broadcast_to([P, 4, P])
                for c in range(2):
                    now("g", c + 1, 2)
                    now("dpl", c + 1, 2)
                    step(dve.tensor_tensor(GT[:, c, :, :], four(banks[2 + c][:, :]), dg, ALU.mult))
                    dve.tensor_tensor(GT[:, c, :, :], GT[:, c, :, :], dPL[:, c, :, :], ALU.add)\
                        .then_inc(ev["gc"], 1)
                    now("h", c + 1, 2)
                    dve.tensor_tensor(HS[:, c, :, :], four(banks[6 + c][:, :]), dg, ALU.mult)\
                        .then_inc(ev["hc"], 1)
                for c in range(2):
                    now("st", c + 1, 2)
                    now("hc", c + 1, 2)
                    if c == 0:
                        before("y")
                    dve.tensor_tensor(S[1 - c][:, :, :], four(banks[c][:, :]), HS[:, c, :, :], ALU.add)\
                        .then_inc(ev["stc"], 1)
                now("m")
                dve.tensor_tensor(Yc[:, :, :], Y[:, :, :], four(banks[5][:, :]), ALU.subtract)\
                    .then_inc(ev["mc"], 1)
                now("va")
                dve.tensor_scalar(Yv[:, :, :], four(banks[5][:, :]), GN_EPS, None, ALU.add).then_inc(ev["vac"], 1)
                for g in range(2):
                    for e in range(2):
                        now("sc", 2 * g + e + 1, 4)
                        b = (2, 3, 6, 7)[2 * g + e]
                        last = dve.tensor_tensor(
                            SC[:, 4 * g + e:4 * g + e + 3:2, :], banks[b][:, :].rearrange("p (h k) -> p h k", h=2),
                            window[:, bass.ds((n + 3) // 4, 1), :].broadcast_to([P, 2, 2 * P]), ALU.add)
                        last.then_inc(ev["scm"], 1)
                now("scm", 4, 4)
                step(dve.tensor_reduce(mx[:, :], SC[:, :, :], AX.X, ALU.max))
                step(dve.tensor_tensor(mx[:, :], mx[:, :], sinks[:, :], ALU.max))
                dve.tensor_scalar(nm[:, :], mx[:, :], -1.0, None, ALU.mult)
                dve.tensor_tensor(es[:, :], sinks[:, :], mx[:, :], ALU.subtract).then_inc(ev["mx"], 1)
                now("root")
                lx = [par[:, r:r + 4].unsqueeze(2).broadcast_to([P, 4, P]) for r in (R_LXG, R_LXB)]
                step(dve.reciprocal(Yv[:, :, :], Yv[:, :, :]))
                step(dve.tensor_tensor(Yc[:, :, :], Yc[:, :, :], Yv[:, :, :], ALU.mult))
                step(dve.tensor_tensor(Yc[:, :, :], Yc[:, :, :], lx[0], ALU.mult))
                step(dve.tensor_tensor(Yc[:, :, :], Yc[:, :, :], lx[1], ALU.add))
                step(dve.tensor_tensor(Yc[:, :, :], Yc[:, :, :], BO[:, :, cols(n)], ALU.add))
                dve.tensor_tensor(yT[:, 4:8, cols(n)], Yc[:, :, :], GG[:, :, cols(n)], ALU.mult)\
                    .then_inc(ev["gn"], 1)
                now("ex", 9, 9)
                step(dve.tensor_tensor(rs[:, :], rs[:, :], es[:, :], ALU.add))
                dve.reciprocal(rs[:, :], rs[:, :]).then_inc(ev["rsum"], 1)
                now("gramK", 4, 4)
                rows_of_tile((n + 1) % NT)
                now("rsum")
                now("o")
                before("ot")
                dve.tensor_tensor(ON[:, :].rearrange("p (h d) -> p h d", h=HEADS),
                                  banks[6][:, :].rearrange("p (h d) -> p h d", h=HEADS),
                                  rs[:, :].unsqueeze(2).broadcast_to([P, HEADS, HD]), ALU.mult)\
                    .then_inc(ev["oc"], 1)
                chain.leave(NT)


TB = 32


class Norm:

    def __init__(self, nc, sb, prefix):
        self.nc = nc
        self.stats = [sb(f"{prefix}stats{i}", [P, 2, 6]) for i in range(2)]
        self.mv = [sb(f"{prefix}mv{i}", [P, 2]) for i in range(2)]
        self.sd = [sb(f"{prefix}sd{i}", [P, 1]) for i in range(2)]

    def moments(self, dve, step, t, tile):
        for h in range(2):
            last = dve.bn_stats(out=self.stats[t % 2][:, h, :], in_=tile[:, 512 * h:512 * h + 512])
        step(last)
        step(dve.bn_aggr(out=self.mv[t % 2][:, :], in_=self.stats[t % 2][:, :, :].rearrange("p a b -> p (a b)")))
        return dve.tensor_scalar(self.sd[t % 2][:, :], self.mv[t % 2][:, 1:2], LN_EPS, None, ALU.add)

    def root(self, act, t):
        return act.activation(self.sd[t % 2][:, :], self.sd[t % 2][:, :], ACT.Sqrt)

    def scaled(self, dve, step, t, tile):
        step(dve.reciprocal(self.sd[t % 2][:, :], self.sd[t % 2][:, :]))
        return dve.tensor_scalar(tile, tile, self.mv[t % 2][:, 0:1], self.sd[t % 2][:, :], ALU.subtract, ALU.mult)


def query_weights(peer_wq):
    return peer_wq[0].rearrange("(k p) n -> p k n", p=P)


def subkey_rows(peer_subkeys):
    return peer_subkeys[0].rearrange("h c n d -> n (h c) d")


def expert_rows(experts):
    return experts[0].rearrange("(i j) d -> i j d", j=NKEYS)


def emit_mix_out(nc, banks, sem, v):
    (x, w_out, ln1_g, ln1_b, ident, mod, gt1, yT, x1_kept, h2, hh, hl, peer_wq, peer_subkeys, peer_u, wq, sk,
     urows) = (v[n] for n in ("x", "w_out", "ln1_g", "ln1_b", "ident", "mod", "gt1", "yT", "x1_kept", "h2", "hh",
                              "hl", "peer_wq", "peer_subkeys", "peer_u", "wq", "sk", "urows"))
    ctx = ExitStack()
    with ctx:
        def sb(name, shape, dt=F32):
            return ctx.enter_context(nc.sbuf_tensor(name, shape, dt))

        wo = [sb(f"wo{k}", [P, D]) for k in range(KD)]
        xs = sb("xs", [P, NT, D])
        x1 = sb("x1", [P, NT, D])
        lg, lb = sb("lg", [P, D]), sb("lb", [P, D])
        norm = Norm(nc, sb, "n1_")
        wo_in = [sem(f"wo_in{k}") for k in range(KD)]
        xs_in, ln_in = sem("xs_in"), sem("ln_in")
        y_up, y_used, var_up, root_up = sem("y_up"), sem("y_used"), sem("var_up"), sem("root_up")
        centred, gained, x1_up = sem("centred"), sem("gained"), sem("x1_up")
        xt_up, h_up, hh_up, hl_up = sem("x1t_up"), sem("h2_up"), sem("hh_up"), sem("hl_up")
        p_dve, kept, asked_in = sem("p_dve3"), sem("x1_kept3"), sem("asked_in")
        nc.all_engine_barrier()
        block = ctx.enter_context(nc.Block())

        @block.sync
        def _(sp):
            wv = w_out[0].rearrange("(k p) n -> k p n", p=P)
            for k in range(KD):
                sp.dma_start(wo[k][:, :], wv[k]).then_inc(wo_in[k], 16)
            sp.dma_start(xs[:, :, :], x[0].rearrange("(t p) d -> p t d", p=P)).then_inc(xs_in, 16)
            for dst, src in ((lg, ln1_g), (lb, ln1_b)):
                sp.dma_start(dst[:, :], src.rearrange("o n -> (o n)").partition_broadcast(P)).then_inc(ln_in, 16)
            for c in range(2):
                sp.dma_start(wq[c][:, :, :], query_weights(peer_wq)[:, :, c * P:(c + 1) * P]).then_inc(asked_in, 16)
                sp.dma_start(sk[c][:, :], subkey_rows(peer_subkeys)[:, c, :]).then_inc(asked_in, 16)
            for s in range(4):
                sp.dma_start(urows[s][:, :], expert_rows(peer_u)[:, s, :]).then_inc(asked_in, 16)
            for t in range(NT):
                sp.wait_ge(x1_up, START + t + 1)
                sp.dma_start(x1_kept[t], x1[:, t, :]).then_inc(kept, 16)
            sp.wait_ge(ln_in, START + 32)
            sp.wait_ge(kept, START + 16 * NT)
            sp.wait_ge(asked_in, START + 16 * 8)

        @block.tensor
        def _(pe):
            def turn(t):
                pe.wait_ge(x1_up, START + t + 1)
                for h in range(2):
                    for k in range(4):
                        last = pe.transpose(banks[4 + 2 * (t % 2) + h][:, k * P:(k + 1) * P],
                                            x1[:, t, (4 * h + k) * P:(4 * h + k + 1) * P], ident[:, :])
                    last.then_inc(xt_up, 1)
            for t in range(NT):
                if t >= 2:
                    pe.wait_ge(y_used, START + 2 * (t - 1))
                for h in range(2):
                    for k in range(KD):
                        if t == 0 and h == 0:
                            pe.wait_ge(wo_in[k], START + 16)
                        last = pe.matmul(banks[2 * (t % 2) + h][:, :], yT[:, k, t * P:(t + 1) * P],
                                         wo[k][:, 512 * h:512 * h + 512], start=(k == 0), stop=(k == KD - 1))
                    last.then_inc(y_up, 1)
                if t >= 1:
                    if t >= 3:
                        pe.wait_ge(h_up, START + 8 * (t - 2))
                    turn(t - 1)
            pe.wait_ge(h_up, START + 8 * (NT - 2))
            turn(NT - 1)

        def split(dve, t):
            cols = slice(t * P, (t + 1) * P)
            dve.wait_ge(h_up, START + 8 * (t + 1))
            dve.tensor_copy(hh[:, :, cols], h2[:, :, cols]).then_inc(hh_up, 1)
            dve.wait_ge(hh_up, START + t + 1)
            dve.tensor_tensor(hl[:, :, cols], h2[:, :, cols], hh[:, :, cols].bitcast(F32), ALU.subtract)\
                .then_inc(hl_up, 1)

        @block.vector
        def _(dve):
            step = stepper(dve, Tally(p_dve))
            def head(t):
                for h in range(2):
                    half = slice(512 * h, 512 * h + 512)
                    dve.wait_ge(y_up, START + 2 * t + h + 1)
                    ins = dve.tensor_tensor(x1[:, t, half], banks[2 * (t % 2) + h][:, :], gt1[:, half], ALU.mult)
                    ins.then_inc(y_used, 1)
                dve.wait_ge(xs_in, START + 16)
                dve.wait_ge(y_used, START + 2 * t + 2)
                step(dve.scalar_tensor_tensor(out=x1[:, t, :], in0=xs[:, t, :], scalar=ALPHA, in1=x1[:, t, :],
                                              op0=ALU.mult, op1=ALU.add))
                norm.moments(dve, step, t, x1[:, t, :]).then_inc(var_up, 1)

            def tail(t):
                dve.wait_ge(root_up, START + t + 1)
                norm.scaled(dve, step, t, x1[:, t, :]).then_inc(centred, 1)
                dve.wait_ge(gained, START + t + 1)
                dve.tensor_tensor(x1[:, t, :], x1[:, t, :], lb[:, :], ALU.add).then_inc(x1_up, 1)
            dve.wait_ge(ln_in, START + 32)
            for t in range(NT):
                head(t)
                tail(t)
                if t >= 1:
                    split(dve, t - 1)
            split(dve, NT - 1)

        @block.gpsimd
        def _(pool):
            pool.wait_ge(ln_in, START + 32)
            for t in range(NT):
                pool.wait_ge(centred, START + t + 1)
                pool.tensor_tensor(x1[:, t, :], x1[:, t, :], lg[:, :], ALU.mult).then_inc(gained, 1)

        @block.scalar
        def _(act):
            for t in range(NT):
                act.wait_ge(var_up, START + t + 1)
                norm.root(act, t).then_inc(root_up, 1)
                for k in range(KD):
                    act.wait_ge(xt_up, START + 2 * t + k // 4 + 1)
                    act.activation(h2[:, k, t * P:(t + 1) * P],
                                   banks[4 + 2 * (t % 2) + k // 4][:, (k % 4) * P:(k % 4 + 1) * P], ACT.Identity,
                                   bias=mod[:, 16 + k:17 + k], scale=mod[:, 24 + k:25 + k]).then_inc(h_up, 1)


class ExpertScores:

    def __init__(self, nc, sb, sem, prefix, banks, ident, hh, hl, ring, peer_u, urows):
        self.nc, self.banks, self.ident, self.hh, self.hl, self.ring = nc, banks, ident, hh, hl, ring
        self.u = urows
        self.uraw = sb(prefix + "uraw", [P, KD, P])
        self.uh = [sb(f"{prefix}uh{s}", [P, KD, P], F32R) for s in range(2)]
        self.ul = [sb(f"{prefix}ul{s}", [P, KD, P], F32R) for s in range(2)]
        self.u_in = [sem(f"{prefix}u_in{s}") for s in range(4)]
        self.turned, self.uh_up, self.uraw_up, self.ul_up, self.a_up, self.gelu_up = (
            sem(prefix + n) for n in ("turned", "uh_up", "uraw_up", "ul_up", "a_up", "gelu_up"))
        self.src = expert_rows(peer_u)

    def load(self, sp, i, s, tile):
        sp.dma_start(self.u[s][:, :], self.src[:, tile, :]).then_inc(self.u_in[s], 16)

    def turn(self, pe, i, s):
        pe.wait_ge(self.u_in[s], START + 16 * i)
        for h in range(2):
            pe.wait_ge(self.uraw_up, START + 8 * i + (2 * s + h - 1))
            for k in range(4):
                last = pe.transpose(self.banks[2 + h][:, k * P:(k + 1) * P],
                                    self.u[s][:, (4 * h + k) * P:(4 * h + k + 1) * P], self.ident[:, :])
            last.then_inc(self.turned, 1)

    def product(self, pe, i, s, part=None):
        bank, uh, ul = self.banks[s % 2], self.uh[s % 2], self.ul[s % 2]
        if part in (None, 0):
            pe.wait_ge(self.uh_up, START + 8 * i + 2 * s + 2)
            pe.wait_ge(self.gelu_up, START + 4 * i + (s - 1))
        steps = [(uh, k, self.hh) for k in range(KD)] + [(uh, k, self.hl) for k in range(KD)]
        steps = [x for pair in zip(steps[:KD], steps[KD:]) for x in pair] + [(ul, k, self.hh) for k in range(KD)]
        for n in range(3 * KD) if part is None else range(3 * part, 3 * part + 3):
            if n == 2 * KD:
                pe.wait_ge(self.ul_up, START + 4 * i + s + 1)
            u, k, h = steps[n]
            last = pe.matmul(bank[:, :], u[:, k, :], h[:, k, :], start=(n == 0), stop=(n == 3 * KD - 1))
        if part in (None, KD - 1):
            last.then_inc(self.a_up, 1)

    def evacuate(self, act, i, s):
        act.wait_ge(self.a_up, START + 4 * i + (s - 1))
        for h in range(2):
            act.wait_ge(self.turned, START + 8 * i + 2 * s + h + 1)
            act.activation(self.uh[s % 2][:, 4 * h:4 * h + 4, :],
                           self.banks[2 + h][:, :].rearrange("p (k e) -> p k e", k=4), ACT.Copy)\
                .then_inc(self.uh_up, 1)
            if h == 0:
                act.wait_ge(self.ul_up, START + 4 * i + s)
            act.activation(self.uraw[:, 4 * h:4 * h + 4, :],
                           self.banks[2 + h][:, :].rearrange("p (k e) -> p k e", k=4), ACT.Copy)\
                .then_inc(self.uraw_up, 1)

    def remainder(self, pool, i, s):
        pool.wait_ge(self.uraw_up, START + 8 * i + 2 * s + 2)
        pool.wait_ge(self.uh_up, START + 8 * i + 2 * s + 2)
        pool.wait_ge(self.a_up, START + 4 * i + (s - 1))
        pool.tensor_tensor(self.ul[s % 2][:, :, :], self.uraw[:, :, :], self.uh[s % 2][:, :, :].bitcast(F32),
                           ALU.subtract).then_inc(self.ul_up, 1)

    def gelu(self, act, i, s, slot):
        act.wait_ge(self.a_up, START + 4 * i + s + 1)
        act.activation(self.ring[:, slot, :], self.banks[s % 2][:, :], ACT.Gelu).then_inc(self.gelu_up, 1)


def emit_routing(nc, banks, sem, v):
    peer_wq, peer_subkeys, peer_u, ident, h2, hh, hl, ring, gates, wq, sk, urows = (
        v[n] for n in ("peer_wq", "peer_subkeys", "peer_u", "ident", "h2", "hh", "hl", "ring", "gates", "wq", "sk",
                       "urows"))
    ctx = ExitStack()
    with ctx:
        def sb(name, shape, dt=F32):
            return ctx.enter_context(nc.sbuf_tensor(name, shape, dt))

        FV, IS, JS = (sb(n, [P, NT, HEADS, TOPK]) for n in ("FV", "IS", "JS"))
        skT = [sb(f"skT{c}", [P, P]) for c in range(2)]
        q2 = [sb(f"q2{c}", [P, T]) for c in range(2)]
        SS = sb("SS", [P, 8, 8, NKEYS])
        last3 = sb("last3", [P, 8, NKEYS])
        st2 = sb("st2", [P, 8, NKEYS])
        cands = [SS[:, k].rearrange("p (t a) (c b) -> p t (a c) b", t=NT, b=TOPK) for k in range(2)]
        cand2 = st2[:, :, :].rearrange("p (t a) (c b) -> p t (a c) b", t=NT, b=TOPK)
        sv = sb("sv", [P, 8, TOPK])
        si = sb("si", [P, 8, TOPK], U32)
        sif = sb("sif", [P, 8, TOPK])
        fv = sb("fv", [P, NT, TOPK])
        fp = sb("fp", [P, NT, TOPK], U32)
        fa = [sb(f"fa{c}", [P, NT * TOPK], U32) for c in range(2)]
        ff = [sb(f"ff{c}", [P, NT * TOPK]) for c in range(2)]
        iota = sb("iota", [P, P])
        iota16 = iota[:, 0:TOPK]
        passed = sem("passed")
        gatepost = sb("gatepost", [P, 1])
        tot = sb("tot", [P, NT, HEADS])
        SLOTS = 4
        turned = [m.rearrange("p u n -> p (u n)") for m in (last3[:, 0:4, :], last3[:, 4:8, :],
                                                                    st2[:, 0:4, :])]
        OI, OJ = ([h2[:, SLOTS * j + q, :].rearrange("p (t n) -> p t n", t=4) for q in range(SLOTS)]
                  for j in range(2))
        stage = [SS[:, 4 * b:4 * b + 4, :, :].rearrange("p h t n -> p (h t n)")
                 .rearrange("p (j t) -> p j t", t=TB) for b in range(2)]
        less_up, exp_up, gate_up, t_up, t_out = (
            sem(n) for n in ("less_up", "exp_up4", "gate_up4", "t_up4", "t_out4"))
        picked = sem("picked")
        ones_up, hot, spread, staged, p_soft = sem("ones_up"), sem("hot"), sem("spread"), sem("staged"), sem("p_soft")
        sent = [sem(f"sent{b}") for b in range(2)]
        HT = HEADS // 2
        QB = TB // 4
        BS = T // TB // (4 * (AHEAD - HT))
        assert BS * 4 * (AHEAD - HT) * TB == T and BS % 2 == 0
        scores = ExpertScores(nc, sb, sem, "r_", banks, ident, hh, hl, ring, peer_u, urows)
        wq_in = [sem(f"wq_in{c}") for c in range(2)]
        sk_in = [sem(f"sk_in{c}") for c in range(2)]
        q_up, q_out, k_up, k_out, s_up, s_out = (sem(n) for n in ("q_up", "q_out", "k_up", "k_out", "s_up", "s_out"))
        iota_up, p_dve = sem("iota_up"), sem("p_dve4")
        nc.all_engine_barrier()
        block = ctx.enter_context(nc.Block())

        @block.sync
        def _(sp):
            wv, kv = query_weights(peer_wq), subkey_rows(peer_subkeys)
            with sp.Fori(0, HT) as i:
                for s in range(4):
                    if s % 2 == 0:
                        h, nxt = 2 * i + s // 2, (2 * i + (s // 2 + 1)) % HEADS
                        for c in range(2):
                            sp.wait_ge(q_up, START + 2 * h + (c + 1))
                            sp.dma_start(wq[c][:, :, :], wv[:, :, bass.ds((2 * nxt + c) * P, P)])\
                                .then_inc(wq_in[c], 16)
                            sp.wait_ge(k_up, START + 2 * h + (c + 1))
                            sp.dma_start(sk[c][:, :],
                                         kv[:, bass.ds(2 * nxt + c, 1), :].rearrange("n o d -> n (o d)"))\
                                .then_inc(sk_in[c], 16)
                    sp.wait_ge(scores.turned, START + 8 * i + (2 * s + 2))
                    scores.load(sp, i + 1, s, bass.ds(4 * (i + 1) + s, 1))
            with sp.Fori(HT, AHEAD) as i:
                for s in range(4):
                    for o in range(BS):
                        n = BS * (4 * (i - HT) + s) + o
                        sp.wait_ge(staged, START + QB * (n + 1))
                        sp.dma_start(gates[:, bass.ds(n, 1), :, :].rearrange("p o j t -> p (o j t)"),
                                     stage[o % 2].rearrange("p j t -> p (j t)")).then_inc(sent[o % 2], 16)
                    sp.wait_ge(scores.turned, START + 8 * i + (2 * s + 2))
                    scores.load(sp, i + 1, s, bass.ds(4 * (i + 1) + s, 1))
            for b in range(2):
                sp.wait_ge(sent[b], START + 16 * (T // TB // 2))
                sp.wait_ge(wq_in[b], START + 16 * HEADS)
                sp.wait_ge(sk_in[b], START + 16 * HEADS)
            for s in range(4):
                sp.wait_ge(scores.u_in[s], START + 16 * AHEAD)

        @block.gpsimd
        def _(pool):
            pool.iota(iota[:, :], pattern=[[1, P]], base=0, channel_multiplier=0,
                      allow_small_or_imprecise_dtypes=True).then_inc(iota_up, 1)
            with pool.Fori(0, HT) as i:
                for s in range(4):
                    scores.remainder(pool, i, s)
            with pool.Fori(HT, AHEAD) as i:
                for s in range(4):
                    for q in range(BS * QB):
                        n = BS * QB * (4 * (i - HT) + s) + q
                        pool.wait_ge(ones_up, START + n + 1)
                        pool.sem_inc(passed, 1)
                        pool.tensor_tensor(OJ[q % SLOTS], OJ[q % SLOTS],
                                           turned[2][:, bass.ds(4 * n, 4)].unsqueeze(2).broadcast_to([P, 4, P]),
                                           ALU.mult).then_inc(hot, 1)
                        if q == BS * QB // 2:
                            scores.remainder(pool, i, s)

        @block.tensor
        def _(pe):
            with pe.Fori(0, HT) as i:
                scores.turn(pe, i, 0)
                for s in range(4):
                    if s % 2:
                        if s < 3:
                            scores.turn(pe, i, s + 1)
                        scores.product(pe, i, s)
                        continue
                    h = 2 * i + s // 2
                    for c in range(2):
                        pe.wait_ge(wq_in[c], START + 16 * h)
                        pe.wait_ge(q_out, START + 2 * h)
                        for k in range(KD):
                            last = pe.matmul(banks[4 + c][:, :], wq[c][:, k, :], h2[:, k, :], start=(k == 0),
                                             stop=(k == KD - 1))
                        last.then_inc(q_up, 1)
                        pe.wait_ge(sk_in[c], START + 16 * h)
                        pe.wait_ge(k_out, START + 2 * h + c)
                        pe.transpose(banks[6][:, c * P:(c + 1) * P], sk[c][:, :], ident[:, :]).then_inc(k_up, 1)
                    for c in range(2):
                        pe.wait_ge(q_out, START + 2 * h + (c + 1))
                        pe.wait_ge(k_out, START + 2 * h + (c + 1))
                        pe.wait_ge(s_out, START + 2 * h + c)
                        for t in range(NT):
                            last = pe.matmul(banks[7][:, t * P:(t + 1) * P], q2[c][:, t * P:(t + 1) * P],
                                             skT[c][:, :], start=True, stop=True)
                        last.then_inc(s_up, 1)
                        if c == 0:
                            scores.turn(pe, i, s + 1)
                    scores.product(pe, i, s)
            for j, src in enumerate((IS, JS, FV)):
                pe.wait_ge(less_up, START + 1)
                if j == 2:
                    pe.wait_ge(gate_up, START + 1)
                for t in range(NT):
                    last = pe.transpose(banks[4 + j][:, t * P:(t + 1) * P],
                                        src[:, t, :, :].rearrange("p h k -> p (h k)"), ident[:, :])
                last.then_inc(t_up, 1)
            pe.wait_ge(t_out, START + 3)
            with pe.Fori(HT, AHEAD) as i:
                scores.turn(pe, i, 0)
                for s in range(4):
                    for q in range(BS * QB):
                        pe.wait_ge(hot, START + BS * QB * (4 * (i - HT) + s) + (q + 1))
                        pe.wait_ge(staged, START + BS * QB * (4 * (i - HT) + s) + (q - 3))
                        for k in range(4):
                            last = pe.matmul(banks[4 + q % 4][:, k * P:(k + 1) * P], OI[q % SLOTS][:, k, :],
                                             OJ[q % SLOTS][:, k, :], start=True, stop=True)
                        last.then_inc(spread, 1)
                        if q % 2:
                            scores.product(pe, i, s, q // 2)
                        if q == BS * QB // 2 and s < 3:
                            scores.turn(pe, i, s + 1)

        @block.scalar
        def _(act):
            with act.Fori(0, HT) as i:
                scores.evacuate(act, i, 0)
                for s in range(4):
                    h = 2 * i + s // 2
                    if s % 2 == 0:
                        for c in range(2):
                            act.wait_ge(q_up, START + 2 * h + (c + 1))
                            act.wait_ge(s_up, START + 2 * h)
                            act.activation(q2[c][:, :], banks[4 + c][:, :], ACT.Copy).then_inc(q_out, 1)
                            act.wait_ge(k_up, START + 2 * h + (c + 1))
                            act.activation(skT[c][:, :], banks[6][:, c * P:(c + 1) * P], ACT.Copy)\
                                .then_inc(k_out, 1)
                        for c in range(2):
                            act.wait_ge(s_up, START + 2 * h + (c + 1))
                            act.wait_ge(picked, START + h - 1)
                            act.activation(SS[:, s // 2, 4 * c:4 * c + 4, :].rearrange("p t n -> p (t n)"),
                                           banks[7][:, :], ACT.Copy).then_inc(s_out, 1)
                    if s < 3:
                        scores.evacuate(act, i, s + 1)
                    scores.gelu(act, i, s, bass.ds(4 * i + s, 1))
            act.wait_ge(less_up, START + 1)
            act.activation(FV[:, :, :, :], FV[:, :, :, :], ACT.Exp).then_inc(exp_up, 1)
            for j in range(3):
                act.wait_ge(t_up, START + j + 1)
                act.activation(turned[j][:, :], banks[4 + j][:, :], ACT.Copy).then_inc(t_out, 1)
            with act.Fori(HT, AHEAD) as i:
                scores.evacuate(act, i, 0)
                for s in range(4):
                    for q in range(BS * QB):
                        o = q // QB
                        if q % QB == 0:
                            act.wait_ge(sent[o % 2], START + 16 * ((BS // 2) * (4 * (i - HT) + s) + o // 2))
                        act.wait_ge(spread, START + BS * QB * (4 * (i - HT) + s) + (q + 1))
                        act.activation(stage[o % 2][:, :, 4 * (q % QB):4 * (q % QB) + 4],
                                       banks[4 + q % 4][:, :].rearrange("p (t j) -> p j t", t=4), ACT.Copy)\
                            .then_inc(staged, 1)
                        if q == BS * QB // 2 and s < 3:
                            scores.evacuate(act, i, s + 1)
                    scores.gelu(act, i, s, bass.ds(4 * i + s, 1))

        @block.vector
        def _(dve):
            per = 14
            chain = Tally(p_dve)
            dve.wait_ge(iota_up, START + 1)
            with dve.Fori(0, HEADS // 2) as g:
                chain.enter(g, 2 * per)
                step = stepper(dve, chain)

                def settled(ins):
                    step(ins)
                    dve.tensor_copy(gatepost[:, :], iota16[:, 0:1])

                def best16(src, spare, vals, places, n):
                    for u in range(n):
                        last = dve.max(vals[:, u, 0:8], src[u])
                    settled(last)
                    for u in range(n):
                        last = dve.max_index(places[:, u, 0:8], vals[:, u, 0:8], src[u])
                    for u in range(n):
                        last = dve.match_replace(spare[u], vals[:, u, 0:8], src[u], -3.0e38)
                    settled(last)
                    for u in range(n):
                        last = dve.max(vals[:, u, 8:16], spare[u])
                    settled(last)
                    for u in range(n):
                        last = dve.max_index(places[:, u, 8:16], vals[:, u, 8:16], spare[u])
                    settled(last)
                for k in range(2):
                    h, st, cand = 2 * g + k, SS[:, k], cands[k]
                    dve.wait_ge(s_out, START + 2 * h + 2)
                    dve.tensor_copy(gatepost[:, :], iota16[:, 0:1])
                    best16([st[:, u, :] for u in range(8)], [st2[:, u, :] for u in range(8)], sv, si, 8)
                    dve.tensor_copy(sif[:, :, :], si[:, :, :])
                    settled(dve.tensor_tensor(cand[:, :, :, :], sv[:, 0:4, :].unsqueeze(3).broadcast_to([P, NT, TOPK, TOPK]),
                                           sv[:, 4:8, :].unsqueeze(2).broadcast_to([P, NT, TOPK, TOPK]), ALU.add))
                    flat = [[m[:, t, :, :].rearrange("p a b -> p (a b)") for t in range(NT)] for m in (cand, cand2)]
                    best16(flat[0], flat[1], fv, fp, NT)
                    dve.tensor_copy(FV[:, :, bass.ds(h, 1), :].rearrange("p t o k -> p t (o k)"), fv[:, :, :])
                    fpf = fp[:, :, :].rearrange("p t k -> p (t k)")
                    dve.tensor_scalar(fa[0][:, :], fpf, 4, None, ALU.logical_shift_right)
                    step(dve.tensor_scalar(fa[1][:, :], fpf, 15, None, ALU.bitwise_and))
                    dve.tensor_copy(ff[0][:, :], fa[0][:, :])
                    step(dve.tensor_copy(ff[1][:, :], fa[1][:, :]))
                    for c, work, dst in ((0, cand, IS), (1, cand2, JS)):
                        one = work[:, :, :, :].rearrange("p t k a -> p (t k) a")
                        last = dve.tensor_tensor(one, ff[c][:, :].unsqueeze(2).broadcast_to([P, NT * TOPK, TOPK]),
                                          iota16[:, :].unsqueeze(1).broadcast_to([P, NT * TOPK, TOPK]), ALU.is_equal)
                    step(last)
                    emit_pick(dve, step, cand, cand2, sif, IS, JS, h)
                    dve.sem_inc(picked, 1)
                assert chain.local == 2 * per, chain.local
                chain.leave(HEADS // 2)
            soft = stepper(dve, Tally(p_soft))
            top = FV[:, :, :, :].rearrange("p t h k -> p (t h) k")
            heads = NT * HEADS
            soft(dve.tensor_copy(tot[:, :, :], FV[:, :, :, 0]))
            flat = tot[:, :, :].rearrange("p t h -> p (t h)")
            dve.tensor_tensor(top, top, flat.unsqueeze(2).broadcast_to([P, heads, TOPK]), ALU.subtract)\
                .then_inc(less_up, 1)
            dve.wait_ge(exp_up, START + 1)
            soft(dve.tensor_reduce(flat, top, AX.X, ALU.add))
            soft(dve.reciprocal(flat, flat))
            dve.tensor_tensor(top, top, flat.unsqueeze(2).broadcast_to([P, heads, TOPK]), ALU.mult)\
                .then_inc(gate_up, 1)
            dve.wait_ge(t_out, START + 3)
            with dve.Fori(0, T // (4 * SLOTS)) as g:
                for q in range(SLOTS):
                    dve.wait_ge(spread, START + SLOTS * g + (q - 3))
                    dve.tensor_tensor(OI[q], iota[:, :].unsqueeze(1).broadcast_to([P, 4, P]),
                                      turned[0][:, bass.ds(4 * SLOTS * g + 4 * q, 4)].unsqueeze(2)
                                      .broadcast_to([P, 4, P]), ALU.is_equal)
                    dve.tensor_tensor(OJ[q], iota[:, :].unsqueeze(1).broadcast_to([P, 4, P]),
                                      turned[1][:, bass.ds(4 * SLOTS * g + 4 * q, 4)].unsqueeze(2)
                                      .broadcast_to([P, 4, P]), ALU.is_equal).then_inc(ones_up, 1)


def emit_pick(dve, step, cand, cand2, sif, IS, JS, h):
    dve.tensor_tensor(cand[:, :, :, :], cand[:, :, :, :],
                      sif[:, 0:4, :].unsqueeze(2).broadcast_to([P, NT, TOPK, TOPK]), ALU.mult)
    step(dve.tensor_tensor(cand2[:, :, :, :], cand2[:, :, :, :],
                           sif[:, 4:8, :].unsqueeze(2).broadcast_to([P, NT, TOPK, TOPK]), ALU.mult))
    for work, dst in ((cand, IS), (cand2, JS)):
        last = dve.tensor_reduce(dst[:, :, bass.ds(h, 1), :].rearrange("p t o k -> p t (o k)"),
                                 work[:, :, :, :], AX.X, ALU.add)
    step(last)


def emit_experts(nc, bank, banks, sem, v):
    urows, peer_u, peer_v, ln2_g, ln2_b, ident, hh, hl, ring, gates, x1_kept, gt2, out = (
        v[n] for n in ("urows", "peer_u", "peer_v", "ln2_g", "ln2_b", "ident", "hh", "hl", "ring", "gates",
                       "x1_kept", "gt2", "out"))
    acc = v["acc"]
    ctx = ExitStack()
    with ctx:
        def sb(name, shape, dt=F32):
            return ctx.enter_context(nc.sbuf_tensor(name, shape, dt))

        scores = ExpertScores(nc, sb, sem, "e_", banks, ident, hh, hl, ring, peer_u, urows)
        vraw = [v["gt1"]] + [sb(f"vraw{s}", [P, D]) for s in range(1, 4)]
        vh = [sb(f"vh{q}", [P, 2, D], F32R) for q in range(2)]
        vl = [sb(f"vl{q}", [P, 2, D], F32R) for q in range(2)]
        gt = [sb(f"gtile{q}", [P, T // TB, 2, TB]) for q in range(2)]
        w = [sb(f"w{b}", [P, 2, P]) for b in range(2)]
        wh = [sb(f"wh{t}", [P, 2, P], F32R) for t in range(NT)]
        wl = [sb(f"wl{t}", [P, 2, P], F32R) for t in range(NT)]
        v_in = [sem(f"v_in{s}") for s in range(4)]
        g_in = [sem(f"g_in{q}") for q in range(2)]
        vh_up, vl_up, w_up, wh_up, wl_up, y_up, y_added, zeroed = (
            sem(n) for n in ("vh_up", "vl_up", "w_up", "wh_up", "wl_up", "y_up6", "y_added", "zeroed"))
        IT = NKEYS // 4
        MAIN = IT - AHEAD
        vsrc = expert_rows(peer_v)

        lg, lb = (ring[:, 2 * j:2 * j + 2, :].rearrange("p a b -> p (a b)") for j in range(2))
        norm = Norm(nc, sb, "n2_")
        ln_in, var_up, root_up, centred, gained, x2_up, p_dve, p_y = (
            sem(n) for n in ("ln_in6", "var_up6", "root_up6", "centred6", "gained6", "x2_up", "p_dve6", "p_y"))
        out_sent, x1_in = sem("out_sent"), [sem(f"x1_in{t}") for t in range(NT)]

        nc.all_engine_barrier()
        block = ctx.enter_context(nc.Block())

        def load_v(sp, s, turn):
            sp.dma_start(vraw[s][:, :], vsrc[:, bass.ds(4 * turn + s, 1), :].rearrange("i o d -> i (o d)"))\
                .then_inc(v_in[s], 16)

        def load_g(sp, q, turn):
            sp.dma_start(gt[q][:, :, :, :], gates[:, :, bass.ds(4 * turn + 2 * q, 2), :]).then_inc(g_in[q], 16)

        @block.sync
        def _(sp):
            for q in range(2):
                for s in (2 * q, 2 * q + 1):
                    sp.dma_start(vraw[s][:, :], vsrc[:, s, :]).then_inc(v_in[s], 16)
                sp.dma_start(gt[q][:, :, :, :], gates[:, :, 2 * q:2 * q + 2, :]).then_inc(g_in[q], 16)

            def loads(i, with_u):
                def u(s):
                    if with_u:
                        sp.wait_ge(scores.turned, START + 8 * i + 2 * s + 2)
                        scores.load(sp, i, s, bass.ds(4 * ((i + AHEAD + 1) % IT) + s, 1))
                for s in (0, 1):
                    sp.wait_ge(vl_up, START + 4 * i + (s + 1))
                    sp.wait_ge(vh_up, START + 4 * i + (s + 1))
                    load_v(sp, s, (i + 1) % IT)
                sp.wait_ge(wl_up, START + 8 * i + 4)
                sp.wait_ge(w_up, START + 8 * i + 4)
                load_g(sp, 0, (i + 1) % IT)
                u(0)
                for s in (2, 3):
                    sp.wait_ge(vl_up, START + 4 * i + (s + 1))
                    sp.wait_ge(vh_up, START + 4 * i + (s + 1))
                    load_v(sp, s, (i + 1) % IT)
                u(1)
                sp.wait_ge(w_up, START + 8 * i + 8)
                load_g(sp, 1, (i + 1) % IT)
                u(2)
                u(3)
            with sp.Fori(0, MAIN) as i:
                loads(i, True)
            with sp.Fori(MAIN, IT) as i:
                loads(i, False)
            for t in range(NT):
                sp.wait_ge(v_in[t], START + 16 * (IT + 1))
                sp.wait_ge(vl_up, START + 4 * IT + 2)
                sp.wait_ge(vh_up, START + 4 * IT + 2)
                sp.dma_start(vraw[t][:, :], x1_kept[t]).then_inc(x1_in[t], 16)
            sp.wait_ge(w_up, START + 8 * IT + 4)
            for dst, src in ((lg, ln2_g), (lb, ln2_b)):
                sp.dma_start(dst, src.rearrange("o n -> (o n)").partition_broadcast(P)).then_inc(ln_in, 16)
            for t in range(NT):
                sp.wait_ge(x2_up, START + t + 1)
                sp.dma_start(out[0, t * P:(t + 1) * P, :], acc[:, t, :]).then_inc(out_sent, 16)
            sp.wait_ge(out_sent, START + 16 * NT)
            for s in range(4):
                sp.wait_ge(v_in[s], START + 16 * (IT + 1))
                sp.wait_ge(scores.u_in[s], START + 16 * MAIN)
            for q in range(2):
                sp.wait_ge(g_in[q], START + 16 * (IT + 1))

        def v_ready(eng, i, q, ahead):
            for s in (2 * q, 2 * q + 1):
                eng.wait_ge(v_in[s], START + (16 * i + (32 if ahead else 16)))

        @block.gpsimd
        def _(pool):
            pool.memset(acc[:, :, :], 0.0).then_inc(zeroed, 1)

            def rest(i, q, n, done):
                v_ready(pool, i, q, ahead=(done is not None and q == 0))
                if done is not None:
                    pool.wait_ge(y_up, START + done)
                for k in range(2):
                    pool.wait_ge(vh_up, START + 2 * n + (k + 1))
                    pool.tensor_tensor(vl[q][:, k, :], vraw[2 * q + k][:, :], vh[q][:, k, :].bitcast(F32),
                                       ALU.subtract).then_inc(vl_up, 1)
            rest(0, 0, 0, None)

            def turn(i, with_u):
                if with_u:
                    scores.remainder(pool, i, 0)
                rest(i, 1, 2 * i + 1, 8 * i)
                if with_u:
                    scores.remainder(pool, i, 1)
                    scores.remainder(pool, i, 2)
                rest(i, 0, 2 * i + 2, 8 * i + 4)
                if with_u:
                    scores.remainder(pool, i, 3)
            with pool.Fori(0, MAIN) as i:
                turn(i, True)
            with pool.Fori(MAIN, IT) as i:
                turn(i, False)
            for t in range(NT):
                if t == 0:
                    pool.wait_ge(ln_in, START + 32)
                pool.wait_ge(centred, START + t + 1)
                pool.tensor_tensor(acc[:, t, :], acc[:, t, :], lg[:, :], ALU.mult).then_inc(gained, 1)

        @block.scalar
        def _(act):
            def rounded(i, q, done):
                v_ready(act, i, q, ahead=(done is not None and q == 0))
                if done is not None:
                    act.wait_ge(y_up, START + done)
                for k in range(2):
                    act.activation(vh[q][:, k, :], vraw[2 * q + k][:, :], ACT.Copy).then_inc(vh_up, 1)
            rounded(0, 0, None)

            def turn(i, with_u):
                def gelu(s):
                    if with_u:
                        act.wait_ge(w_up, START + 8 * i + (0, 0, 4, 4)[s] + 4)
                        scores.gelu(act, i, s, bass.ds(4 * (i % AHEAD) + s, 1))
                if with_u:
                    scores.evacuate(act, i, 0)
                rounded(i, 1, 8 * i)
                if with_u:
                    scores.evacuate(act, i, 1)
                    gelu(0)
                    scores.evacuate(act, i, 2)
                    gelu(1)
                rounded(i, 0, 8 * i + 4)
                if with_u:
                    scores.evacuate(act, i, 3)
                    gelu(2)
                    gelu(3)
            with act.Fori(0, MAIN) as i:
                turn(i, True)
            with act.Fori(MAIN, IT) as i:
                turn(i, False)
            for t in range(NT):
                act.wait_ge(var_up, START + t + 1)
                norm.root(act, t).then_inc(root_up, 1)

        @block.tensor
        def _(pe):
            def unit(i, q, t):
                u = 4 * q + t
                pe.wait_ge(wl_up, START + 8 * i + (u + 1))
                pe.wait_ge(wh_up, START + 8 * i + (u + 1))
                if t == 0:
                    pe.wait_ge(vl_up, START + 4 * i + (2 * q + 2))
                pe.wait_ge(y_added, START + 8 * i + (u - 1))
                for h in range(2):
                    b = banks[4 + 2 * (u % 2) + h]
                    half = slice(512 * h, 512 * h + 512)
                    for k in range(2):
                        pe.matmul(b[:, :], wh[t][:, k, :], vh[q][:, k, half], start=(k == 0), stop=False)
                        pe.matmul(b[:, :], wh[t][:, k, :], vl[q][:, k, half], start=False, stop=False)
                        last = pe.matmul(b[:, :], wl[t][:, k, :], vh[q][:, k, half], start=False, stop=(k == 1))
                last.then_inc(y_up, 1)

            def turn(i, with_u):
                for s in range(4):
                    if with_u:
                        scores.turn(pe, i, s)
                    unit(i, s // 2, 2 * (s % 2))
                    unit(i, s // 2, 2 * (s % 2) + 1)
                    if with_u:
                        scores.product(pe, i, s)
            with pe.Fori(0, MAIN) as i:
                turn(i, True)
            with pe.Fori(MAIN, IT) as i:
                turn(i, False)

        @block.vector
        def _(dve):
            def gated(n, i, q, t, slot, turn_of_gates):
                if t == 0:
                    dve.wait_ge(g_in[q], START + 16 * turn_of_gates + 16)
                dve.tensor_tensor(w[t % 2][:, :, :].rearrange("p j (b t) -> p j b t", b=P // TB),
                                  ring[:, slot, t * P:(t + 1) * P].rearrange("p j (b t) -> p j b t", b=P // TB),
                                  gt[q][:, (P // TB) * t:(P // TB) * (t + 1), :, :].rearrange("p b j t -> p j b t"), ALU.mult)\
                    .then_inc(w_up, 1)
                dve.wait_ge(w_up, START + n + (t + 1))
                dve.tensor_copy(wh[t][:, :, :], w[t % 2][:, :, :]).then_inc(wh_up, 1)
                dve.wait_ge(wh_up, START + n + (t + 1))
                dve.tensor_tensor(wl[t][:, :, :], w[t % 2][:, :, :], wh[t][:, :, :].bitcast(F32), ALU.subtract)\
                    .then_inc(wl_up, 1)

            dve.wait_ge(zeroed, START + 1)
            for t in range(NT):
                gated(0, 0, 0, t, slice(0, 2), 0)

            def turn(i):
                for q in range(2):
                    for t in range(NT):
                        u = 4 * q + t
                        dve.wait_ge(y_up, START + 8 * i + (u + 1))
                        b = bank[:, 512 * (4 + 2 * (u % 2)):512 * (6 + 2 * (u % 2))]
                        dve.wait_ge(y_added, START + 8 * i + (u - 3))
                        dve.tensor_tensor(acc[:, t, :], acc[:, t, :], b, ALU.add).then_inc(y_added, 1)
                        if q == 0:
                            gated(8 * i + 4, i, 1, t, bass.ds(4 * (i % AHEAD) + 2, 2), i)
                        else:
                            gated(8 * i + 8, i, 0, t, bass.ds(4 * ((i + 1) % AHEAD), 2), i + 1)
            with dve.Fori(0, MAIN) as i:
                turn(i)
            with dve.Fori(MAIN, IT) as i:
                turn(i)
            step = stepper(dve, Tally(p_dve))
            dve.wait_ge(y_added, START + 8 * IT)
            def head(t):
                step(dve.tensor_tensor(acc[:, t, :], acc[:, t, :], gt2[:, :], ALU.mult))
                dve.wait_ge(x1_in[t], START + 16)
                step(dve.scalar_tensor_tensor(out=acc[:, t, :], in0=vraw[t][:, :], scalar=ALPHA, in1=acc[:, t, :],
                                              op0=ALU.mult, op1=ALU.add))
                norm.moments(dve, step, t, acc[:, t, :]).then_inc(var_up, 1)

            def tail(t):
                dve.wait_ge(root_up, START + t + 1)
                norm.scaled(dve, step, t, acc[:, t, :]).then_inc(centred, 1)

            def last(t):
                dve.wait_ge(gained, START + t + 1)
                dve.tensor_tensor(acc[:, t, :], acc[:, t, :], lb[:, :], ALU.add).then_inc(x2_up, 1)
            for t in range(NT):
                head(t)
                if t >= 1:
                    tail(t - 1)
                if t >= 2:
                    last(t - 2)
            tail(NT - 1)
            last(NT - 2)
            last(NT - 1)


_INS = ["x", "c", "ada_w", "ada_b", "w_in", "attn_sink", "shift_mu", "decay_w0", "decay_w2", "iclr_a0", "iclr_a2",
        "gate_g2", "k_k", "k_a", "r_k", "lnx_g", "lnx_b", "w_out", "ln1_g", "ln1_b", "peer_wq", "peer_subkeys",
        "peer_u", "peer_v", "ln2_g", "ln2_b"]


def kernel(**inputs):
    import numpy as np
    import concourse.bacc as bacc
    from concourse.bass_utils import run_bass_kernel_spmd

    nc = bacc.Bacc("TRN2", target_bir_lowering=False, num_devices=1)
    arrays, args = {}, []
    for name in _INS:
        a = np.ascontiguousarray(inputs[name])
        arrays["in_" + name] = a
        args.append(nc.dram_tensor("in_" + name, a.shape, mybir.dt.from_np(a.dtype), kind="ExternalInput").ap())
    args.append(nc.dram_tensor("out_x", (1, T, D), F32, kind="ExternalOutput").ap())
    hybrid_layer(nc, *args)
    r = run_bass_kernel_spmd(nc, [arrays], core_ids=[0])
    return r.results[0]["out_x"]
```
